# Optimizing a Trainium2 kernel written in Bass

```python
import math
import jax
import jax.numpy as jnp
from jax import lax
import numpy as np

D_MODEL = 1024
BATCH = 1
SEQ = 1024
DEPTH = 1
DEC_BATCH = 8
DEC_SEQ = 8
PAST_LEN = 4096
PAGE_SIZE = 128

HEAD_DIM = 64
W_A = D_MODEL // 2
W_B = D_MODEL // 4
W_C = D_MODEL // 4
W_MIX = W_A + W_B + W_C
H_A = W_A // HEAD_DIM
KV_A = 2
REP_A = H_A // KV_A
Q_COLS = H_A * HEAD_DIM
KV_COLS = KV_A * HEAD_DIM
L_CMP = 32
SEL_BLOCK = 64
TOP_K = 16
N_LOCAL_FORCED = 2
FORCE_SCORE = 1.0e4
WINDOW = 512
WIN_QBLK = 128
SEL_QBLK = 64
CONV_B = 31
GN_GROUPS = 4
CONV_C = 4
LRU_BLOCKS = 4
LRU_BW = W_C // LRU_BLOCKS
LRU_C = 8.0
NUM_BUCKETS = 32
MAX_DISTANCE = 128
SM_SCALE = HEAD_DIM ** -0.5
EPS = 1e-6
NEG = -1e30
_SIZES = (Q_COLS, KV_COLS, KV_COLS, KV_COLS, KV_COLS, KV_COLS, KV_COLS, 3 * H_A, W_A, 2 * W_B, W_B, W_C, W_C)
D_IN = Q_COLS + 6 * KV_COLS + 3 * H_A + W_A + 3 * W_B + 2 * W_C

kernel_name = 'hymba_nsa_conformer_rglru_step'

def _rms_norm(x, g):
    xf = x.astype(jnp.float32)
    y = xf * lax.rsqrt(jnp.mean(xf * xf, axis=-1, keepdims=True) + EPS)
    return (y * g.astype(jnp.float32)).astype(x.dtype)

def _split_points():
    pts, acc = [], 0
    for s in _SIZES[:-1]:
        acc += s
        pts.append(acc)
    return pts

def _t5_bucket(dist):
    n = jnp.maximum(dist, 0)
    max_exact = NUM_BUCKETS // 2
    nf = jnp.maximum(n, 1).astype(jnp.float32)
    large = max_exact + (jnp.log(nf / max_exact) / math.log(MAX_DISTANCE / max_exact) * (NUM_BUCKETS - max_exact)).astype(jnp.int32)
    return jnp.where(n < max_exact, n, jnp.minimum(large, NUM_BUCKETS - 1))

def _last_rows(a, n):
    length = a.shape[1]
    if length >= n:
        return a[:, length - n:]
    pad = [(0, 0)] * a.ndim
    pad[1] = (n - length, 0)
    return jnp.pad(a, pad)

def _causal_dwconv(x_ext, w, b):
    y = lax.conv_general_dilated(x_ext, w[:, None, :].astype(x_ext.dtype), (1,), 'VALID',
                                 dimension_numbers=('NWC', 'WIO', 'NWC'),
                                 feature_group_count=x_ext.shape[-1])
    return y + b

def _masked_softmax(logits, mask):
    p = jax.nn.softmax(jnp.where(mask, logits, NEG), axis=-1)
    return jnp.where(mask, p, 0.0)

def _q_heads(a):
    return a.reshape(a.shape[:2] + (KV_A, REP_A, HEAD_DIM))

def _kv_heads(a):
    return a.reshape(a.shape[:2] + (KV_A, HEAD_DIM))

def _compress_blocks(k, w):
    bsz, length, g, d = k.shape
    n = length // L_CMP
    kb = k[:, :n * L_CMP].reshape(bsz, n, L_CMP, g, d)
    return jnp.einsum('bnjgd,jd->bngd', kb, w)

def _nsa_compressed(q, q_pos, kc, vc, rel_bias):
    t, n = q.shape[1], kc.shape[1]
    blk_end = (jnp.arange(n, dtype=jnp.int32) + 1) * L_CMP - 1
    dist = q_pos[:, None] - blk_end[None, :]
    bias = rel_bias[_t5_bucket(dist)].reshape(t, n, KV_A, REP_A).transpose(0, 2, 3, 1)
    logits = jnp.einsum('btgrd,bngd->btgrn', q, kc).astype(jnp.float32) * SM_SCALE + bias.astype(jnp.float32)
    p = _masked_softmax(logits, (dist >= 0)[:, None, None, :])
    o = jnp.einsum('btgrn,bngd->btgrd', p.astype(vc.dtype), vc)
    return o, p

def _select_blocks(p_cmp, q_pos, n_sel):
    bsz, t = p_cmp.shape[:2]
    per = SEL_BLOCK // L_CMP
    imp = p_cmp.sum(axis=3)
    imp = jnp.pad(imp, ((0, 0), (0, 0), (0, 0), (0, n_sel * per - imp.shape[-1])))
    imp = imp.reshape(bsz, t, KV_A, n_sel, per).sum(-1)
    blk = jnp.arange(n_sel, dtype=jnp.int32)[None, :]
    cur = (q_pos // SEL_BLOCK)[:, None]
    forced = (blk == 0) | ((blk <= cur) & (blk > cur - N_LOCAL_FORCED))
    score = jnp.where(forced[None, :, None, :], FORCE_SCORE, imp)
    score = jnp.where((blk <= cur)[None, :, None, :], score, NEG)
    _, top_i = lax.top_k(score, min(TOP_K, n_sel))
    valid = top_i <= (q_pos // SEL_BLOCK)[None, :, None, None]
    return top_i, valid

def _sel_attend(q, q_pos, ks, vs, key_pos, valid, rel_bias):
    bsz, t, g, r, d = q.shape
    k_top, s = ks.shape[3], ks.shape[4]
    dist = q_pos[None, :, None, None, None] - key_pos
    g_idx = jnp.arange(KV_A)[None, None, :, None, None]
    bias = jnp.moveaxis(rel_bias.reshape(NUM_BUCKETS, KV_A, REP_A)[_t5_bucket(dist), g_idx], -1, 3)
    logits = jnp.einsum('btgrd,btgksd->btgrks', q, ks).astype(jnp.float32) * SM_SCALE + bias.astype(jnp.float32)
    mask = ((dist >= 0) & valid[..., None])[:, :, :, None]
    p = _masked_softmax(logits.reshape(bsz, t, g, r, k_top * s), mask.reshape(bsz, t, g, 1, k_top * s))
    return jnp.einsum('btgrks,btgksd->btgrd', p.reshape(bsz, t, g, r, k_top, s).astype(vs.dtype), vs)

def _window_banded(q, k, v, rel_bias):
    bsz, t = q.shape[:2]
    nb = t // WIN_QBLK
    span = WINDOW + WIN_QBLK
    pad = ((0, 0), (WINDOW, 0), (0, 0), (0, 0))
    idx = jnp.arange(nb)[:, None] * WIN_QBLK + jnp.arange(span)[None, :]
    kb = jnp.pad(k, pad)[:, idx]
    vb = jnp.pad(v, pad)[:, idx]
    qb = q.reshape(bsz, nb, WIN_QBLK, KV_A, REP_A, HEAD_DIM)
    dist = WINDOW + jnp.arange(WIN_QBLK)[:, None] - jnp.arange(span)[None, :]
    bias = rel_bias[_t5_bucket(dist)].reshape(WIN_QBLK, span, KV_A, REP_A).transpose(2, 3, 0, 1)
    logits = jnp.einsum('bnqgrd,bnsgd->bngrqs', qb, kb).astype(jnp.float32) * SM_SCALE + bias.astype(jnp.float32)
    mask = ((dist >= 0) & (dist < WINDOW))[None] & (idx >= WINDOW)[:, None, :]
    p = _masked_softmax(logits, mask[None, :, None, None])
    o = jnp.einsum('bngrqs,bnsgd->bnqgrd', p.astype(v.dtype), vb)
    return o.reshape(bsz, t, KV_A, REP_A, HEAD_DIM)

def _window_dense(q, q_pos, k, v, k_pos, rel_bias):
    t, length = q.shape[1], k.shape[1]
    dist = q_pos[:, None] - k_pos[None, :]
    bias = rel_bias[_t5_bucket(dist)].reshape(t, length, KV_A, REP_A).transpose(0, 2, 3, 1)
    logits = jnp.einsum('btgrd,blgd->btgrl', q, k).astype(jnp.float32) * SM_SCALE + bias.astype(jnp.float32)
    p = _masked_softmax(logits, ((dist >= 0) & (dist < WINDOW))[:, None, None, :])
    return jnp.einsum('btgrl,blgd->btgrd', p.astype(v.dtype), v)

def _nsa_prompt(q, k_c, v_c, k_s, v_s, k_w, v_w, w_ck, w_cv, rel_bias):
    bsz, t = q.shape[:2]
    q_pos = jnp.arange(t, dtype=jnp.int32)
    o_c, p_c = _nsa_compressed(q, q_pos, _compress_blocks(k_c, w_ck), _compress_blocks(v_c, w_cv), rel_bias)
    top_i, valid = _select_blocks(p_c, q_pos, -(-t // SEL_BLOCK))
    n_chunks = t // SEL_QBLK
    s_ar = jnp.arange(SEL_BLOCK, dtype=jnp.int32)
    b5 = jnp.arange(bsz)[:, None, None, None, None]
    g5 = jnp.arange(KV_A)[None, None, :, None, None]

    def chunk(args):
        q_c, i_c, ok_c, pos_c = args
        key_pos = i_c[..., None] * SEL_BLOCK + s_ar
        return _sel_attend(q_c, pos_c, k_s[b5, key_pos, g5], v_s[b5, key_pos, g5], key_pos, ok_c, rel_bias)

    def to_chunks(a):
        return jnp.moveaxis(a.reshape((bsz, n_chunks, SEL_QBLK) + a.shape[2:]), 1, 0)

    o_s = lax.map(chunk, (to_chunks(q), to_chunks(top_i), to_chunks(valid), q_pos.reshape(n_chunks, SEL_QBLK)))
    o_s = jnp.moveaxis(o_s, 0, 1).reshape(q.shape)
    o_w = _window_banded(q, k_w, v_w, rel_bias)
    return o_c, o_s, o_w

def _nsa_decode(q, k_c, v_c, k_s, v_s, k_w, v_w, pool_ck, pool_cv, pool_sk, pool_sv, win_k, win_v, page_table, w_ck, w_cv, rel_bias):
    bsz, t = q.shape[:2]
    n_pages = page_table.shape[1]
    past = n_pages * PAGE_SIZE
    q_pos = past + jnp.arange(t, dtype=jnp.int32)

    def past_rows(pool):
        return pool[page_table].reshape(bsz, past, KV_A, HEAD_DIM)

    kc = _compress_blocks(jnp.concatenate([past_rows(pool_ck), k_c], axis=1), w_ck)
    vc = _compress_blocks(jnp.concatenate([past_rows(pool_cv), v_c], axis=1), w_cv)
    o_c, p_c = _nsa_compressed(q, q_pos, kc, vc, rel_bias)
    n_sel = -(-(past + t) // SEL_BLOCK)
    n_past_sel = past // SEL_BLOCK
    n_new_sel = n_sel - n_past_sel
    top_i, valid = _select_blocks(p_c, q_pos, n_sel)
    s_ar = jnp.arange(SEL_BLOCK, dtype=jnp.int32)
    b4 = jnp.arange(bsz)[:, None, None, None]
    b5 = b4[..., None]
    g5 = jnp.arange(KV_A)[None, None, :, None, None]
    start = jnp.clip(top_i, 0, n_past_sel - 1) * SEL_BLOCK
    phys = page_table[b4, start // PAGE_SIZE]
    rows = (start % PAGE_SIZE)[..., None] + s_ar
    new_rows = jnp.clip(top_i - n_past_sel, 0, n_new_sel - 1)[..., None] * SEL_BLOCK + s_ar
    pad = ((0, 0), (0, n_new_sel * SEL_BLOCK - t), (0, 0), (0, 0))
    is_past = (top_i < n_past_sel)[..., None, None]
    ks = jnp.where(is_past, pool_sk[phys[..., None], rows, g5], jnp.pad(k_s, pad)[b5, new_rows, g5])
    vs = jnp.where(is_past, pool_sv[phys[..., None], rows, g5], jnp.pad(v_s, pad)[b5, new_rows, g5])
    key_pos = top_i[..., None] * SEL_BLOCK + s_ar
    o_s = _sel_attend(q, q_pos, ks, vs, key_pos, valid, rel_bias)
    w_buf = win_k.shape[1]
    kw = jnp.concatenate([win_k, k_w], axis=1)
    vw = jnp.concatenate([win_v, v_w], axis=1)
    k_pos = past - w_buf + jnp.arange(w_buf + t, dtype=jnp.int32)
    o_w = _window_dense(q, q_pos, kw, vw, k_pos, rel_bias)
    return o_c, o_s, o_w, _last_rows(kw, w_buf), _last_rows(vw, w_buf)

def _nsa_merge(o_c, o_s, o_w, gate, z_a):
    bsz, t = gate.shape[:2]
    g = jax.nn.sigmoid(gate).reshape(bsz, t, 3, KV_A, REP_A, 1)
    o = g[:, :, 0] * o_c + g[:, :, 1] * o_s + g[:, :, 2] * o_w
    return o.reshape(bsz, t, W_A) * jax.nn.silu(z_a)

def _conformer(glu, z, buf, conv_w, conv_b, gn_gain, gn_bias, w_pw):
    val, gate = jnp.split(glu, 2, axis=-1)
    u = val * jax.nn.sigmoid(gate)
    u_ext = jnp.concatenate([buf, u], axis=1)
    c = _causal_dwconv(u_ext, conv_w, conv_b)
    bsz, t = c.shape[:2]
    cg = c.astype(jnp.float32).reshape(bsz, t, GN_GROUPS, W_B // GN_GROUPS)
    mu = jnp.mean(cg, axis=-1, keepdims=True)
    var = jnp.mean(jnp.square(cg - mu), axis=-1, keepdims=True)
    cn = ((cg - mu) * lax.rsqrt(var + EPS)).reshape(bsz, t, W_B) * gn_gain.astype(jnp.float32) + gn_bias.astype(jnp.float32)
    out = jax.nn.silu(cn).astype(c.dtype) @ w_pw
    return out * jax.nn.silu(z), _last_rows(u_ext, CONV_B - 1)

def _rglru(x_c, z, buf, h0, conv_w, conv_b, w_a, b_a, w_x, b_x, lam):
    x_ext = jnp.concatenate([buf, x_c], axis=1)
    u = _causal_dwconv(x_ext, conv_w, conv_b)
    bsz, t = u.shape[:2]
    ub = u.reshape(bsz, t, LRU_BLOCKS, LRU_BW)
    r = jax.nn.sigmoid(jnp.einsum('btnc,ncd->btnd', ub, w_a).reshape(bsz, t, W_C) + b_a).astype(jnp.float32)
    i = jax.nn.sigmoid(jnp.einsum('btnc,ncd->btnd', ub, w_x).reshape(bsz, t, W_C) + b_x)
    log_a = -LRU_C * r * jax.nn.softplus(-lam.astype(jnp.float32))
    a = jnp.exp(log_a)
    b = jnp.sqrt(-jnp.expm1(2.0 * log_a)) * (i * u).astype(jnp.float32)
    b = b.at[:, 0].add(a[:, 0] * h0.astype(jnp.float32))

    def combine(left, right):
        return left[0] * right[0], right[0] * left[1] + right[1]

    _, h = lax.associative_scan(combine, (a, b), axis=1)
    y = h.astype(u.dtype) * jax.nn.silu(z)
    return y, _last_rows(x_ext, CONV_C - 1), h[:, -1].astype(x_c.dtype)

def _project(h, g_pre, w_in):
    return jnp.split(_rms_norm(h, g_pre) @ w_in, _split_points(), axis=-1)

def _output(h, a_out, b_out, c_out, w_out, g_post):
    y = jnp.concatenate([a_out, b_out, c_out], axis=-1) @ w_out
    return h + _rms_norm(y, g_post)

def setup_inputs(seed: int = 0) -> dict:
    key = jax.random.key(seed)
    ks = jax.random.split(key, 32)
    n_pages = PAST_LEN // PAGE_SIZE
    n_phys = (5 * DEC_BATCH * n_pages) // 4
    w_buf = min(WINDOW, PAST_LEN)

    def nrm(k, shape, scale=1.0):
        return scale * jax.random.normal(k, shape, jnp.float32)

    pool = (DEPTH, n_phys, PAGE_SIZE, KV_A, HEAD_DIM)
    win = (DEPTH, DEC_BATCH, w_buf, KV_A, HEAD_DIM)
    page_table = jax.random.permutation(ks[11], n_phys)[:DEC_BATCH * n_pages].reshape(DEC_BATCH, n_pages).astype(jnp.int32)
    a0 = jax.random.uniform(ks[30], (DEPTH, W_C), jnp.float32, 0.9, 0.999)
    return {
        'x_prompt': nrm(ks[0], (BATCH, SEQ, D_MODEL)),
        'x_sample': nrm(ks[1], (DEC_BATCH, DEC_SEQ, D_MODEL)),
        'cache_cmp_k': nrm(ks[2], pool),
        'cache_cmp_v': nrm(ks[3], pool),
        'cache_sel_k': nrm(ks[4], pool),
        'cache_sel_v': nrm(ks[5], pool),
        'cache_win_k': nrm(ks[6], win),
        'cache_win_v': nrm(ks[7], win),
        'state_conv_b': nrm(ks[8], (DEPTH, DEC_BATCH, CONV_B - 1, W_B), 0.5),
        'state_conv_c': nrm(ks[9], (DEPTH, DEC_BATCH, CONV_C - 1, W_C)),
        'state_rglru': nrm(ks[10], (DEPTH, DEC_BATCH, W_C), 0.5),
        'page_table': page_table,
        'rel_bias': nrm(ks[12], (NUM_BUCKETS, H_A), 0.5),
        'g_pre': 1.0 + nrm(ks[13], (DEPTH, D_MODEL), 0.05),
        'g_post': 1.0 + nrm(ks[14], (DEPTH, D_MODEL), 0.05),
        'w_in': nrm(ks[15], (DEPTH, D_MODEL, D_IN), D_MODEL ** -0.5),
        'w_out': nrm(ks[16], (DEPTH, W_MIX, D_MODEL), W_MIX ** -0.5),
        'w_cmp_k': (1.0 + nrm(ks[17], (DEPTH, L_CMP, HEAD_DIM), 0.1)) * (L_CMP ** -0.5),
        'w_cmp_v': (1.0 + nrm(ks[18], (DEPTH, L_CMP, HEAD_DIM), 0.1)) * (L_CMP ** -0.5),
        'conv_b_w': nrm(ks[19], (DEPTH, CONV_B, W_B), CONV_B ** -0.5),
        'conv_b_b': nrm(ks[20], (DEPTH, W_B), 0.02),
        'gn_gain': 1.0 + nrm(ks[21], (DEPTH, W_B), 0.05),
        'gn_bias': nrm(ks[22], (DEPTH, W_B), 0.02),
        'w_pw_b': nrm(ks[23], (DEPTH, W_B, W_B), W_B ** -0.5),
        'conv_c_w': nrm(ks[24], (DEPTH, CONV_C, W_C), CONV_C ** -0.5),
        'conv_c_b': nrm(ks[25], (DEPTH, W_C), 0.02),
        'w_lru_a': nrm(ks[26], (DEPTH, LRU_BLOCKS, LRU_BW, LRU_BW), LRU_BW ** -0.5),
        'b_lru_a': nrm(ks[27], (DEPTH, W_C), 0.02),
        'w_lru_x': nrm(ks[28], (DEPTH, LRU_BLOCKS, LRU_BW, LRU_BW), LRU_BW ** -0.5),
        'b_lru_x': nrm(ks[29], (DEPTH, W_C), 0.02),
        'lru_lambda': jnp.log(a0) - jnp.log1p(-a0),
    }

def reference(x_prompt, x_sample, cache_cmp_k, cache_cmp_v, cache_sel_k, cache_sel_v, cache_win_k, cache_win_v,
              state_conv_b, state_conv_c, state_rglru, page_table, rel_bias, g_pre, g_post, w_in, w_out,
              w_cmp_k, w_cmp_v, conv_b_w, conv_b_b, gn_gain, gn_bias, w_pw_b, conv_c_w, conv_c_b,
              w_lru_a, b_lru_a, w_lru_x, b_lru_x, lru_lambda):
    w_buf = cache_win_k.shape[2]
    hp, hs = x_prompt, x_sample
    prompt_states, sample_states = [], []
    for l in range(DEPTH):
        bsz = hp.shape[0]
        q, k_c, v_c, k_s, v_s, k_w, v_w, gate, z_a, glu, z_b, x_c, z_c = _project(hp, g_pre[l], w_in[l])
        o_c, o_s, o_w = _nsa_prompt(_q_heads(q), _kv_heads(k_c), _kv_heads(v_c), _kv_heads(k_s), _kv_heads(v_s),
                                    _kv_heads(k_w), _kv_heads(v_w), w_cmp_k[l], w_cmp_v[l], rel_bias)
        a_out = _nsa_merge(o_c, o_s, o_w, gate, z_a)
        b_out, cb = _conformer(glu, z_b, jnp.zeros((bsz, CONV_B - 1, W_B), hp.dtype), conv_b_w[l], conv_b_b[l],
                               gn_gain[l], gn_bias[l], w_pw_b[l])
        c_out, cc, hc = _rglru(x_c, z_c, jnp.zeros((bsz, CONV_C - 1, W_C), hp.dtype), jnp.zeros((bsz, W_C), hp.dtype),
                               conv_c_w[l], conv_c_b[l], w_lru_a[l], b_lru_a[l], w_lru_x[l], b_lru_x[l], lru_lambda[l])
        hp = _output(hp, a_out, b_out, c_out, w_out[l], g_post[l])
        prompt_states.append((_kv_heads(k_c), _kv_heads(v_c), _kv_heads(k_s), _kv_heads(v_s),
                              _last_rows(_kv_heads(k_w), w_buf), _last_rows(_kv_heads(v_w), w_buf), cb, cc, hc))
        q, k_c, v_c, k_s, v_s, k_w, v_w, gate, z_a, glu, z_b, x_c, z_c = _project(hs, g_pre[l], w_in[l])
        o_c, o_s, o_w, wk, wv = _nsa_decode(_q_heads(q), _kv_heads(k_c), _kv_heads(v_c), _kv_heads(k_s), _kv_heads(v_s),
                                            _kv_heads(k_w), _kv_heads(v_w), cache_cmp_k[l], cache_cmp_v[l],
                                            cache_sel_k[l], cache_sel_v[l], cache_win_k[l], cache_win_v[l],
                                            page_table, w_cmp_k[l], w_cmp_v[l], rel_bias)
        a_out = _nsa_merge(o_c, o_s, o_w, gate, z_a)
        b_out, cb = _conformer(glu, z_b, state_conv_b[l], conv_b_w[l], conv_b_b[l], gn_gain[l], gn_bias[l], w_pw_b[l])
        c_out, cc, hc = _rglru(x_c, z_c, state_conv_c[l], state_rglru[l], conv_c_w[l], conv_c_b[l],
                               w_lru_a[l], b_lru_a[l], w_lru_x[l], b_lru_x[l], lru_lambda[l])
        hs = _output(hs, a_out, b_out, c_out, w_out[l], g_post[l])
        sample_states.append((_kv_heads(k_c), _kv_heads(v_c), _kv_heads(k_s), _kv_heads(v_s), wk, wv, cb, cc, hc))
    ck_p, cv_p, sk_p, sv_p, wk_p, wv_p, cb_p, cc_p, h_p = [jnp.stack(a) for a in zip(*prompt_states)]
    ck_s, cv_s, sk_s, sv_s, wk_s, wv_s, cb_s, cc_s, h_s = [jnp.stack(a) for a in zip(*sample_states)]
    return (hp, hs, ck_p, ck_s, cv_p, cv_s, sk_p, sk_s, sv_p, sv_s, wk_p, wk_s, wv_p, wv_s, cb_p, cb_s, cc_p, cc_s, h_p, h_s)


_drawn_inputs = setup_inputs


def setup_inputs(seed=0):
    import zlib

    import numpy as np

    out = dict(_drawn_inputs(seed))
    spreads = {}
    factors = {'w_cmp_k': 2.979, 'gn_bias': 6.267, 'b_lru_a': 8.0, 'b_lru_x': 8.0, 'conv_b_b': 2.745}
    for name, (base, spread) in spreads.items():
        noise = np.random.default_rng([zlib.crc32(name.encode()), seed]).standard_normal(out[name].shape)
        drawn = base * np.exp(spread * noise) if base else spread * noise
        out[name] = jnp.asarray(drawn.astype(out[name].dtype))
    for name, factor in factors.items():
        out[name] = (out[name] * factor).astype(out[name].dtype)
    return out
```

```python
from contextlib import ExitStack

import numpy as np

import concourse.bass as bass
from concourse import mybir

F32 = mybir.dt.float32
I32 = mybir.dt.int32
ALU = mybir.AluOpType
ACT = mybir.ActivationFunctionType
X = mybir.AxisListType.X

P = 128
D = 1024
T = 1024
NB = 8
DS = 8
S = NB * DS
TOK = T + S
NT = T // P
KD = D // P
HD = 64
G = 2
R = 4
H = G * R
PAST = 4096
PAGE = 128
NPAGE = PAST // PAGE
WIN = 512
L_CMP = 32
SEL = 64
NBLK = PAST // SEL
NCB = PAST // L_CMP
TOP_K = 16
BUCKETS = 32
MAX_DIST = 128
CB_W = 31
CC_W = 4
EPS = 1e-6
NEG = -1e30
FORCE = 1e4
Q = S
CHUNKS = [(0, 512), (512, 512), (1024, S)]

def columns(widths):
    at, out = 0, {}
    for name, n in widths.items():
        out[name] = (at, n)
        at += n
    return out, at


GLU_V, GLU_G, XC, ZB, ZC, QT, KC, VC, KS, VS, KW, VW, ZA = 0, 2, 4, 6, 8, 10, 14, 15, 16, 17, 18, 19, 20
NPROJ = 24

PAR_COLS = dict(g_pre=KD, conv_b_b=2, gn_gain=2, gn_bias=2, conv_c_b=2, b_a=2, b_x=2, lam=2,
                conv_b_w=2 * CB_W, conv_c_w=2 * CC_W, wk=L_CMP, wv=L_CMP)
CST_COLS = dict(ident=P, groupmean=P, winmask=P, page4=1)


PAR_AT, NPAR = columns(PAR_COLS)
CST_AT, NCST = columns(CST_COLS)

NEAR = 4
BIAS_COLS = dict(cmp=NCB, near=L_CMP * NEAR, new=DS, win=WIN)
OH_DEC = 8 * P
SKEW = 3 * P


BIAS_AT, NBIAS = columns(BIAS_COLS)
NOH = OH_DEC + DS * NBIAS + SKEW


def bucket(dist):
    n = np.maximum(np.asarray(dist), 0)
    half = BUCKETS // 2
    nf = np.maximum(n, 1).astype(np.float32)
    large = half + (np.log(nf / np.float32(half)) / np.float32(np.log(MAX_DIST / half)) * (BUCKETS - half)).astype(np.int32)
    return np.where(n < half, n, np.minimum(large, BUCKETS - 1))


def one_hot_tables():
    p = np.arange(P)
    dist, masked = [], []
    for n in range(8):
        d = p - L_CMP * (n - 4) - (L_CMP - 1)
        dist.append(d), masked.append(d < 0)
    for t in range(DS):
        d = PAST + t - (L_CMP * (p + 1) - 1)
        dist.append(d), masked.append(d < 0)
        j, e = np.arange(L_CMP)[:, None], np.arange(NEAR)[None, :]
        d = (PAST + t - (L_CMP * (P - NEAR + e) + j)).ravel()
        dist.append(d), masked.append(d < 0)
        d = t - np.arange(DS)
        dist.append(d), masked.append(d < 0)
        d = (WIN + t - (WIN // P * p[None, :] + np.arange(WIN // P)[:, None])).ravel()
        dist.append(d), masked.append((d < 0) | (d >= WIN))
    strip = 2 * P - 1 - np.arange(SKEW)
    dist.append(strip), masked.append(strip < 0)
    dist, masked = np.concatenate(dist), np.concatenate(masked)
    oh = np.zeros((BUCKETS + 1, dist.size), np.float32)
    oh[bucket(dist), np.arange(dist.size)] = 1.0
    oh[:BUCKETS, masked] = 0.0
    oh[BUCKETS, masked] = 1.0
    return oh


def constant_pack():
    c = np.zeros((P, NCST), np.float32)
    p = np.arange(P)[:, None]

    def put(name, v):
        a, n = CST_AT[name]
        c[:, a:a + n] = v
    q = np.arange(P)[None, :]
    put("ident", p == q)
    put("groupmean", (p // HD == q // HD) / HD)
    put("winmask", np.where(q > p, 0.0, NEG))
    put("page4", p % (PAGE // L_CMP))
    return c


def decode_selectors():
    row = np.arange(P)
    b2, g, t, r = row // Q, row // 32 % G, row // R % DS, row % R
    o = np.zeros((P, 4, 3, P), np.float32)
    for pr in range(4):
        bgt = ((2 * pr + b2) * G + g) * DS + t
        o[bgt, pr, 0, row] = 1.0
        o[row, pr, 1, bgt] = 1.0
        o[(2 * pr + b2) * DS + t, pr, 2, row] = 1.0
    head = (np.arange(H)[None, :] == (g * R + r)[:, None]).astype(np.float32)
    return np.concatenate([o.reshape(P, -1), head], 1)


def program(nc, dram, outs, scratch):
    with ExitStack() as ctx:
        def sb(name, shape, dt=F32):
            return ctx.enter_context(nc.sbuf_tensor(name, shape, dt))

        def sem(name):
            return ctx.enter_context(nc.semaphore(name))

        sizes = dict(stage=2 * 2048, wcmp=2048, ring=2 * D, xT=KD * TOK, proj=NPROJ * TOK)
        at, total = {}, 0
        for name, n in sizes.items():
            at[name] = total
            total += n
        MAIN = sb("main", [P, total])

        def main(name, n=None, off=0):
            a = at[name] + off
            return MAIN[:, a:a + (sizes[name] - off if n is None else n)]

        FREE = at["proj"] + 6 * TOK
        stage = main("stage").rearrange("p (h n) -> p h n", h=2)
        wcmp = main("wcmp")
        ring = main("ring").rearrange("p (s n) -> p s n", s=2)
        xT = main("xT").rearrange("p (k t) -> p k t", k=KD)
        proj_flat = main("proj")
        proj = proj_flat.rearrange("p (c t) -> p c t", c=NPROJ)

        xn = main("proj", 9 * D).rearrange("p (n d) -> p n d", n=9)
        oh = main("proj", NOH, 9 * D)[0:BUCKETS + 1, :]
        states = main("proj", 4 * 256, 9 * D + NOH)
        tok_tab = main("proj", DS * P, 10 * D + NOH)[0:BUCKETS + 1, :].rearrange("p (t q) -> p t q", t=DS)

        cst = sb("cst", [P, NCST])
        par = sb("par", [P, NPAR])

        def c_(name):
            a, n = CST_AT[name]
            return cst[:, a:a + n]

        def p_(name, i=0, n=1):
            a = PAR_AT[name][0] + i
            return par[:, a:a + n]

        ident = c_("ident")
        pages = sb("pages", [P, NB], I32)
        row16 = sb("row16", [P, NB], I32)
        row8 = sb("row8", [P, NB, 2], I32)
        tab = sb("tab", [P, H])
        rel = sb("rel", [P, 2 * H])
        diag = sb("diag", [P, H, 2 * P])
        cbias = sb("cbias", [P, H, 60])
        dec_bias = sb("dec_bias", [P, NBIAS])
        kcn = sb("kcn", [P, NB, P])
        vcn = sb("vcn", [P, NB, P])
        half = sb("half", [P, 2, P])
        ext_b = sb("ext_b", [P, 2, NB, CB_W - 1 + DS])
        ext_c = sb("ext_c", [P, 2, NB, CC_W - 1 + DS])
        h0 = sb("h0", [P, 2, NB])
        w_gate = sb("w_gate", [P, KD, 3 * H])
        gate_n = sb("gate_n", [P, NT, 3 * H])
        gate_t = sb("gate_t", [S, 3 * H])
        late = sb("late", [P, 1536])
        scr = late[:, 0:TOK]
        ssq = sb("ssq", [P, 9])
        rstd = sb("rstd", [P, 9])
        spl = sb("spl", [P, 2 * 8])
        cwb = sb("cwb", [P, 2 * 256 + 4 * P])
        w_pw = cwb[:, 0:512].rearrange("p (k n) -> p k n", k=2)
        w_a = cwb[:, 512:768].rearrange("p (c n) -> p c n", c=2)
        w_x = cwb[:, 768:1024].rearrange("p (c n) -> p c n", c=2)

        PS = ctx.enter_context(nc.psum_tensor("PS", [P, 8 * 512], F32))

        def bank(b, n=1):
            return PS[:, 512 * b:512 * (b + n)]

        ld_cst, ld_par, ld_oh, ld_rel, ld_st, ld_pg, ld_wc, ld_wbc, ld_wcmp, ld_wcmp_v = [
            sem(n) for n in ("ld_cst", "ld_par", "ld_oh", "ld_rel", "ld_st", "ld_pg", "ld_wc", "ld_wbc", "ld_wcmp", "ld_wcmp_v")]
        ld_x = [sem(f"ld_x{n}") for n in range(9)]
        w_ld = [sem(f"w_ld{s}") for s in range(2)]
        sq_done, x_scaled, x_turned, xt_done, tab_done, oh_used = [
            sem(n) for n in ("sq_done", "x_scaled", "x_turned", "xt_done", "tab_done", "oh_used")]
        startup_evac, strip_out, strip_in = sem("startup_evac"), sem("strip_out"), sem("strip_in")
        rows_ready, stage_ld, stage_free = sem("rows_ready"), [sem("stage_ld0"), sem("stage_ld1")], [sem("stage_free0"), sem("stage_free1")]
        k_compressed = sem("k_compressed")
        proj_ps = [sem(f"proj_ps{s}") for s in range(2)]
        proj_sb = [sem(f"proj_sb{s}") for s in range(2)]
        mail = [sem("mail0"), sem("mail1")]
        taken = [sem("taken0"), sem("taken1")]
        glu_sig, u_done, uc_done, conv_done, sq_ready, norm_done = [
            sem(n) for n in ("glu_sig", "u_done", "uc_done", "conv_done", "sq_ready", "norm_done")]
        bz_silu, gates_done, h_done, c_done, scan_in, silu_n = [
            sem(n) for n in ("bz_silu", "gates_done", "h_done", "c_done", "scan_in", "silu_n")]
        a_done, th_done, th_sqrt, mean_sq, rms = [sem(n) for n in ("a_done", "th_done", "th_sqrt", "mean_sq", "rms")]
        var_rt = sem("var_rt")
        st_sb, so_out, out_done = sem("st_sb"), sem("so_out"), sem("out_done")
        gate_done = sem("gate_done")
        SEM = {}

        def mail_bank(m):
            return bank(6 + m % 2)

        def post(pe, m, last):
            last.then_inc(mail[m % 2], 1)

        def bank_free(eng, m):
            if m >= 2:
                eng.wait_ge(taken[m % 2], m // 2)

        def posted(eng, m):
            eng.wait_ge(mail[m % 2], m // 2 + 1)

        M_ST = 0
        M_GATE = 2
        M_MEAN = 14
        M_VAR = 20
        M_PW = 26
        M_H = 32
        M_G = 33
        M_END = 34
        CC = [(c, t0, n) for c in range(2) for t0, n in CHUNKS]

        block = ctx.enter_context(nc.Block())

        def sp_startup(sp):
            sp.dma_start(cst[:, :], dram["constants"]).then_inc(ld_cst, 16)
            for n in range(NT):
                sp.dma_start(xn[:, n, :], dram["x_prompt"][n * P:(n + 1) * P, :]).then_inc(ld_x[n], 16)
            sp.dma_start(xn[0:S, 8, :], dram["x_sample"]).then_inc(ld_x[8], 16)
            for s in range(2):
                sp.dma_start(ring[:, s, :], dram["w_tiles"][s]).then_inc(w_ld[s], 16)
            sp.wait_ge(startup_evac, 5)
            sp.dma_start(scratch["strip"], strip[0:H, :].rearrange("h (o c) -> h o c", o=1).to_broadcast([H, P, SKEW])).then_inc(strip_out, 16)
            sp.wait_ge(strip_out, 16)
            sp.dma_start(diag[:, :, :], scratch["skewed"]).then_inc(strip_in, 16)

        def sp_project(sp):
            with sp.Fori(1, NPROJ // 2) as i:
                for s in range(2):
                    sp.wait_ge(proj_ps[s], i)
                    sp.dma_start(ring[:, s, :], dram["w_tiles"][bass.ds(i * 2 + s, 1)].rearrange("a p n -> (a p) n")).then_inc(w_ld[s], 16)

        def sp_states(sp):
            sp.dma_start(outs[15][0, :, 0:CB_W - 1 - DS, :], dram["state_conv_b"][:, DS:, :]).then_inc(out_done, 16)
            sp.wait_ge(st_sb, 1)
            sp.dma_start(outs[14][0, 0], so[0:CB_W - 1, 0, :]).then_inc(so_out, 16)
            sp.dma_start(outs[15][0, :, CB_W - 1 - DS:, :], so[0:S, 1, :]).then_inc(so_out, 16)
            sp.wait_ge(st_sb, 2)
            sp.dma_start(outs[16][0, 0], so[0:3, 2, :]).then_inc(so_out, 16)
            for b in range(NB):
                sp.dma_start(outs[17][0, b], so[b * DS + DS - 3:(b + 1) * DS, 3, :]).then_inc(so_out, 16)
            sp.wait_ge(st_sb, 3)
            sp.dma_start(outs[18][0], so[0:1, 4, :]).then_inc(so_out, 16)
            sp.dma_start(outs[19][0], so[1:1 + NB, 4, :]).then_inc(so_out, 16)

        strip = late[:, 0:SKEW]
        so = wcmp[0:S, 0:5 * 256].rearrange("p (a c) -> p a c", a=5)

        def pool_startup(pool):
            pool.memset(cbias[:, :, 0:24], 0.0)
            pool.memset(cbias[:, :, 32:60], NEG).then_inc(tab_done, 1)

        def pool_compress(pool):
            pool.wait_ge(rows_ready, 1)
            for n in range(2 * NB):
                src = dram["cmp_k"] if n < NB else dram["cmp_v"]
                if n == NB:
                    pool.wait_ge(k_compressed, 1)
                    pool.dma_start(wcmp, dram["w_cmp_v"].to_broadcast([P, L_CMP * HD])).then_inc(ld_wcmp_v, 16)
                for h in range(2):
                    if n >= 1:
                        pool.wait_ge(stage_free[h], n)
                    pool.indirect_dma_start(stage[:, h, :], None, src,
                                            bass.IndirectOffsetOnAxis(row8[:, n % NB, h:h + 1], 0)).then_inc(stage_ld[h], 16)

        def act_startup(act):
            act.dma_start(rel[0:BUCKETS, 0:H], dram["rel_bias"]).then_inc(ld_rel, 16)
            act.dma_start(rel[0:BUCKETS, H:2 * H], dram["rel_bias"][BUCKETS - 1:BUCKETS, :].to_broadcast([BUCKETS, H])).then_inc(ld_rel, 16)
            act.dma_start(pages[:, :], dram["pages"]).then_inc(ld_pg, 16)
            act.dma_start(par[:, :], dram["parameters"]).then_inc(ld_par, 16)
            act.dma_start(oh, dram["one_hot"]).then_inc(ld_oh, 16)
            act.dma_start(wcmp, dram["w_cmp_k"].to_broadcast([P, L_CMP * HD])).then_inc(ld_wcmp, 16)
            act.dma_start(states[0:120, 0:512].rearrange("p (a c) -> p a c", a=2), dram["state_conv_b"].rearrange("(a b) t c -> (b t) a c", a=2)).then_inc(ld_st, 16)
            act.dma_start(states[0:24, 512:768], dram["state_conv_c"]).then_inc(ld_st, 16)
            act.dma_start(states[0:NB, 768:1024], dram["state_rglru"]).then_inc(ld_st, 16)
            act.dma_start(w_gate[:, :, :], dram["w_gate"]).then_inc(ld_wc, 16)
            act.dma_start(cwb[:, :], dram["w_small"]).then_inc(ld_wbc, 16)
            def root(n):
                rows = P if n < NT else S
                act.wait_ge(mean_sq, n + 1)
                act.activation(rstd[0:rows, n:n + 1], rstd[0:rows, n:n + 1], ACT.Sqrt).then_inc(rms, 1)
            for n in range(9):
                rows = P if n < NT else S
                act.wait_ge(ld_x[n], 16)
                act.drain()
                act.activation(late[0:rows, 0:D], xn[0:rows, n, :], ACT.Square, accum_out=ssq[0:rows, n:n + 1]).then_inc(sq_done, 1)
                if n >= 1:
                    root(n - 1)
            root(8)
            act.wait_ge(oh_used, 1)
            act.wait_ge(tab_done, 2)
            act.activation(cbias[:, :, 24:32], bank(6)[:, 448:512].rearrange("p (x h) -> p h x", h=H), ACT.Copy).then_inc(startup_evac, 1)
            act.activation(dec_bias[:, 0:NBIAS - WIN], bank(4)[:, 0:NBIAS - WIN], ACT.Copy).then_inc(startup_evac, 1)
            act.activation(dec_bias[:, NBIAS - WIN:], bank(5), ACT.Copy).then_inc(startup_evac, 1)
            act.activation(h0[:, :, :], bank(6)[:, 432:448].rearrange("p (c b) -> p c b", c=2), ACT.Copy).then_inc(startup_evac, 1)
            act.wait_ge(sq_done, 9)
            act.activation(strip[0:H, :], bank(6)[0:H, 0:SKEW], ACT.Copy).then_inc(startup_evac, 1)
            act.activation(ext_c[:, :, :, 0:CC_W - 1], bank(6)[:, 384:432].rearrange("p (c b t) -> p c b t", c=2, b=NB), ACT.Copy).then_inc(startup_evac, 1)
            for c in range(2):
                last = act.activation(ext_b[:, c, :, 0:CB_W - 1],
                                      bank(7)[:, 240 * c:240 * (c + 1)].rearrange("p (b t) -> p b t", b=NB), ACT.Copy)
            last.then_inc(startup_evac, 1)
            for s in range(2):
                act.activation(spl[:, 14 + s:15 + s], c_("page4"), ACT.Copy).then_inc(proj_sb[s], 1)

        def act_project(act, a, b):
            with act.Fori(a, b) as i:
                for s in range(2):
                    act.wait_ge(proj_ps[s], i + 1)
                    act.activation(proj_flat[:, bass.ds(i * 2 * TOK + s * TOK, TOK)], PS[:, 1536 * s:1536 * s + TOK], ACT.Copy).then_inc(proj_sb[s], 1)

        def act_bc_inputs(act):
            act.drain()
            for c in range(2):
                act.activation(proj[:, GLU_G + c, :], proj[:, GLU_G + c, :], ACT.Sigmoid).then_inc(glu_sig, 1)
            for c in range(2):
                act.activation(proj[:, ZB + c, :], proj[:, ZB + c, :], ACT.Silu)
                last = act.activation(proj[:, ZC + c, :], proj[:, ZC + c, :], ACT.Silu)
            last.then_inc(bz_silu, 1)

        def act_states(act):
            posted(act, M_ST)
            act.activation(so[0:CB_W - 1, 0, :], mail_bank(M_ST)[0:CB_W - 1, 0:256], ACT.Copy)
            act.activation(so[0:S, 1, :], mail_bank(M_ST)[0:S, 256:512], ACT.Copy)
            act.drain()
            act.drain().then_inc(taken[0], 1)
            act.drain().then_inc(st_sb, 1)
            posted(act, M_ST + 1)
            act.activation(so[0:3, 2, :], mail_bank(M_ST + 1)[0:3, 0:256], ACT.Copy)
            act.activation(so[0:S, 3, :], mail_bank(M_ST + 1)[0:S, 256:512], ACT.Copy)
            act.drain()
            act.drain().then_inc(taken[1], 1)
            act.drain().then_inc(st_sb, 1)

        r_gate = lambda c: proj[:, XC + c, :]

        def act_softplus(act):
            act.wait_ge(ld_par, 16)
            act.activation(spl[:, 0:2], p_("lam", 0, 2), ACT.Abs)
            act.drain()
            act.activation(spl[:, 2:4], spl[:, 0:2], ACT.Exp, scale=-1.0).then_inc(a_done, 1)
            act.wait_ge(th_done, 1)
            act.activation(spl[:, 6:8], spl[:, 4:6], ACT.Ln).then_inc(a_done, 1)

        def act_gates(act):
            for k, (c, t0, n) in enumerate(CC + CC):
                m = M_GATE + k
                posted(act, m)
                dst = (r_gate(c) if k < 6 else i_gate[c])[:, t0:t0 + n]
                bias = p_("b_a" if k < 6 else "b_x", c)
                act.activation(dst, mail_bank(m)[:, 0:n], ACT.Sigmoid, bias=bias).then_inc(taken[m % 2], 1)
            act.drain()
            act.drain().then_inc(gates_done, 1)

        def act_decay(act):
            for c in range(2):
                act.wait_ge(scan_in, c + 1)
                act.activation(i_gate[c], r_gate(c), ACT.Tanh, scale=spl[:, 10 + c:11 + c]).then_inc(a_done, 1)
                act.drain()
                act.activation(r_gate(c), r_gate(c), ACT.Exp, scale=spl[:, 12 + c:13 + c]).then_inc(a_done, 1)
            for c in range(2):
                act.wait_ge(th_done, c + 2)
                act.activation(i_gate[c], i_gate[c], ACT.Sqrt).then_inc(th_sqrt, 1)

        def act_squares(act):
            for k, (c, t0, n) in enumerate(CC):
                act.wait_ge(norm_done, k + 1)
                act.activation(scr2[c][:, t0:t0 + n], conv[c][:, t0:t0 + n], ACT.Square).then_inc(sq_ready, 1)

        def act_var(act):
            for k, (c, t0, n) in enumerate(CC):
                act.wait_ge(var_rt, 6)
                act.activation(scr2[c][:, t0:t0 + n], scr2[c][:, t0:t0 + n], ACT.Sqrt).then_inc(var_rt, 1)

        def act_swish(act):
            for c in range(2):
                act.wait_ge(norm_done, 6 + 3 * (c + 1))
                act.activation(conv[c], conv[c], ACT.Silu, scale=p_("gn_gain", c), bias=p_("gn_bias", c)).then_inc(silu_n, 1)

        def act_last_states(act):
            posted(act, M_H)
            act.activation(so[0:1 + NB, 4, :], mail_bank(M_H)[0:1 + NB, 0:256], ACT.Copy).then_inc(taken[M_H % 2], 1)
            act.wait_ge(taken[M_H % 2], M_H // 2 + 1)
            act.drain().then_inc(st_sb, 1)

        def act_branch_gates(act):
            posted(act, M_G)
            act.activation(gate_n[:, :, :], mail_bank(M_G)[:, 0:NT * 3 * H].rearrange("p (n c) -> p n c", n=NT), ACT.Sigmoid)
            act.activation(gate_t[:, :], mail_bank(M_G)[0:S, 256:256 + 3 * H], ACT.Sigmoid)
            act.drain()
            act.drain().then_inc(taken[M_G % 2], 1)
            act.drain().then_inc(gate_done, 1)

        conv = [proj[:, GLU_G + c, :] for c in range(2)]
        uu = [proj[:, GLU_V + c, :] for c in range(2)]
        i_gate = [main("stage", TOK), main("stage", TOK, TOK)]
        scr2 = [main("stage", TOK, 2 * TOK), scr]

        def dve_startup(dve):
            dve.wait_ge(ld_rel, 32)
            dve.memset(tab[BUCKETS:BUCKETS + 1, :], NEG)
            dve.tensor_tensor(tab[0:BUCKETS, :], rel[0:BUCKETS, 0:H], rel[0:BUCKETS, H:2 * H], ALU.subtract)
            dve.memset(tok_tab, 0.0)
            dve.drain()
            for t in range(DS):
                for b2 in range(2):
                    dve.tensor_copy(tok_tab[:, t, b2 * Q:(b2 + 1) * Q].rearrange("p (g t r) -> p g t r", g=G, r=R)[:, :, t, :],
                                    tab[0:BUCKETS + 1, :].rearrange("p (g r) -> p g r", g=G))
            dve.wait_ge(ld_cst, 16)
            dve.drain().then_inc(tab_done, 1)
            dve.wait_ge(ld_pg, 16)
            dve.tensor_scalar(row16[:, :], pages[:, :], 4.0, c_("page4"), ALU.mult, ALU.add)
            dve.drain()
            for h in range(2):
                last = dve.tensor_scalar(row8[:, :, h], row16[:, :], 2.0, float(h), ALU.mult, ALU.add)
            last.then_inc(rows_ready, 1)
            dve.wait_ge(ld_par, 16)

            def square(n):
                rows = P if n < NT else S
                dve.wait_ge(sq_done, n + 1)
                dve.tensor_scalar(rstd[0:rows, n:n + 1], ssq[0:rows, n:n + 1], 1.0 / D, EPS, ALU.mult, ALU.add).then_inc(mean_sq, 1)

            def scale(n):
                rows = P if n < NT else S
                dve.wait_ge(rms, n + 1)
                dve.reciprocal(rstd[0:rows, n:n + 1], rstd[0:rows, n:n + 1])
                dve.drain()
                dve.tensor_scalar(xn[0:rows, n, :], xn[0:rows, n, :], rstd[0:rows, n:n + 1], None, ALU.mult).then_inc(x_scaled, 1)

            def evac(n):
                w = P if n < NT else S
                for h in range(2):
                    m = 2 * n + h
                    dve.wait_ge(x_turned, m + 1)
                    src = bank(m % 4).rearrange("p (k t) -> p k t", k=4)[:, :, 0:w]
                    g = p_("g_pre", 4 * h, 4).rearrange("p (k o) -> p k o", o=1).to_broadcast([P, 4, w])
                    dve.tensor_tensor(xT[:, 4 * h:4 * h + 4, n * P:n * P + w], src, g, ALU.mult).then_inc(xt_done, 1)
            for n in range(11):
                if n < 9:
                    square(n)
                if 1 <= n < 10:
                    scale(n - 1)
                if n >= 2:
                    evac(n - 2)

        def dve_compress(dve, v):
            dst = vcn if v else kcn
            dve.wait_ge(ld_wcmp_v if v else ld_wcmp, 16)
            w = wcmp.rearrange("p (j d) -> p j d", j=L_CMP)
            with dve.Fori(0, NB) as b:
                for h in range(2):
                    dve.wait_ge(stage_ld[h], 16 * b + 16 * (NB * v + 1))
                    for g in range(G):
                        rows = stage[:, h, :].rearrange("p (j g d) -> p j g d", j=16, g=G)[:, :, g, :]
                        dve.tensor_tensor(rows, rows, w[:, 16 * h:16 * h + 16, :], ALU.mult)
                    dve.drain()
                    dve.tensor_reduce(half[:, h, :], stage[:, h, :].rearrange("p (j c) -> p c j", j=16), X, ALU.add).then_inc(stage_free[h], 1)
                dve.drain()
                dve.tensor_tensor(dst[:, bass.ds(b, 1), :].rearrange("p o c -> p (o c)"), half[:, 0, :], half[:, 1, :], ALU.add)
                dve.drain()
            dve.drain().then_inc(k_compressed, 1)

        def dve_u(dve):
            dve.wait_ge(startup_evac, 7)
            for c in range(2):
                dve.wait_ge(glu_sig, c + 1)
                dve.tensor_tensor(uu[c], uu[c], proj[:, GLU_G + c, :], ALU.mult)
            dve.drain()
            for c in range(2):
                dve.tensor_copy(ext_b[:, c, :, CB_W - 1:], uu[c][:, T:].rearrange("p (b t) -> p b t", b=NB))
                last = dve.tensor_copy(ext_c[:, c, :, CC_W - 1:], proj[:, XC + c, T:].rearrange("p (b t) -> p b t", b=NB))
            last.then_inc(u_done, 1)
            dve.drain()

        def taps(dve, dst, src, ext, width, w, b):
            full = dst[:, 0:T]
            smp = dst[:, T:].rearrange("p (b t) -> p b t", b=NB)
            dve.tensor_scalar(full, src[:, 0:T], w(width - 1), b, ALU.mult, ALU.add)
            dve.tensor_scalar(smp, ext[:, :, width - 1:], w(width - 1), b, ALU.mult, ALU.add)
            for k in range(width - 1):
                lag = width - 1 - k
                dve.drain()
                dve.scalar_tensor_tensor(full[:, lag:], src[:, 0:T - lag], w(k), full[:, lag:], ALU.mult, ALU.add)
                dve.scalar_tensor_tensor(smp, ext[:, :, k:k + DS], w(k), smp, ALU.mult, ALU.add)

        def dve_conv_b(dve):
            for c in range(2):
                taps(dve, conv[c], uu[c], ext_b[:, c], CB_W, lambda k: p_("conv_b_w", c * CB_W + k), p_("conv_b_b", c))
            dve.drain()
            dve.drain().then_inc(conv_done, 1)

        def dve_conv_c(dve):
            dve.wait_ge(mail[0], 1)
            for c in range(2):
                taps(dve, uu[c], proj[:, XC + c, :], ext_c[:, c], CC_W, lambda k: p_("conv_c_w", c * CC_W + k), p_("conv_c_b", c))
            dve.drain()
            dve.drain().then_inc(uc_done, 1)

        def dve_softplus(dve):
            dve.wait_ge(a_done, 1)
            dve.tensor_scalar(spl[:, 4:6], spl[:, 2:4], 1.0, None, ALU.add).then_inc(th_done, 1)
            dve.drain()
            dve.tensor_scalar(spl[:, 0:2], spl[:, 4:6], 1.0, None, ALU.subtract)
            dve.drain()
            dve.tensor_scalar(spl[:, 8:10], spl[:, 0:2], 0.0, None, ALU.is_equal)
            dve.drain()
            dve.tensor_tensor(spl[:, 0:2], spl[:, 0:2], spl[:, 8:10], ALU.add)
            dve.wait_ge(a_done, 2)
            dve.tensor_tensor(spl[:, 6:8], spl[:, 6:8], spl[:, 8:10], ALU.add)
            dve.drain()
            dve.reciprocal(spl[:, 0:2], spl[:, 0:2])
            dve.drain()
            dve.tensor_tensor(spl[:, 6:8], spl[:, 6:8], spl[:, 0:2], ALU.mult)
            dve.drain()
            dve.tensor_tensor(spl[:, 6:8], spl[:, 6:8], spl[:, 2:4], ALU.mult)
            dve.tensor_scalar(spl[:, 8:10], p_("lam", 0, 2), -1.0, 0.0, ALU.mult, ALU.max)
            dve.drain()
            dve.tensor_tensor(spl[:, 6:8], spl[:, 6:8], spl[:, 8:10], ALU.add)
            dve.drain()
            dve.tensor_scalar(spl[:, 10:12], spl[:, 6:8], 8.0, None, ALU.mult)
            dve.tensor_scalar(spl[:, 12:14], spl[:, 6:8], -8.0, None, ALU.mult)
            dve.drain()

        def dve_scan(dve):
            dve.wait_ge(gates_done, 1)
            for c in range(2):
                dve.tensor_tensor(uu[c], uu[c], i_gate[c], ALU.mult).then_inc(scan_in, 1)
            for c in range(2):
                a, th, iu = r_gate(c), i_gate[c], uu[c]
                dve.wait_ge(a_done, 2 + 2 * (c + 1))
                sq = scr
                dve.tensor_tensor(sq, a, a, ALU.mult)
                dve.drain()
                dve.scalar_tensor_tensor(th, sq, 1.0, th, ALU.add, ALU.mult)
                dve.drain().then_inc(th_done, 1)
                dve.wait_ge(th_sqrt, c + 1)
                dve.tensor_tensor(iu, iu, th, ALU.mult)
                starts = lambda x: x[:, T:].rearrange("p (b t) -> p b t", b=NB)[:, :, 0]
                dve.tensor_tensor(h0[:, c, :], h0[:, c, :], starts(a), ALU.mult)
                dve.drain()
                dve.tensor_tensor(starts(iu), starts(iu), h0[:, c, :], ALU.add)
                dve.memset(starts(a), 0.0)
                dve.drain()
                dve.tensor_tensor_scan(th, a, iu, 0.0, ALU.mult, ALU.add).then_inc(h_done, 1)
                dve.drain()
                dve.tensor_tensor(proj[:, ZC + c, :], proj[:, ZC + c, :], th, ALU.mult)

        def dve_mean(dve):
            for k, (c, t0, n) in enumerate(CC):
                m = M_MEAN + k
                posted(dve, m)
                y = conv[c][:, t0:t0 + n]
                dve.tensor_tensor(y, y, mail_bank(m)[:, 0:n], ALU.subtract).then_inc(taken[m % 2], 1)
                dve.wait_ge(taken[m % 2], m // 2 + 1)
                dve.drain().then_inc(norm_done, 1)

        def dve_var(dve):
            for k, (c, t0, n) in enumerate(CC):
                m = M_VAR + k
                posted(dve, m)
                y, v = conv[c][:, t0:t0 + n], scr2[c][:, t0:t0 + n]
                dve.tensor_scalar(v, mail_bank(m)[:, 0:n], EPS, None, ALU.add).then_inc(taken[m % 2], 1)
                dve.wait_ge(taken[m % 2], m // 2 + 1)
                dve.drain().then_inc(var_rt, 1)
            for k, (c, t0, n) in enumerate(CC):
                y, v = conv[c][:, t0:t0 + n], scr2[c][:, t0:t0 + n]
                dve.wait_ge(var_rt, 7 + k)
                dve.reciprocal(v, v)
                dve.drain()
                dve.tensor_tensor(y, y, v, ALU.mult).then_inc(norm_done, 1)

        def dve_pointwise(dve):
            dve.wait_ge(bz_silu, 1)
            for k, (c, t0, n) in enumerate(CC):
                m = M_PW + k
                posted(dve, m)
                z = proj[:, ZB + c, t0:t0 + n]
                dve.tensor_tensor(z, z, mail_bank(m)[:, 0:n], ALU.mult).then_inc(taken[m % 2], 1)

        def pe_startup(pe):
            pe.wait_ge(ld_cst, 16)
            for n in range(9):
                pe.wait_ge(x_scaled, n + 1)
                rows = P if n < NT else S
                for h in range(2):
                    m = 2 * n + h
                    if m >= 4:
                        pe.wait_ge(xt_done, m - 3)
                    for k in range(4):
                        kk = 4 * h + k
                        last = pe.transpose(bank(m % 4)[:, k * P:k * P + rows], xn[0:rows, n, kk * P:(kk + 1) * P], ident[0:rows, 0:rows])
                    last.then_inc(x_turned, 1)
            pe.wait_ge(ld_oh, 16)
            pe.wait_ge(tab_done, 2)
            K = BUCKETS + 1
            for n in range(8):
                pe.matmul(bank(6)[:, 448 + n * H:448 + (n + 1) * H], oh[:, n * P:(n + 1) * P], tab[0:K, :], start=True, stop=True)
            for first, n, b in ((0, NBIAS - WIN, 4), (NBIAS - WIN, WIN, 5)):
                for t in range(DS):
                    a = OH_DEC + t * NBIAS + first
                    pe.matmul(bank(b)[:, 0:n], tok_tab[:, t, :], oh[:, a:a + n], start=(t == 0), stop=(t == DS - 1))
            pe.matmul(bank(6)[0:H, 0:SKEW], tab[0:K, :], oh[:, NOH - SKEW:], start=True, stop=True)
            pe.wait_ge(ld_st, 48)
            for c in range(2):
                cols = slice(c * P, (c + 1) * P)
                pe.transpose(bank(6)[:, 384 + 24 * c:408 + 24 * c], states[0:24, 512 + c * P:512 + (c + 1) * P], ident[0:24, 0:24])
                pe.transpose(bank(6)[:, 432 + NB * c:440 + NB * c], states[0:NB, 768 + c * P:768 + (c + 1) * P], ident[0:NB, 0:NB])
                for a in range(2):
                    last = pe.transpose(bank(7)[:, 240 * c + 120 * a:240 * c + 120 * (a + 1)],
                                        states[0:120, 256 * a + c * P:256 * a + (c + 1) * P], ident[0:120, 0:120])
            last.then_inc(oh_used, 1)
            pe.wait_ge(xt_done, 18)

        def pe_project(pe, a, b):
            with pe.Fori(a, b) as i:
                for s in range(2):
                    pe.wait_ge(w_ld[s], i * 16 + 16)
                    pe.wait_ge(proj_sb[s], i + 1)
                    for t0, n in CHUNKS:
                        for k in range(KD):
                            last = pe.matmul(PS[:, 1536 * s + t0:1536 * s + t0 + n], ring[:, s, k * P:(k + 1) * P],
                                             xT[:, k, t0:t0 + n], start=(k == 0), stop=(k == KD - 1))
                    last.then_inc(proj_ps[s], 1)

        def pe_states(pe):
            pe.wait_ge(startup_evac, 7)
            pe.wait_ge(u_done, 1)
            b = mail_bank(M_ST)
            for c in range(2):
                pe.transpose(b[0:CB_W - 1, c * P:(c + 1) * P], uu[c][:, T - CB_W + 1:T], ident)
                last = pe.transpose(b[0:S, 256 + c * P:256 + (c + 1) * P], uu[c][:, T:], ident)
            post(pe, M_ST, last)
            b = mail_bank(M_ST + 1)
            for c in range(2):
                x = proj[:, XC + c, :]
                pe.transpose(b[0:3, c * P:(c + 1) * P], x[:, T - 3:T], ident)
                last = pe.transpose(b[0:S, 256 + c * P:256 + (c + 1) * P], x[:, T:], ident)
            post(pe, M_ST + 1, last)

        def pe_gates(pe):
            pe.wait_ge(ld_wbc, 16)
            pe.wait_ge(uc_done, 1)
            for k, (c, t0, n) in enumerate(CC + CC):
                m = M_GATE + k
                bank_free(pe, m)
                post(pe, m, pe.matmul(mail_bank(m)[:, 0:n], (w_a if k < 6 else w_x)[:, c, :], uu[c][:, t0:t0 + n], start=True, stop=True))

        def pe_mean(pe):
            pe.wait_ge(conv_done, 1)
            for k, (c, t0, n) in enumerate(CC):
                m = M_MEAN + k
                bank_free(pe, m)
                post(pe, m, pe.matmul(mail_bank(m)[:, 0:n], c_("groupmean"), conv[c][:, t0:t0 + n], start=True, stop=True))

        def pe_var(pe):
            for k, (c, t0, n) in enumerate(CC):
                m = M_VAR + k
                pe.wait_ge(sq_ready, k + 1)
                bank_free(pe, m)
                post(pe, m, pe.matmul(mail_bank(m)[:, 0:n], c_("groupmean"), scr2[c][:, t0:t0 + n], start=True, stop=True))

        def pe_pointwise(pe):
            pe.wait_ge(silu_n, 2)
            for k, (c, t0, n) in enumerate(CC):
                m = M_PW + k
                bank_free(pe, m)
                for kk in range(2):
                    last = pe.matmul(mail_bank(m)[:, 0:n], w_pw[:, kk, c * P:(c + 1) * P], conv[kk][:, t0:t0 + n], start=(kk == 0), stop=(kk == 1))
                post(pe, m, last)

        def pe_last_states(pe):
            pe.wait_ge(h_done, 2)
            m = M_H
            bank_free(pe, m)
            for c in range(2):
                last = pe.transpose(mail_bank(m)[0:1 + NB, c * P:(c + 1) * P], i_gate[c][:, T - 1::DS], ident)
            post(pe, m, last)

        def pe_branch_gates(pe):
            pe.wait_ge(ld_wc, 16)
            m = M_G
            bank_free(pe, m)
            b = mail_bank(m)
            for n in range(NT):
                for k in range(KD):
                    pe.matmul(b[:, n * 24:(n + 1) * 24], xT[:, k, n * P:(n + 1) * P], w_gate[:, k, :], start=(k == 0), stop=(k == KD - 1))
            for k in range(KD):
                last = pe.matmul(b[0:S, 256:256 + 3 * H], xT[:, k, T:], w_gate[:, k, :], start=(k == 0), stop=(k == KD - 1))
            post(pe, m, last)

        def carve(a, n):
            return MAIN[:, a:a + n]

        X0 = at["xT"]
        NAT = [VS, VW, KC, VC, KS, KW]
        nat = carve(X0, 6 * 9 * P).rearrange("p (s n c) -> p s n c", s=6, n=9)
        a1 = X0 + 6 * 9 * P
        ptc = carve(a1, NT * G * P).rearrange("p (i g q) -> p i g q", i=NT, g=G)
        qpad = carve(a1 + 2048, 2 * T).rearrange("p (g t) -> p g t", g=G)
        vcur = carve(a1 + 4096, P)
        sc = carve(a1 + 4224, 2048)
        psel, pwin = sc[:, 0:T], sc[:, T:T + 5 * P]
        pt = carve(a1 + 6272, 2 * 512).rearrange("p (b n) -> p b n", b=2)
        vb = carve(a1 + 7296, R * P).rearrange("p (r c) -> p r c", r=R)
        kcs = carve(a1 + 7808, 64).rearrange("p (k n) -> p k n", k=2)
        kcb = carve(a1 + 7872, 64)
        vc4 = carve(a1 + 7936, P)
        assert a1 + 8064 <= FREE
        kd = carve(0, 2 * PAST).rearrange("p (b n) -> p b n", b=2)
        vd = carve(X0, 2 * PAST).rearrange("p (b n) -> p b n", b=2)
        selectors = carve(0, 4 * 3 * P + H)
        SN = PAST + 2 * DS + WIN
        sd = carve(X0 + 8192, SN)
        ktc = carve(X0 + 8192 + SN, 2 * 512).rearrange("p (b n) -> p b n", b=2)
        ptd2 = carve(X0 + 8192 + SN + 1024, 2 * 512).rearrange("p (b n) -> p b n", b=2)
        qcur = carve(X0 + 8192 + SN + 2048, P)
        pcur = carve(X0 + 8192 + SN + 2176, P)
        kncur = carve(X0 + 8192 + SN + 2304, 2 * 2 * DS).rearrange("p (b k t) -> p b k t", b=2, k=2)
        assert X0 + 8192 + SN + 2304 + 2 * 2 * DS <= FREE
        kw_d = diag[:, 0:4, :].rearrange("p h c -> p (h c)").rearrange("p (b n) -> p b n", b=2)
        vw_d = diag[:, 4:8, :].rearrange("p h c -> p (h c)").rearrange("p (b n) -> p b n", b=2)
        kct = late[:, 0:NB * P]
        scd = late[:, NB * P:NB * P + 4 * P].rearrange("p (a n) -> p a n", a=4)
        extb_flat = ext_b[:, :, :, :].rearrange("p c b t -> p (c b t)")
        extc_flat = ext_c[:, :, :, :].rearrange("p c b t -> p (c b t)")
        vccur = late[:, NB * P:NB * P + 2 * P]
        vncur = late[:, NB * P + 2 * P:NB * P + 4 * P]
        ptd = extb_flat[:, 0:4 * P]
        gtmp = extb_flat[:, 512:512 + 12 * H].rearrange("p (a h) -> p a h", h=H)
        mc, lc, top8 = extc_flat[:, 0:64], extc_flat[:, 64:128], extc_flat[:, 128:144]
        vn = cwb
        halves = half[:, :, :].rearrange("p a c -> p (a c)")
        pair4 = halves.rearrange("p (a n) -> p a n", a=4)
        kcn_flat = kcn[:, :, :].rearrange("p b c -> p (b c)")
        qbd = kcn_flat[:, 0:NB * Q].rearrange("p (b q) -> p b q", b=NB)
        vnt = kcn_flat[:, NB * Q:NB * Q + NB * 2 * DS]
        mask2 = kcn_flat[:, 640:768]
        osb = kcn_flat[:, 768:896]
        gd = sb("gd", [P, 4, 3])
        sm = sb("sm", [P, 48])
        topk = kcn_flat[:, 896:968]

        names = """bc_done nat_ps nat_sb nat_out kc_ready vb_ready cmp_ps cmp_max cmp_exp cmp_p cmp_pt_ps cmp_pt kct_ps kct_sb
            qbd_ready dc_sub dc_exp dc_pair dc_p ld_sel imp_used topk_done mask_done vnt_ready vn_sb ptd_sb gd_ready za_silu
            q_ready pair_done qk_s qk_w mx_s mx_w ex_s ex_w p_s p_w pt_ps pt_sb pv o_ps oz
            cur_ready dpair kused vused wkused wvused sd_ps sd_used mx_d ex_d p_d dp_ps o_d o_sb ot_ps z_d
            ld_gp ld_wo y_ps y_sq y_ms y_rt y_free y_out""".split()
        for n in names:
            assert n not in SEM
            SEM[n] = sem(n)
        kd_ld, vd_ld, kw_ld, vw_ld, kt_ps, kt_sb, dp_sb, dv = [[sem(f"{n}{b}") for b in range(2)] for n in
                                                               "kd_ld vd_ld kw_ld vw_ld kt_ps kt_sb dp_sb dv".split()]
        xo_ld, y_st = [sem(f"xo_ld{b}") for b in range(3)], [sem(f"y_st{b}") for b in range(3)]

        M_VC, M_TG, M_DC, M_IMP, M_DPT, M_MASK, M_VN = 34, 35, 36, 37, 38, 39, 40

        def wait_projections(eng):
            for s in range(2):
                eng.wait_ge(proj_sb[s], 1 + NPROJ // 2)

        def pe_natural(pe):
            wait_projections(pe)
            for n in range(9):
                w = P if n < NT else S
                if n >= 2:
                    pe.wait_ge(SEM["nat_sb"], n - 1)
                b = bank(2 * (n % 2), 2)
                for s, c in enumerate(NAT):
                    last = pe.transpose(b[0:w, s * P:(s + 1) * P], proj[:, c, n * P:n * P + w], ident)
                last.then_inc(SEM["nat_ps"], 1)

        def act_natural(act):
            act.wait_ge(taken[M_G % 2], M_G // 2 + 1)
            for n in range(9):
                w = P if n < NT else S
                act.wait_ge(SEM["nat_ps"], n + 1)
                act.activation(nat[0:w, :, n, :], bank(2 * (n % 2), 2)[0:w, 0:6 * P].rearrange("p (s c) -> p s c", s=6), ACT.Copy).then_inc(SEM["nat_sb"], 1)

        def sp_natural(sp):
            for k, key in enumerate(("win_k", "win_v")):
                sp.dma_start(outs[11 + 2 * k][0, :, 0:WIN - DS].rearrange("b w g d -> b w (g d)"), dram[key][:, DS:, :]).then_inc(out_done, 16)
            sp.wait_ge(SEM["nat_sb"], 9)
            for s, o in ((2, 2), (3, 4), (4, 6), (0, 8)):
                sp.dma_start(outs[o][0, 0].rearrange("(n p) g d -> p n (g d)", p=P), nat[:, s, 0:NT, :]).then_inc(SEM["nat_out"], 16)
                sp.dma_start(outs[o + 1][0].rearrange("b t g d -> (b t) (g d)"), nat[0:S, s, 8, :]).then_inc(SEM["nat_out"], 16)
            for s, o in ((5, 10), (1, 12)):
                sp.dma_start(outs[o][0, 0].rearrange("(n p) g d -> p n (g d)", p=P), nat[:, s, NT - WIN // P:NT, :]).then_inc(SEM["nat_out"], 16)
                sp.dma_start(outs[o + 1][0, :, WIN - DS:].rearrange("b t g d -> b t (g d)"), nat[0:S, s, 8, :]).then_inc(SEM["nat_out"], 16)

        def dve_prompt_blocks(dve):
            wait_projections(dve)
            q = proj_flat[:, QT * TOK:(QT + R) * TOK]
            dve.tensor_scalar(q, q, HD ** -0.5, None, ALU.mult)
            dve.memset(kcb, 0.0)
            dve.memset(vb, 0.0)
            for k, (c, w) in enumerate(((KC, "wk"), (VC, "wv"))):
                wb = p_(w, 0, L_CMP).rearrange("p (o j) -> p o j", o=1).to_broadcast([P, T // L_CMP, L_CMP])
                prod = scr[:, 0:T].rearrange("p (n j) -> p n j", j=L_CMP)
                dve.drain()
                dve.tensor_tensor(prod, proj[:, c, 0:T].rearrange("p (n j) -> p n j", j=L_CMP), wb, ALU.mult)
                dve.drain()
                dve.tensor_reduce(kcs[:, k, :], prod, X, ALU.add)
            dve.drain()
            for g in range(G):
                dve.tensor_copy(kcb[g * HD:(g + 1) * HD, g * 32:(g + 1) * 32], kcs[g * HD:(g + 1) * HD, 0, :])
            dve.tensor_copy(vc4.rearrange("p (r n) -> p r n", r=R), kcs[:, 1:2, :].to_broadcast([P, R, 32]))
            dve.drain().then_inc(SEM["kc_ready"], 1)

        def pe_prompt_blocks(pe):
            pe.wait_ge(SEM["kc_ready"], 1)
            bank_free(pe, M_VC)
            post(pe, M_VC, pe.transpose(mail_bank(M_VC)[:, 0:P], vc4, ident))
            pe.wait_ge(SEM["nat_sb"], 9)
            s = bank(0, 4).rearrange("p (i r n) -> p i r n", i=NT, r=R)
            for i in range(NT):
                for r in range(R):
                    last = pe.matmul(s[:, i, r, :], proj[:, QT + r, i * P:(i + 1) * P], kcb, start=True, stop=True)
                last.then_inc(SEM["cmp_ps"], 1)

        def dve_prompt_cmp(dve):
            posted(dve, M_VC)
            for r in range(R):
                last = dve.tensor_copy(vb[32 * r:32 * r + 32, r, :], mail_bank(M_VC)[32 * r:32 * r + 32, 0:P])
            last.then_inc(taken[M_VC % 2], 1)
            s = bank(0, 4).rearrange("p (i r g n) -> p i g r n", i=NT, r=R, g=G)
            o = sc.rearrange("p (i g r n) -> p i g r n", i=NT, r=R, g=G)
            for i in range(NT):
                dve.wait_ge(SEM["cmp_ps"], 2 * (i // 2) + 2)
                b = cbias[:, :, 28 - 4 * i:60 - 4 * i].rearrange("p (g r) n -> p g r n", g=G)
                dve.tensor_tensor(o[:, i], s[:, i], b, ALU.add)
            rows = sc.rearrange("p (h n) -> p h n", n=32)
            spread = lambda x: x.rearrange("p (h o) -> p h o", o=1).to_broadcast([P, 64, 32])
            dve.drain()
            dve.tensor_reduce(mc[:, :], rows, X, ALU.max)
            dve.drain()
            dve.tensor_scalar(mc[:, :], mc[:, :], NEG / 10, None, ALU.max)
            dve.drain()
            dve.tensor_tensor(rows, rows, spread(mc[:, :]), ALU.subtract).then_inc(SEM["cmp_max"], 1)
            dve.wait_ge(SEM["cmp_exp"], 1)
            dve.tensor_reduce(lc[:, :], rows, X, ALU.add)
            dve.drain()
            dve.tensor_scalar(lc[:, :], lc[:, :], 1e-30, None, ALU.max)
            dve.drain()
            dve.reciprocal(lc[:, :], lc[:, :])
            dve.wait_ge(gate_done, 1)
            dve.drain()
            dve.tensor_tensor(lc[:, :].rearrange("p (i h) -> p i h", h=H), lc[:, :].rearrange("p (i h) -> p i h", h=H), gate_n[:, :, 0:H], ALU.mult)
            dve.drain()
            dve.tensor_tensor(rows, rows, spread(lc[:, :]), ALU.mult).then_inc(SEM["cmp_p"], 1)

        def act_prompt_exp(act):
            act.wait_ge(SEM["cmp_max"], 1)
            act.activation(sc, sc, ACT.Exp).then_inc(SEM["cmp_exp"], 1)

        def pe_prompt_turn(pe):
            pe.wait_ge(SEM["cmp_p"], 1)
            for k in range(2 * NT):
                last = pe.transpose(bank(0, 4)[:, k * P:(k + 1) * P], sc[:, k * P:(k + 1) * P], ident)
            last.then_inc(SEM["cmp_pt_ps"], 1)

        def act_prompt_turn(act):
            act.wait_ge(SEM["cmp_pt_ps"], 1)
            flat = ptc.rearrange("p i g q -> p (i g q)")
            for h in range(2):
                act.activation(flat[:, h * T:(h + 1) * T], bank(2 * h, 2), ACT.Copy)
            for c in range(R):
                act.activation(proj[:, ZA + c, :], proj[:, ZA + c, :], ACT.Silu)
            act.drain().then_inc(SEM["cmp_pt"], 1)

        def pe_decode_keys(pe):
            for b in range(NB):
                last = pe.transpose(bank(4, 2)[:, b * P:(b + 1) * P], kcn[:, b, :], ident)
            last.then_inc(SEM["kct_ps"], 1)

        def act_decode_keys(act):
            act.wait_ge(SEM["kct_ps"], 1)
            act.wait_ge(SEM["kc_ready"], 1)
            act.activation(kct, bank(4, 2), ACT.Copy).then_inc(SEM["kct_sb"], 1)

        def dve_decode_queries(dve):
            dve.wait_ge(SEM["kct_sb"], 1)
            dve.memset(kcn_flat[:, 0:NB * Q], 0.0)
            dve.drain()
            for g in range(G):
                rows = slice(g * HD, (g + 1) * HD)
                for r in range(R):
                    dve.tensor_copy(qbd[rows].rearrange("p b (g t r) -> p b g t r", g=G, r=R)[:, :, g, :, r],
                                    proj[rows, QT + r, T:].rearrange("p (b t) -> p b t", b=NB))
            for k, c in enumerate((VS, VW)):
                dve.tensor_copy(vnt.rearrange("p (b k t) -> p b k t", b=NB, k=2)[:, :, k, :], proj[:, c, T:].rearrange("p (b t) -> p b t", b=NB))
            dve.drain().then_inc(SEM["qbd_ready"], 1)

        def sp_selectors(sp):
            sp.wait_ge(SEM["bc_done"], 1)
            sp.wait_ge(mail[M_H % 2], M_H // 2 + 1)
            sp.dma_start(selectors, dram["selectors"]).then_inc(SEM["ld_sel"], 16)

        def pe_decode_cmp(pe):
            pe.wait_ge(SEM["ld_sel"], 16)
            pe.wait_ge(gate_done, 1)
            bank_free(pe, M_TG)
            for pr in range(4):
                last = pe.matmul(mail_bank(M_TG)[:, pr * 24:(pr + 1) * 24], sel(pr, 2)[0:S, :], gate_t[:, :], start=True, stop=True)
            post(pe, M_TG, last)
            pe.wait_ge(SEM["qbd_ready"], 1)
            bank_free(pe, M_DC)
            for b in range(NB):
                last = pe.matmul(mail_bank(M_DC)[Q * (b % 2):Q * (b % 2 + 1), b // 2 * P:(b // 2 + 1) * P], qbd[:, b, :], kct[:, b * P:(b + 1) * P], start=True, stop=True)
            post(pe, M_DC, last)

        def sel(pr, k):
            return selectors[:, (pr * 3 + k) * P:(pr * 3 + k + 1) * P]

        def dve_decode_cmp(dve):
            posted(dve, M_TG)
            hm = selectors[:, 12 * P:].rearrange("p (o h) -> p o h", o=1).to_broadcast([P, 12, H])
            dve.tensor_tensor(gtmp[:, :, :], mail_bank(M_TG)[:, 0:96].rearrange("p (a h) -> p a h", h=H), hm, ALU.mult).then_inc(taken[M_TG % 2], 1)
            dve.wait_ge(taken[M_TG % 2], M_TG // 2 + 1)
            dve.tensor_reduce(gd[:, :, :].rearrange("p a b -> p (a b)"), gtmp[:, :, :], X, ALU.add)
            posted(dve, M_DC)
            spread = lambda x: x.rearrange("p (a o) -> p a o", o=1).to_broadcast([P, 4, P])
            bias = dec_bias[:, 0:NCB].rearrange("p (o n) -> p o n", o=1).to_broadcast([P, 4, P])
            dve.tensor_tensor(scd, mail_bank(M_DC).rearrange("p (a n) -> p a n", a=4), bias, ALU.add).then_inc(taken[M_DC % 2], 1)
            dve.wait_ge(taken[M_DC % 2], M_DC // 2 + 1)
            dve.tensor_reduce(sm[:, 0:4], scd, X, ALU.max)
            dve.drain()
            dve.tensor_tensor(scd, scd, spread(sm[:, 0:4]), ALU.subtract).then_inc(SEM["dc_sub"], 1)
            dve.wait_ge(SEM["dc_exp"], 1)
            dve.tensor_reduce(sm[:, 4:8], scd, X, ALU.add)
            dve.drain()
            dve.reciprocal(sm[:, 4:8], sm[:, 4:8])
            dve.drain()
            dve.tensor_tensor(scd, scd, spread(sm[:, 4:8]), ALU.mult)
            dve.drain()
            two = scd.rearrange("p a (n k) -> p a n k", k=2)
            dve.tensor_tensor(pair4, two[:, :, :, 0], two[:, :, :, 1], ALU.add).then_inc(SEM["dc_pair"], 1)
            dve.drain()
            dve.tensor_tensor(scd, scd, spread(gd[:, :, 0]), ALU.mult).then_inc(SEM["dc_p"], 1)

        def act_decode_exp(act):
            act.wait_ge(SEM["dc_sub"], 1)
            act.activation(scd, scd, ACT.Exp).then_inc(SEM["dc_exp"], 1)

        def pe_importance(pe):
            pe.wait_ge(SEM["dc_pair"], 1)
            bank_free(pe, M_IMP)
            for pr in range(4):
                last = pe.matmul(mail_bank(M_IMP)[:, 0:NBLK], sel(pr, 1), pair4[:, pr, :], start=(pr == 0), stop=(pr == 3))
            post(pe, M_IMP, last)
            pe.wait_ge(SEM["dc_p"], 1)
            bank_free(pe, M_DPT)
            for pr in range(4):
                last = pe.transpose(mail_bank(M_DPT)[:, pr * P:(pr + 1) * P], scd[:, pr, :], ident)
            post(pe, M_DPT, last)

        def dve_select(dve):
            posted(dve, M_IMP)
            dve.tensor_copy(topk[:, 1:NBLK - 1], mail_bank(M_IMP)[:, 1:NBLK - 1]).then_inc(taken[M_IMP % 2], 1)
            dve.memset(topk[:, 0:1], FORCE)
            dve.memset(topk[:, NBLK - 1:NBLK + 1], FORCE)
            for k in range(TOP_K // 8):
                dve.drain()
                dve.max(top8[:, 8 * k:8 * k + 8], topk[:, 0:NBLK + 1])
                dve.drain()
                dve.match_replace(topk[:, 0:NBLK + 1], top8[:, 8 * k:8 * k + 8], topk[:, 0:NBLK + 1], -2.0)
            dve.drain()
            dve.tensor_scalar(topk[:, 0:NBLK], topk[:, 0:NBLK], -2.0, NEG, ALU.not_equal, ALU.mult).then_inc(SEM["topk_done"], 1)

        def act_decode_turn(act):
            posted(act, M_DPT)
            act.activation(ptd, mail_bank(M_DPT), ACT.Copy).then_inc(taken[M_DPT % 2], 1)

        def pe_masks(pe):
            pe.wait_ge(SEM["topk_done"], 1)
            bank_free(pe, M_MASK)
            for pr in range(4):
                last = pe.matmul(mail_bank(M_MASK)[:, pr * NBLK:(pr + 1) * NBLK], sel(pr, 0), topk[:, 0:NBLK], start=True, stop=True)
            post(pe, M_MASK, last)
            for h in range(2):
                m = M_VN + h
                bank_free(pe, m)
                for b in range(4):
                    last = pe.transpose(mail_bank(m)[0:2 * DS, b * P:(b + 1) * P], vnt[:, (4 * h + b) * 2 * DS:(4 * h + b + 1) * 2 * DS], ident)
                post(pe, m, last)

        def act_masks(act):
            posted(act, M_MASK)
            act.activation(halves, mail_bank(M_MASK)[:, 0:4 * NBLK], ACT.Copy).then_inc(taken[M_MASK % 2], 1)
            for h in range(2):
                posted(act, M_VN + h)
                act.activation(vn[0:2 * DS, h * 512:(h + 1) * 512], mail_bank(M_VN + h)[0:2 * DS, :], ACT.Copy).then_inc(taken[(M_VN + h) % 2], 1)

        UNITS = [(i, g) for i in range(NT) for g in range(G)]

        def tiles_of(k):
            i = UNITS[k][0]
            w0 = max(0, i - WIN // P)
            return list(range(i + 1)), list(range(w0, i + 1))

        chunk_of, nch = {}, 0
        for k in range(len(UNITS)):
            for br in range(2):
                ts = tiles_of(k)[br]
                chunk_of[k, br] = [(nch + c, ts[4 * c:4 * c + 4]) for c in range((len(ts) + 3) // 4)]
                nch += len(chunk_of[k, br])
        NCH, NU = nch, len(UNITS)
        assert NCH % 2 == 0

        def dve_pairs_prepare(dve):
            dve.memset(qpad[HD:P, 0, :], 0.0)
            dve.memset(qpad[0:HD, 1, :], 0.0)
            dve.drain().then_inc(SEM["vb_ready"], 1)
            for _ in range(2):
                dve.drain().then_inc(SEM["oz"], 1)

        def act_pairs(act):
            for _ in range(2):
                act.drain().then_inc(SEM["pt_sb"], 1)
            act.wait_ge(SEM["vb_ready"], 1)
            with act.Fori(0, R) as r:
                act.wait_ge(SEM["pair_done"], r + 1)
                for g in range(G):
                    rows = slice(g * HD, (g + 1) * HD)
                    act.activation(qpad[rows, g, :], proj_flat[rows, bass.ds(r * TOK + QT * TOK, T)], ACT.Copy)
                act.activation(vcur, vb[:, bass.ds(r, 1), :].rearrange("p o c -> p (o c)"), ACT.Copy)
                act.drain().then_inc(SEM["q_ready"], 1)

                def evac(k, br):
                    for c, ts in chunk_of[k, br]:
                        act.wait_ge(SEM["pt_ps"], r * NCH + (c + 1))
                        act.wait_ge(SEM["pv"], r * NCH + (c + 1))
                        n = len(ts) * P
                        act.activation(pt[:, c % 2, 0:n], bank(4 + c % 2)[:, 0:n], ACT.Copy).then_inc(SEM["pt_sb"], 1)

                def exp(k, br):
                    n = len(tiles_of(k)[br]) * P
                    act.wait_ge(SEM["mx_s" if br == 0 else "mx_w"], r * NU + (k + 1))
                    act.activation((psel, pwin)[br][:, 0:n], bank(2 * br, 2)[:, 0:n], ACT.Exp, bias=sm[:, 8 + br:9 + br],
                                   accum_out=sm[:, 10 + br:11 + br]).then_inc(SEM["ex_s" if br == 0 else "ex_w"], 1)
                for k in range(NU + 1):
                    for br in range(2):
                        if k >= 1:
                            evac(k - 1, br)
                        if k < NU:
                            exp(k, br)

        def dve_pairs(dve):
            with dve.Fori(0, R) as r:
                def peak(k, br):
                    (i, g), ts = UNITS[k], tiles_of(k)[br]
                    n = len(ts) * P
                    s = bank(2 * br, 2)[:, 0:n]
                    dve.wait_ge(SEM["qk_s" if br == 0 else "qk_w"], r * NU + (k + 1))
                    w = min(n, 2 * P)
                    d = diag[:, bass.ds(r + g * R, 1), 2 * P - w:].rearrange("p o c -> p (o c)")
                    dve.tensor_tensor(s[:, n - w:], s[:, n - w:], d, ALU.add)
                    if br == 1 and i >= WIN // P:
                        dve.tensor_tensor(s[:, 0:P], s[:, 0:P], c_("winmask"), ALU.add)
                    dve.drain()
                    dve.tensor_reduce(sm[:, 8 + br:9 + br], s, X, ALU.max, negate=True).then_inc(SEM["mx_s" if br == 0 else "mx_w"], 1)

                def scale(k, br):
                    (i, g), n = UNITS[k], len(tiles_of(k)[br]) * P
                    dve.wait_ge(SEM["ex_s" if br == 0 else "ex_w"], r * NU + (k + 1))
                    w = sm[:, 12 + br:13 + br]
                    dve.reciprocal(w, sm[:, 10 + br:11 + br])
                    dve.drain()
                    gate = gate_n[:, i, bass.ds(r + ((br + 1) * H + g * R), 1)]
                    p = (psel, pwin)[br][:, 0:n]
                    dve.tensor_scalar(w, w, gate, None, ALU.mult)
                    dve.drain()
                    dve.tensor_scalar(p, p, w, None, ALU.mult).then_inc(SEM["p_s" if br == 0 else "p_w"], 1)
                for k in range(NU + 1):
                    if k < NU:
                        peak(k, 0)
                    if k >= 1:
                        scale(k - 1, 1)
                    if k < NU:
                        peak(k, 1)
                        scale(k, 0)
                    if k >= 1 and UNITS[k - 1][1] == 1:
                        i = UNITS[k - 1][0]
                        dve.wait_ge(SEM["o_ps"], r * NT + (i + 1))
                        z = proj_flat[:, bass.ds(r * TOK + (ZA * TOK + i * P), P)]
                        dve.tensor_tensor(z, bank(6 + i % 2)[:, 0:P], z, ALU.mult).then_inc(SEM["oz"], 1)

        def pe_pairs(pe):
            pe.wait_ge(SEM["cmp_pt"], 1)
            for h in range(2):
                pe.wait_ge(taken[(M_VN + h) % 2], (M_VN + h) // 2 + 1)
            pe.drain().then_inc(SEM["pair_done"], 1)
            for _ in range(2):
                pe.drain().then_inc(SEM["pv"], 1)
            pe.wait_ge(strip_in, 16)
            with pe.Fori(0, R) as r:
                pe.wait_ge(SEM["q_ready"], r + 1)

                def scores(k, br):
                    (i, g), ts = UNITS[k], tiles_of(k)[br]
                    if k >= 1:
                        pe.wait_ge(SEM["ex_s" if br == 0 else "ex_w"], r * NU + k)
                    n, k0 = len(ts) * P, ts[0] * P
                    for a in range(0, n, 512):
                        m = min(512, n - a)
                        last = pe.matmul(bank(2 * br, 2)[:, a:a + m], qpad[:, g, i * P:(i + 1) * P],
                                         proj[:, (KS, KW)[br], k0 + a:k0 + a + m], start=True, stop=True)
                    last.then_inc(SEM["qk_s" if br == 0 else "qk_w"], 1)

                def turn(k, br):
                    pe.wait_ge(SEM["p_s" if br == 0 else "p_w"], r * NU + (k + 1))
                    for c, ts in chunk_of[k, br]:
                        pe.wait_ge(SEM["pt_sb"], r * NCH + (c + 1))
                        for e, t in enumerate(ts):
                            off = (t - tiles_of(k)[br][0]) * P
                            last = pe.transpose(bank(4 + c % 2)[:, e * P:(e + 1) * P], (psel, pwin)[br][:, off:off + P], ident)
                        last.then_inc(SEM["pt_ps"], 1)

                def values(k, br):
                    i, g = UNITS[k]
                    o = bank(6 + i % 2)[g * HD:(g + 1) * HD, 0:P]
                    if br == 0:
                        if g == 0:
                            pe.wait_ge(SEM["oz"], r * NT + (i + 1))
                        pe.matmul(o, vcur[:, g * HD:(g + 1) * HD], ptc[:, i, g, :], start=True, stop=False)
                    for c, ts in chunk_of[k, br]:
                        pe.wait_ge(SEM["pt_sb"], r * NCH + (c + 3))
                        for e, t in enumerate(ts):
                            end = br == 1 and t == i
                            last = pe.matmul(o, nat[:, br, t, g * HD:(g + 1) * HD], pt[:, c % 2, e * P:(e + 1) * P], start=False, stop=end)
                        last.then_inc(SEM["pv"], 1)
                    if br == 1 and g == 1:
                        pe.drain().then_inc(SEM["o_ps"], 1)
                for k in range(NU + 1):
                    if k < NU:
                        scores(k, 0)
                    if k >= 1:
                        turn(k - 1, 0)
                    if k < NU:
                        scores(k, 1)
                    if k >= 1:
                        values(k - 1, 0)
                        turn(k - 1, 1)
                        values(k - 1, 1)
                pe.drain().then_inc(SEM["pair_done"], 1)

        NC = PAST // 512

        def pool_decode(pool):
            for pr in range(4):
                for b2 in range(2):
                    if pr == 0 and b2 == 0:
                        pool.wait_ge(taken[M_MASK % 2], M_MASK // 2 + 1)
                        pool.wait_ge(so_out, 16 * N_SO)
                    elif b2 == 0:
                        pool.wait_ge(SEM["kused"], pr)
                    pool.indirect_dma_start(kd[:, b2, :], None, dram["sel_k"],
                                            bass.IndirectOffsetOnAxis(row16[:, 2 * pr + b2:2 * pr + b2 + 1], 0)).then_inc(kd_ld[b2], 16)
                for b2 in range(2):
                    if b2 == 0 and pr == 0:
                        pool.wait_ge(SEM["pair_done"], R + 1)
                        pool.wait_ge(SEM["nat_out"], 16 * N_NAT)
                    elif b2 == 0:
                        pool.wait_ge(SEM["vused"], pr)
                    pool.indirect_dma_start(vd[:, b2, :], None, dram["sel_v"],
                                            bass.IndirectOffsetOnAxis(row16[:, 2 * pr + b2:2 * pr + b2 + 1], 0)).then_inc(vd_ld[b2], 16)

        def sp_decode(sp):
            for pr in range(4):
                for src, dst, ld, used in ((dram["win_k"], kw_d, kw_ld, "wkused"), (dram["win_v"], vw_d, vw_ld, "wvused")):
                    if pr == 0:
                        sp.wait_ge(SEM["oz"], 2 + NT * R)
                    else:
                        sp.wait_ge(SEM[used], pr)
                    for b2 in range(2):
                        sp.dma_start(dst[:, b2, :], src[2 * pr + b2].rearrange("(p j) c -> p (j c)", p=P)).then_inc(ld[b2], 16)

        def kt_evac(eng, b2, pr):
            copy = (lambda o, i: eng.activation(o, i, ACT.Copy)) if b2 == 0 else (lambda o, i: eng.tensor_copy(o, i))

            def chunk(c):
                eng.wait_ge(kt_ps[b2], pr * (NC + 1) + (c + 1))
                if c >= 1:
                    eng.wait_ge(SEM["sd_ps"], pr * (NC + 1) + c)
                copy(ktc[:, b2, :], bank(2 + b2)).then_inc(kt_sb[b2], 1)
            return chunk

        def pt_evac(eng, par, pr):
            copy = (lambda o, i: eng.activation(o, i, ACT.Copy)) if par == 0 else (lambda o, i: eng.tensor_copy(o, i))
            for c in range(par, NC + 2, 2):
                eng.wait_ge(SEM["dp_ps"], pr * (NC + 2) + (c + 1))
                if c >= 2:
                    eng.wait_ge(dv[par], pr * ((NC + 2) // 2) + c // 2)
                rows = P if c < NC + 1 else 2 * DS
                n = 512 if c < NC + 1 else P
                copy(ptd2[0:rows, par, 0:n], bank(4 + par)[0:rows, 0:n]).then_inc(dp_sb[par], 1)

        def act_decode(act):
            with act.Fori(0, 4) as pr:
                act.wait_ge(SEM["dpair"], pr + 1)
                act.activation(qcur, kcn_flat[:, bass.ds(pr * 2 * Q, 2 * Q)], ACT.Copy)
                act.activation(pcur, ptd[:, bass.ds(pr * P, P)], ACT.Copy)
                act.activation(vccur, vcn_flat[:, bass.ds(pr * 2 * P, 2 * P)], ACT.Copy)
                act.activation(vncur[0:2 * DS, :], vn[0:2 * DS, bass.ds(pr * 2 * P, 2 * P)], ACT.Copy)
                new = proj[:, KS:KW + 1:2, bass.ds(pr * 2 * DS + T, 2 * DS)]
                act.activation(kncur, new.rearrange("p k (b t) -> p b k t", b=2), ACT.Copy)
                act.drain().then_inc(SEM["cur_ready"], 1)
                chunk = kt_evac(act, 0, pr)
                for c in range(NC + 1):
                    chunk(c)
                act.wait_ge(SEM["mx_d"], pr + 1)
                act.activation(sd[:, 0:PAST + DS], sd[:, 0:PAST + DS], ACT.Exp, bias=sm[:, 40:41], accum_out=sm[:, 42:43])
                act.activation(sd[:, PAST + DS:], sd[:, PAST + DS:], ACT.Exp, bias=sm[:, 41:42], accum_out=sm[:, 43:44])
                act.drain().then_inc(SEM["ex_d"], 1)
                pt_evac(act, 0, pr)

        def dve_decode(dve):
            dve.drain().then_inc(SEM["dpair"], 1)
            near = dec_bias[:, NCB:NCB + L_CMP * NEAR].rearrange("p (j e) -> p j e", e=NEAR)
            new = dec_bias[:, NCB + L_CMP * NEAR:NCB + L_CMP * NEAR + DS]
            win = dec_bias[:, NBIAS - WIN:]
            peaks = sm[:, 16:16 + NC + 3]
            with dve.Fori(0, 4) as pr:
                dve.tensor_copy(mask2.rearrange("p (n k) -> p n k", k=2),
                                halves[:, bass.ds(pr * NBLK, NBLK)].rearrange("p (n o) -> p n o", o=1).to_broadcast([P, NBLK, 2]))
                dve.drain()
                chunk = kt_evac(dve, 1, pr)
                chunk(0)
                for c in range(NC + 1):
                    if c < NC:
                        chunk(c + 1)
                    dve.wait_ge(SEM["sd_ps"], pr * (NC + 1) + (c + 1))
                    s = bank(c % 2)
                    if c < NC:
                        v = s.rearrange("p (j k) -> p j k", j=4)
                        e = v[:, :, P - NEAR:]
                        dve.tensor_tensor(e, e, near[:, 4 * c:4 * c + 4, :], ALU.add)
                        dve.drain()
                        m = mask2.rearrange("p (o k) -> p o k", o=1).to_broadcast([P, 4, P])
                        dve.tensor_tensor_reduce(sd[:, c * 512:(c + 1) * 512].rearrange("p (j k) -> p j k", j=4), v, m, 1.0, NEG,
                                                 ALU.add, ALU.max, peaks[:, c:c + 1]).then_inc(SEM["sd_used"], 1)
                    else:
                        two = sd[:, PAST:PAST + 2 * DS].rearrange("p (k t) -> p k t", k=2)
                        dve.tensor_tensor(two, bank(7)[:, 0:2 * DS].rearrange("p (k t) -> p k t", k=2),
                                          new.rearrange("p (o t) -> p o t", o=1).to_broadcast([P, 2, DS]), ALU.add)
                        dve.tensor_tensor_reduce(sd[:, PAST + 2 * DS:], s, win, 1.0, NEG, ALU.add, ALU.max, peaks[:, NC + 2:NC + 3])
                        dve.drain()
                        dve.tensor_reduce(peaks[:, NC:NC + 2], two, X, ALU.max)
                dve.drain()
                dve.tensor_reduce(sm[:, 40:41], peaks[:, 0:NC + 1], X, ALU.max, negate=True)
                dve.tensor_reduce(sm[:, 41:42], peaks[:, NC + 1:], X, ALU.max, negate=True)
                dve.drain().then_inc(SEM["mx_d"], 1)
                dve.wait_ge(SEM["ex_d"], pr + 1)
                dve.reciprocal(sm[:, 42:44], sm[:, 42:44])
                dve.drain()
                dve.tensor_tensor(sm[:, 44:46], sm[:, 42:44], gd[:, bass.ds(pr, 1), 1:3].rearrange("p o b -> p (o b)"), ALU.mult)
                dve.drain()
                dve.tensor_scalar(sd[:, 0:PAST + DS], sd[:, 0:PAST + DS], sm[:, 44:45], None, ALU.mult)
                dve.tensor_scalar(sd[:, PAST + DS:], sd[:, PAST + DS:], sm[:, 45:46], None, ALU.mult)
                dve.drain().then_inc(SEM["p_d"], 1)
                pt_evac(dve, 1, pr)
                dve.wait_ge(SEM["o_d"], pr + 1)
                dve.tensor_copy(osb, bank(6)[:, 0:P]).then_inc(SEM["o_sb"], 1)
                dve.wait_ge(SEM["ot_ps"], pr + 1)
                for g in range(G):
                    rows = slice(g * HD, (g + 1) * HD)
                    o = bank(6)[rows, P:2 * P].rearrange("p (b g t r) -> p g r b t", b=2, g=G, r=R)[:, g]
                    z = proj[rows, ZA:ZA + R, bass.ds(pr * 2 * DS + T, 2 * DS)].rearrange("p r (b t) -> p r b t", b=2)
                    dve.tensor_tensor(z, o, z, ALU.mult)
                dve.drain().then_inc(SEM["dpair"], 1)

        def pe_decode(pe):
            pe.wait_ge(SEM["oz"], 2 + NT * R)
            with pe.Fori(0, 4) as pr:
                pe.wait_ge(SEM["cur_ready"], pr + 1)

                def turn(c):
                    for b2 in range(2):
                        if c == 0:
                            pe.wait_ge(kd_ld[b2], pr * 16 + 16)
                        if c == NC:
                            pe.wait_ge(kw_ld[b2], pr * 16 + 16)
                        if c >= 1:
                            pe.wait_ge(kt_sb[b2], pr * (NC + 1) + c)
                        src = kd[:, b2, c * 512:(c + 1) * 512] if c < NC else kw_d[:, b2, :]
                        for j in range(4):
                            last = pe.transpose(bank(2 + b2)[:, j * P:(j + 1) * P], src[:, j * P:(j + 1) * P], ident)
                        last.then_inc(kt_ps[b2], 1)

                def scores(c):
                    if 2 <= c:
                        pe.wait_ge(SEM["sd_used"], pr * NC + (c - 1))
                    for b2 in range(2):
                        pe.wait_ge(kt_sb[b2], pr * (NC + 1) + (c + 1))
                        last = pe.matmul(bank(c % 2)[Q * b2:Q * (b2 + 1), :], qcur[:, Q * b2:Q * (b2 + 1)], ktc[:, b2, :], start=True, stop=True)
                    last.then_inc(SEM["sd_ps"], 1)
                turn(0)
                for c in range(NC + 1):
                    if c == NC:
                        for b2 in range(2):
                            pe.matmul(bank(7)[Q * b2:Q * (b2 + 1), 0:2 * DS], qcur[:, Q * b2:Q * (b2 + 1)], kncur[:, b2].rearrange("p k t -> p (k t)"), start=True, stop=True)
                    if c < NC:
                        turn(c + 1)
                    scores(c)
                    if c == NC - 1:
                        pe.drain().then_inc(SEM["kused"], 1)
                pe.drain().then_inc(SEM["wkused"], 1)
                pe.wait_ge(SEM["p_d"], pr + 1)

                def turn_p(c):
                    if c >= 2:
                        pe.wait_ge(dp_sb[c % 2], pr * ((NC + 2) // 2) + c // 2)
                    if c <= NC:
                        a = c * 512 if c < NC else PAST + 2 * DS
                        for j in range(4):
                            last = pe.transpose(bank(4 + c % 2)[:, j * P:(j + 1) * P], sd[:, a + j * P:a + (j + 1) * P], ident)
                    else:
                        last = pe.transpose(bank(4 + c % 2)[0:2 * DS, 0:P], sd[:, PAST:PAST + 2 * DS], ident)
                    last.then_inc(SEM["dp_ps"], 1)

                def values(c):
                    pe.wait_ge(dp_sb[c % 2], pr * ((NC + 2) // 2) + (c // 2 + 1))
                    if c in (0, NC):
                        for b2 in range(2):
                            pe.wait_ge((vd_ld if c == 0 else vw_ld)[b2], pr * 16 + 16)
                    for j in range(4 if c <= NC else 1):
                        for b2 in range(2):
                            o = bank(6)[Q * b2:Q * (b2 + 1), 0:P]
                            if c <= NC:
                                v = (vd[:, b2, c * 512:(c + 1) * 512] if c < NC else vw_d[:, b2, :])[:, j * P:(j + 1) * P]
                                last = pe.matmul(o, ptd2[:, c % 2, j * P + Q * b2:j * P + Q * (b2 + 1)], v, start=False, stop=False)
                            else:
                                last = pe.matmul(o, ptd2[0:2 * DS, c % 2, Q * b2:Q * (b2 + 1)], vncur[0:2 * DS, b2 * P:(b2 + 1) * P], start=False, stop=True)
                    last.then_inc(dv[c % 2], 1)
                for b2 in range(2):
                    pe.matmul(bank(6)[Q * b2:Q * (b2 + 1), 0:P], pcur[:, Q * b2:Q * (b2 + 1)],
                              vccur[:, b2 * P:(b2 + 1) * P], start=True, stop=False)
                turn_p(0)
                for c in range(NC + 2):
                    if c <= NC:
                        turn_p(c + 1)
                    values(c)
                    if c == NC - 1:
                        pe.drain().then_inc(SEM["vused"], 1)
                pe.drain().then_inc(SEM["wvused"], 1)
                pe.drain().then_inc(SEM["o_d"], 1)
                pe.wait_ge(SEM["o_sb"], pr + 1)
                pe.transpose(bank(6)[:, P:2 * P], osb, ident).then_inc(SEM["ot_ps"], 1)

        vcn_flat = vcn[:, :, :].rearrange("p b c -> p (b c)")

        MIX = [ZA, ZA + 1, ZA + 2, ZA + 3, ZB, ZB + 1, ZC, ZC + 1]
        wo = carve(0, KD * D).rearrange("p (k n) -> p k n", k=KD)
        gpost = late[:, 0:D]
        xo = carve(X0, 3 * D).rearrange("p (b n) -> p b n", b=3)
        junk = carve(X0 + 3 * D, D)

        def rows_of(n):
            return P if n < NT else S

        def x_rows(n):
            return dram["x_prompt"][n * P:(n + 1) * P, :] if n < NT else dram["x_sample"]

        def y_rows(n):
            return outs[0][0, n * P:(n + 1) * P, :] if n < NT else outs[1].rearrange("b t d -> (b t) d")

        def sp_output(sp):
            sp.wait_ge(SEM["oz"], 2 + NT * R)
            sp.dma_start(gpost, dram["g_post"].to_broadcast([P, D])).then_inc(SEM["ld_gp"], 16)
            sp.wait_ge(SEM["kused"], 4)
            sp.dma_start(wo, dram["w_out"]).then_inc(SEM["ld_wo"], 16)
            sp.wait_ge(SEM["vused"], 4)
            for n in range(3):
                sp.dma_start(xo[0:rows_of(n), n, :], x_rows(n)).then_inc(xo_ld[n], 16)
            for n in range(9):
                b = n % 3
                sp.wait_ge(SEM["y_out"], n + 1)
                sp.dma_start(y_rows(n), xo[0:rows_of(n), b, :]).then_inc(y_st[b], 16)
                if n + 3 < 9:
                    sp.wait_ge(y_st[b], 16 * (n // 3 + 1))
                    sp.dma_start(xo[0:rows_of(n + 3), b, :], x_rows(n + 3)).then_inc(xo_ld[b], 16)
            for b in range(3):
                sp.wait_ge(y_st[b], 48)

        def pe_output(pe):
            pe.wait_ge(SEM["ld_wo"], 16)
            pe.wait_ge(SEM["dpair"], 5)
            for n in range(9):
                w = rows_of(n)
                if n >= 2:
                    pe.wait_ge(SEM["y_free"], n - 1)
                for h in range(2):
                    for k in range(KD):
                        last = pe.matmul(bank(2 * (n % 2) + h)[0:w, :], proj[:, MIX[k], n * P:n * P + w], wo[:, k, h * 512:(h + 1) * 512],
                                         start=(k == 0), stop=(k == KD - 1))
                last.then_inc(SEM["y_ps"], 1)

        def act_output(act):
            act.wait_ge(SEM["vused"], 4)
            for n in range(10):
                if n < 9:
                    w = rows_of(n)
                    act.wait_ge(SEM["y_ps"], n + 1)
                    act.drain()
                    act.activation(junk[0:w, :], bank(2 * (n % 2), 2)[0:w, :], ACT.Square, accum_out=ssq[0:w, n:n + 1]).then_inc(SEM["y_sq"], 1)
                if n >= 0 and n < 9:
                    act.wait_ge(SEM["y_ms"], n + 1)
                    act.activation(rstd[0:w, n:n + 1], rstd[0:w, n:n + 1], ACT.Sqrt).then_inc(SEM["y_rt"], 1)

        def dve_output(dve):
            dve.wait_ge(SEM["ld_gp"], 16)
            for n in range(9):
                w, b = rows_of(n), n % 3
                dve.wait_ge(SEM["y_sq"], n + 1)
                dve.tensor_scalar(rstd[0:w, n:n + 1], ssq[0:w, n:n + 1], 1.0 / D, EPS, ALU.mult, ALU.add).then_inc(SEM["y_ms"], 1)
                dve.wait_ge(SEM["y_rt"], n + 1)
                dve.reciprocal(rstd[0:w, n:n + 1], rstd[0:w, n:n + 1])
                dve.wait_ge(xo_ld[b], 16 * (n // 3 + 1))
                dve.drain()
                y = yb[0:w, n % 2, :]
                dve.scalar_tensor_tensor(y, bank(2 * (n % 2), 2)[0:w, :], rstd[0:w, n:n + 1], gpost[0:w, :], ALU.mult, ALU.mult).then_inc(SEM["y_free"], 1)
                dve.wait_ge(SEM["y_free"], n + 1)
                dve.tensor_tensor(xo[0:w, b, :], xo[0:w, b, :], y, ALU.add).then_inc(SEM["y_out"], 1)

        yb = carve(X0 + 4 * D, 2 * D).rearrange("p (b n) -> p b n", b=2)
        N_SO = 5 + NB
        N_NAT = 12

        @block.sync
        def _(sp):
            sp_startup(sp)
            sp_project(sp)
            sp_states(sp)
            sp_selectors(sp)
            sp_natural(sp)
            sp_decode(sp)
            sp_output(sp)
            sp.wait_ge(out_done, 16 * 3)
            sp.wait_ge(so_out, 16 * N_SO)
            sp.wait_ge(SEM["nat_out"], 16 * N_NAT)

        @block.gpsimd
        def _(pool):
            pool_startup(pool)
            pool_compress(pool)
            pool_decode(pool)

        @block.scalar
        def _(act):
            act_startup(act)
            act_softplus(act)
            act_project(act, 0, 5)
            act_bc_inputs(act)
            act_project(act, 5, 8)
            act_states(act)
            act_project(act, 8, 10)
            act.wait_ge(k_compressed, 2)
            act_gates(act)
            act_decay(act)
            act_squares(act)
            act_project(act, 10, 12)
            act_var(act)
            act_swish(act)
            act_last_states(act)
            act_branch_gates(act)
            act_natural(act)
            act_prompt_exp(act)
            act_prompt_turn(act)
            act_decode_keys(act)
            act_decode_exp(act)
            act_decode_turn(act)
            act_masks(act)
            act_pairs(act)
            act_decode(act)
            act_output(act)

        @block.vector
        def _(dve):
            dve_startup(dve)
            dve_softplus(dve)
            dve_compress(dve, 0)
            dve_compress(dve, 1)
            dve_u(dve)
            dve_conv_b(dve)
            dve_conv_c(dve)
            dve_scan(dve)
            dve_mean(dve)
            dve_var(dve)
            dve_pointwise(dve)
            dve.drain().then_inc(SEM["bc_done"], 1)
            dve_prompt_blocks(dve)
            dve_prompt_cmp(dve)
            dve_decode_queries(dve)
            dve_decode_cmp(dve)
            dve_select(dve)
            dve_pairs_prepare(dve)
            dve_pairs(dve)
            dve_decode(dve)
            dve_output(dve)

        @block.tensor
        def _(pe):
            pe_startup(pe)
            pe_project(pe, 0, 5)
            pe_project(pe, 5, 8)
            pe_states(pe)
            pe_project(pe, 8, 10)
            pe_gates(pe)
            pe_mean(pe)
            pe_project(pe, 10, 12)
            pe_var(pe)
            pe_pointwise(pe)
            pe_last_states(pe)
            pe_branch_gates(pe)
            pe_natural(pe)
            pe_prompt_blocks(pe)
            pe_decode_keys(pe)
            pe_prompt_turn(pe)
            pe_decode_cmp(pe)
            pe_importance(pe)
            pe_masks(pe)
            pe_pairs(pe)
            pe_decode(pe)
            pe_output(pe)


def lay_out(i):
    w_in, w_out = i["w_in"][0], i["w_out"][0]
    kv = 6 * G * HD
    q0, kv0 = 0, H * HD
    gate0 = kv0 + kv
    za0 = gate0 + 3 * H
    glu0 = za0 + H * HD
    zb0 = glu0 + 512
    xc0 = zb0 + 256
    zc0 = xc0 + 256

    def pair(a, r):
        return np.r_[a + r * HD:a + (r + 1) * HD, a + (r + R) * HD:a + (r + R + 1) * HD]

    def run(a, n):
        return [np.arange(a + P * c, a + P * (c + 1)) for c in range(n)]
    tiles = run(glu0, 4) + run(xc0, 2) + run(zb0, 2) + run(zc0, 2) + [pair(q0, r) for r in range(R)] \
        + run(kv0, 6) + [pair(za0, r) for r in range(R)]

    def k_major(w):
        return w.reshape(KD, P, -1).transpose(1, 0, 2)
    w_tiles = np.stack([k_major(w_in[:, c]).reshape(P, KD * P) for c in tiles])
    rows = np.concatenate([pair(0, r) for r in range(R)] + [np.arange(512, 1024)])

    def per_channel(v):
        v = v.reshape(-1, 2, P)
        return v.transpose(2, 1, 0).reshape(P, -1)

    def blocks(w):
        o = np.zeros((P, 2, P), np.float32)
        for c in range(2):
            for h in range(2):
                o[h * HD:(h + 1) * HD, c, h * HD:(h + 1) * HD] = w[2 * c + h]
        return o.reshape(P, -1)
    par = dict(g_pre=i["g_pre"][0].reshape(KD, P).T, conv_b_b=per_channel(i["conv_b_b"][0]),
               gn_gain=per_channel(i["gn_gain"][0]), gn_bias=per_channel(i["gn_bias"][0]),
               conv_c_b=per_channel(i["conv_c_b"][0]), b_a=per_channel(i["b_lru_a"][0]),
               b_x=per_channel(i["b_lru_x"][0]), lam=per_channel(i["lru_lambda"][0]),
               conv_b_w=per_channel(i["conv_b_w"][0]), conv_c_w=per_channel(i["conv_c_w"][0]),
               wk=np.tile(i["w_cmp_k"][0].T, (2, 1)), wv=np.tile(i["w_cmp_v"][0].T, (2, 1)))
    pool = lambda a, n: a[0].reshape(-1, n * G * HD)
    return {
        "constants": constant_pack(),
        "parameters": np.concatenate([par[n] for n in PAR_COLS], 1),
        "one_hot": one_hot_tables(),
        "selectors": decode_selectors(),
        "x_prompt": i["x_prompt"][0], "x_sample": i["x_sample"].reshape(S, D),
        "w_tiles": w_tiles,
        "w_gate": k_major(w_in[:, gate0:za0]),
        "w_small": np.concatenate([i["w_pw_b"][0].reshape(2, P, 256).transpose(1, 0, 2).reshape(P, -1),
                                   blocks(i["w_lru_a"][0]), blocks(i["w_lru_x"][0])], 1),
        "w_out": k_major(w_out[rows]),
        "g_post": i["g_post"],
        "rel_bias": i["rel_bias"],
        "pages": np.repeat(i["page_table"].T, PAGE // L_CMP, 0),
        "w_cmp_k": i["w_cmp_k"].reshape(1, -1), "w_cmp_v": i["w_cmp_v"].reshape(1, -1),
        "state_conv_b": i["state_conv_b"][0], "state_conv_c": i["state_conv_c"].reshape(NB * 3, 256),
        "state_rglru": i["state_rglru"][0],
        "cmp_k": pool(i["cache_cmp_k"], 16), "cmp_v": pool(i["cache_cmp_v"], 16),
        "sel_k": pool(i["cache_sel_k"], 32), "sel_v": pool(i["cache_sel_v"], 32),
        "win_k": i["cache_win_k"][0].reshape(NB, WIN, G * HD), "win_v": i["cache_win_v"][0].reshape(NB, WIN, G * HD),
    }


_KV_P, _KV_S = (1, 1, T, G, HD), (1, NB, DS, G, HD)
_WIN_P, _WIN_S = (1, 1, WIN, G, HD), (1, NB, WIN, G, HD)
_OUTS = [(1, T, D), (NB, DS, D)] + [_KV_P, _KV_S] * 4 + [_WIN_P, _WIN_S] * 2 \
    + [(1, 1, CB_W - 1, 256), (1, NB, CB_W - 1, 256), (1, 1, CC_W - 1, 256), (1, NB, CC_W - 1, 256), (1, 1, 256), (1, NB, 256)]


def kernel(**inputs):
    import concourse.bacc as _bacc
    from concourse.bass_utils import run_bass_kernel_spmd as _run

    nc = _bacc.Bacc("TRN2", target_bir_lowering=False, num_devices=1)
    arrays, dram = {}, {}
    for name, a in lay_out({k: np.asarray(v) for k, v in inputs.items()}).items():
        a = np.ascontiguousarray(a)
        arrays[f"in_{name}_dram"] = a
        dram[name] = nc.dram_tensor(f"in_{name}_dram", a.shape, mybir.dt.from_np(a.dtype), kind="ExternalInput").ap()
    outs = [nc.dram_tensor(f"out_{n}_dram", shape, F32, kind="ExternalOutput").ap() for n, shape in enumerate(_OUTS)]
    strip = nc.dram_tensor("bias_strip", (H, P, SKEW), F32, kind="Internal").ap()
    skewed = bass.AP(strip.tensor, P - 1, [[SKEW - 1, P], [P * SKEW, H], [1, 2 * P]])
    program(nc, dram, outs, {"strip": strip, "skewed": skewed})
    r = _run(nc, [arrays], core_ids=[0])
    return tuple(r.results[0][f"out_{n}_dram"] for n in range(len(_OUTS)))
```

```python
from contextlib import ExitStack

import numpy as np

import concourse.bass as bass
from concourse import mybir

F32 = mybir.dt.float32
I32 = mybir.dt.int32
ALU = mybir.AluOpType
ACT = mybir.ActivationFunctionType
X = mybir.AxisListType.X

P = 128
D = 1024
T = 1024
NB = 8
DS = 8
S = NB * DS
TOK = T + S
NT = T // P
KD = D // P
HD = 64
G = 2
R = 4
H = G * R
PAST = 4096
PAGE = 128
NPAGE = PAST // PAGE
WIN = 512
L_CMP = 32
SEL = 64
NBLK = PAST // SEL
NCB = PAST // L_CMP
TOP_K = 16
BUCKETS = 32
MAX_DIST = 128
CB_W = 31
CC_W = 4
EPS = 1e-6
NEG = -1e30
FORCE = 1e4
Q = S
CHUNKS = [(0, 384), (384, 352), (736, 352)]

def columns(widths):
    at, out = 0, {}
    for name, n in widths.items():
        out[name] = (at, n)
        at += n
    return out, at


GLU_V, GLU_G, XC, ZB, ZC, QT, KC, VC, KS, VS, KW, VW, ZA = 0, 2, 4, 6, 8, 10, 14, 15, 16, 17, 18, 19, 20
NPROJ = 24

PAR_COLS = dict(g_pre=KD, conv_b_b=2, gn_gain=2, gn_bias=2, conv_c_b=2, b_a=2, b_x=2, lam=2,
                conv_b_w=2 * CB_W, conv_c_w=2 * CC_W, wk=L_CMP, wv=L_CMP)
CST_COLS = dict(ident=P, groupmean=P, winmask=P, page4=1, head=H)


PAR_AT, NPAR = columns(PAR_COLS)
CST_AT, NCST = columns(CST_COLS)

NEAR = 4
BIAS_COLS = dict(cmp=NCB, near=L_CMP * NEAR, new=DS, win=WIN)
OH_DEC = 8 * P
SKEW = 3 * P


BIAS_AT, NBIAS = columns(BIAS_COLS)
NOH = OH_DEC + DS * NBIAS + SKEW


def bucket(dist):
    n = np.maximum(np.asarray(dist), 0)
    half = BUCKETS // 2
    nf = np.maximum(n, 1).astype(np.float32)
    large = half + (np.log(nf / np.float32(half)) / np.float32(np.log(MAX_DIST / half)) * (BUCKETS - half)).astype(np.int32)
    return np.where(n < half, n, np.minimum(large, BUCKETS - 1))


def one_hot_tables():
    p = np.arange(P)
    dist, masked = [], []
    for n in range(8):
        d = p - L_CMP * (n - 4) - (L_CMP - 1)
        dist.append(d), masked.append(d < 0)
    for t in range(DS):
        d = PAST + t - (L_CMP * (p + 1) - 1)
        dist.append(d), masked.append(d < 0)
        j, e = np.arange(L_CMP)[:, None], np.arange(NEAR)[None, :]
        d = (PAST + t - (L_CMP * (P - NEAR + e) + j)).ravel()
        dist.append(d), masked.append(d < 0)
        d = t - np.arange(DS)
        dist.append(d), masked.append(d < 0)
        d = (WIN + t - (WIN // P * p[None, :] + np.arange(WIN // P)[:, None])).ravel()
        dist.append(d), masked.append((d < 0) | (d >= WIN))
    strip = 2 * P - 1 - np.arange(SKEW)
    dist.append(strip), masked.append(strip < 0)
    dist, masked = np.concatenate(dist), np.concatenate(masked)
    oh = np.zeros((BUCKETS + 1, dist.size), np.float32)
    oh[bucket(dist), np.arange(dist.size)] = 1.0
    oh[:BUCKETS, masked] = 0.0
    oh[BUCKETS, masked] = 1.0
    return oh


def constant_pack():
    c = np.zeros((P, NCST), np.float32)
    p = np.arange(P)[:, None]

    def put(name, v):
        a, n = CST_AT[name]
        c[:, a:a + n] = v
    q = np.arange(P)[None, :]
    put("ident", p == q)
    put("groupmean", (p // HD == q // HD) / HD)
    put("winmask", np.where(q > p, 0.0, NEG))
    row = p % Q
    put("head", np.arange(H)[None, :] == row // 32 * R + row % R)
    put("page4", p % (PAGE // L_CMP))
    return c


def decode_selectors():
    row = np.arange(P)
    b2, g, t, r = row // Q, row // 32 % G, row // R % DS, row % R
    o = np.zeros((P, 4, 3, P), np.float32)
    for pr in range(4):
        bgt = ((2 * pr + b2) * G + g) * DS + t
        o[bgt, pr, 0, row] = 1.0
        o[row, pr, 1, bgt] = 1.0
        o[(2 * pr + b2) * DS + t, pr, 2, row] = 1.0
    return o.reshape(P, -1)


def program(nc, dram, outs, scratch):
    with ExitStack() as ctx:
        def sb(name, shape, dt=F32):
            return ctx.enter_context(nc.sbuf_tensor(name, shape, dt))

        def sem(name):
            return ctx.enter_context(nc.semaphore(name))

        sizes = dict(stage=2 * 2048, wcmp=2048, ring=2 * D, xT=KD * TOK, proj=NPROJ * TOK)
        at, total = {}, 0
        for name, n in sizes.items():
            at[name] = total
            total += n
        MAIN = sb("main", [P, total])

        def main(name, n=None, off=0):
            a = at[name] + off
            return MAIN[:, a:a + (sizes[name] - off if n is None else n)]

        FREE = at["proj"] + 6 * TOK
        stage = main("stage").rearrange("p (h n) -> p h n", h=2)
        wcmp = main("wcmp")
        ring = main("ring").rearrange("p (s n) -> p s n", s=2)
        xT = main("xT").rearrange("p (k t) -> p k t", k=KD)
        proj_flat = main("proj")
        proj = proj_flat.rearrange("p (c t) -> p c t", c=NPROJ)

        xn = main("proj", 9 * D).rearrange("p (n d) -> p n d", n=9)
        oh = main("proj", NOH, 9 * D)[0:BUCKETS + 1, :]
        states = main("proj", 4 * 256, 9 * D + NOH)
        tok_tab = main("proj", DS * P, 10 * D + NOH)[0:BUCKETS + 1, :].rearrange("p (t q) -> p t q", t=DS)

        cst = sb("cst", [P, NCST])
        par = sb("par", [P, NPAR])

        def c_(name):
            a, n = CST_AT[name]
            return cst[:, a:a + n]

        def p_(name, i=0, n=1):
            a = PAR_AT[name][0] + i
            return par[:, a:a + n]

        ident = c_("ident")
        pages = sb("pages", [P, NB], I32)
        row16 = sb("row16", [P, NB], I32)
        row8 = sb("row8", [P, NB, 2], I32)
        tab = sb("tab", [P, H])
        rel = sb("rel", [P, 2 * H])
        diag = sb("diag", [P, H, 2 * P])
        cbias = sb("cbias", [P, H, 60])
        dec_bias = sb("dec_bias", [P, NBIAS])
        kcn = sb("kcn", [P, NB, P])
        vcn = sb("vcn", [P, NB, P])
        half = sb("half", [P, 2, P])
        ext_b = sb("ext_b", [P, 2, NB, CB_W - 1 + DS])
        ext_c = sb("ext_c", [P, 2, NB, CC_W - 1 + DS])
        h0 = sb("h0", [P, 2, NB])
        w_gate = sb("w_gate", [P, KD, 3 * H])
        gate_n = sb("gate_n", [P, NT, 3 * H])
        gate_t = sb("gate_t", [S, 3 * H])
        late = sb("late", [P, 1536])
        scr = late[:, 0:TOK]
        ssq = sb("ssq", [P, 9])
        rstd = sb("rstd", [P, 9])
        spl = sb("spl", [P, 2 * 8])
        cwb = sb("cwb", [P, 2 * 256 + 4 * P])
        w_pw = cwb[:, 0:512].rearrange("p (k n) -> p k n", k=2)
        w_a = cwb[:, 512:768].rearrange("p (c n) -> p c n", c=2)
        w_x = cwb[:, 768:1024].rearrange("p (c n) -> p c n", c=2)

        PS = ctx.enter_context(nc.psum_tensor("PS", [P, 8 * 512], F32))

        def bank(b, n=1):
            return PS[:, 512 * b:512 * (b + n)]

        ld_cst, ld_par, ld_oh, ld_rel, ld_st, ld_pg, ld_wc, ld_wbc, ld_wcmp, ld_wcmp_v = [
            sem(n) for n in ("ld_cst", "ld_par", "ld_oh", "ld_rel", "ld_st", "ld_pg", "ld_wc", "ld_wbc", "ld_wcmp", "ld_wcmp_v")]
        ld_x = [sem(f"ld_x{n}") for n in range(9)]
        w_ld = [sem(f"w_ld{s}") for s in range(2)]
        sq_done, x_scaled, x_turned, xt_done, tab_done, oh_used = [
            sem(n) for n in ("sq_done", "x_scaled", "x_turned", "xt_done", "tab_done", "oh_used")]
        startup_evac, strip_out, strip_in = sem("startup_evac"), sem("strip_out"), sem("strip_in")
        rows_ready, stage_ld, stage_free = sem("rows_ready"), [sem("stage_ld0"), sem("stage_ld1")], [sem("stage_free0"), sem("stage_free1")]
        k_compressed = sem("k_compressed")
        proj_ps = [sem(f"proj_ps{s}") for s in range(2)]
        proj_sb = [sem(f"proj_sb{s}") for s in range(2)]
        mail = [sem("mail0"), sem("mail1")]
        taken = [sem("taken0"), sem("taken1")]
        glu_sig, u_done, uc_done, conv_done, sq_ready, norm_done = [
            sem(n) for n in ("glu_sig", "u_done", "uc_done", "conv_done", "sq_ready", "norm_done")]
        bz_silu, gates_done, h_done, scan_in, silu_n = [
            sem(n) for n in ("bz_silu", "gates_done", "h_done", "scan_in", "silu_n")]
        a_done, th_done, th_sqrt, mean_sq, rms = [sem(n) for n in ("a_done", "th_done", "th_sqrt", "mean_sq", "rms")]
        var_rt = sem("var_rt")
        st_sb, so_out, out_done = sem("st_sb"), sem("so_out"), sem("out_done")
        scan_done = sem("scan_done")
        gate_done, gates_sb = sem("gate_done"), sem("gates_sb")
        SEM = {}

        def mail_bank(m):
            return bank(6 + m % 2)

        def post(pe, m, last):
            last.then_inc(mail[m % 2], 1)

        def bank_free(eng, m):
            if m >= 2:
                eng.wait_ge(taken[m % 2], m // 2)

        def posted(eng, m):
            eng.wait_ge(mail[m % 2], m // 2 + 1)

        counts = dict(ST=2, G=3, GT=1, GATE=12, MEAN=6, VAR=6, H=1, PW=6, KT=2, VC=1, PC=4, TG=1, DC=1, IMP=1, DPT=1, MASK=1, VN=2)
        first, total_mail = columns(counts)
        M_ST, M_G, M_GT, M_GATE, M_MEAN, M_VAR, M_H, M_PW, M_KT, M_VC, M_PC, M_TG, M_DC, M_IMP, M_DPT, M_MASK, M_VN = [first[n][0] for n in counts]
        CC = [(c, t0, n) for c in range(2) for t0, n in CHUNKS]

        block = ctx.enter_context(nc.Block())

        def sp_startup(sp):
            sp.dma_start(cst[:, :], dram["constants"]).then_inc(ld_cst, 16)
            for n in range(NT):
                sp.dma_start(xn[:, n, :], dram["x_prompt"][n * P:(n + 1) * P, :]).then_inc(ld_x[n], 16)
            sp.dma_start(xn[0:S, 8, :], dram["x_sample"]).then_inc(ld_x[8], 16)
            for s in range(2):
                sp.dma_start(ring[:, s, :], dram["w_tiles"][s]).then_inc(w_ld[s], 16)
            sp.wait_ge(startup_evac, 5)
            sp.dma_start(scratch["strip"], strip[0:H, :].rearrange("h (o c) -> h o c", o=1).to_broadcast([H, P, SKEW])).then_inc(strip_out, 16)
            sp.wait_ge(strip_out, 16)
            sp.dma_start(diag[:, :, :], scratch["skewed"]).then_inc(strip_in, 16)

        def sp_project(sp, a, b):
            with sp.Fori(a, b) as i:
                for s in range(2):
                    sp.wait_ge(proj_ps[s], i)
                    sp.dma_start(ring[:, s, :], dram["w_tiles"][bass.ds(i * 2 + s, 1)].rearrange("a p n -> (a p) n")).then_inc(w_ld[s], 16)

        def sp_states(sp):
            sp.dma_start(outs[15][0, :, 0:CB_W - 1 - DS, :], dram["state_conv_b"][:, DS:, :]).then_inc(out_done, 16)
            sp.wait_ge(st_sb, 1)
            sp.dma_start(outs[14][0, 0], so[0:CB_W - 1, 0, :]).then_inc(so_out, 16)
            sp.dma_start(outs[15][0, :, CB_W - 1 - DS:, :], so[0:S, 1, :]).then_inc(so_out, 16)
            sp.wait_ge(st_sb, 2)
            sp.dma_start(outs[16][0, 0], so[0:3, 2, :]).then_inc(so_out, 16)
            for b in range(NB):
                sp.dma_start(outs[17][0, b], so[b * DS + DS - 3:(b + 1) * DS, 3, :]).then_inc(so_out, 16)
            sp.wait_ge(st_sb, 3)
            sp.dma_start(outs[18][0], so[0:1, 4, :]).then_inc(so_out, 16)
            sp.dma_start(outs[19][0], so[1:1 + NB, 4, :]).then_inc(so_out, 16)

        strip = late[:, 0:SKEW]
        gates_t = proj[:, 18, :]
        so = proj_flat[0:S, 22 * TOK:22 * TOK + 5 * 256].rearrange("p (a c) -> p a c", a=5)

        def pool_startup(pool):
            pool.memset(cbias[:, :, 0:24], 0.0)
            pool.memset(cbias[:, :, 32:60], NEG).then_inc(tab_done, 1)

        def pool_compress(pool):
            pool.wait_ge(rows_ready, 1)
            for n in range(2 * NB):
                src = dram["cmp_k"] if n < NB else dram["cmp_v"]
                if n == NB:
                    pool.wait_ge(k_compressed, 1)
                    pool.dma_start(wcmp, dram["w_cmp_v"].to_broadcast([P, L_CMP * HD])).then_inc(ld_wcmp_v, 16)
                for h in range(2):
                    if n >= 1:
                        pool.wait_ge(stage_free[h], n)
                    pool.indirect_dma_start(stage[:, h, :], None, src,
                                            bass.IndirectOffsetOnAxis(row8[:, n % NB, h:h + 1], 0)).then_inc(stage_ld[h], 16)

        def act_startup(act):
            act.dma_start(rel[0:BUCKETS, 0:H], dram["rel_bias"]).then_inc(ld_rel, 16)
            act.dma_start(rel[0:BUCKETS, H:2 * H], dram["rel_bias"][BUCKETS - 1:BUCKETS, :].to_broadcast([BUCKETS, H])).then_inc(ld_rel, 16)
            act.dma_start(pages[:, :], dram["pages"]).then_inc(ld_pg, 16)
            act.dma_start(par[:, :], dram["parameters"]).then_inc(ld_par, 16)
            act.dma_start(oh, dram["one_hot"]).then_inc(ld_oh, 16)
            act.dma_start(wcmp, dram["w_cmp_k"].to_broadcast([P, L_CMP * HD])).then_inc(ld_wcmp, 16)
            act.dma_start(states[0:120, 0:512].rearrange("p (a c) -> p a c", a=2), dram["state_conv_b"].rearrange("(a b) t c -> (b t) a c", a=2)).then_inc(ld_st, 16)
            act.dma_start(states[0:24, 512:768], dram["state_conv_c"]).then_inc(ld_st, 16)
            act.dma_start(states[0:NB, 768:1024], dram["state_rglru"]).then_inc(ld_st, 16)
            act.dma_start(w_gate[:, :, :], dram["w_gate"]).then_inc(ld_wc, 16)
            act.dma_start(cwb[:, :], dram["w_small"]).then_inc(ld_wbc, 16)
            def root(n):
                rows = P if n < NT else S
                act.wait_ge(mean_sq, n + 1)
                act.activation(rstd[0:rows, n:n + 1], rstd[0:rows, n:n + 1], ACT.Sqrt).then_inc(rms, 1)
            for n in range(9):
                rows = P if n < NT else S
                act.wait_ge(ld_x[n], 16)
                act.drain()
                act.activation(late[0:rows, 0:D], xn[0:rows, n, :], ACT.Square, accum_out=ssq[0:rows, n:n + 1]).then_inc(sq_done, 1)
                if n >= 1:
                    root(n - 1)
            root(8)
            act.wait_ge(oh_used, 1)
            act.wait_ge(tab_done, 2)
            act.activation(cbias[:, :, 24:32], bank(6)[:, 448:512].rearrange("p (x h) -> p h x", h=H), ACT.Copy).then_inc(startup_evac, 1)
            act.activation(dec_bias[:, 0:NBIAS - WIN], bank(4)[:, 0:NBIAS - WIN], ACT.Copy).then_inc(startup_evac, 1)
            act.activation(dec_bias[:, NBIAS - WIN:], bank(5), ACT.Copy).then_inc(startup_evac, 1)
            act.activation(h0[:, :, :], bank(6)[:, 432:448].rearrange("p (c b) -> p c b", c=2), ACT.Copy).then_inc(startup_evac, 1)
            act.wait_ge(sq_done, 9)
            act.activation(strip[0:H, :], bank(6)[0:H, 0:SKEW], ACT.Copy).then_inc(startup_evac, 1)
            act.activation(ext_c[:, :, :, 0:CC_W - 1], bank(6)[:, 384:432].rearrange("p (c b t) -> p c b t", c=2, b=NB), ACT.Copy).then_inc(startup_evac, 1)
            for c in range(2):
                last = act.activation(ext_b[:, c, :, 0:CB_W - 1],
                                      bank(7)[:, 240 * c:240 * (c + 1)].rearrange("p (b t) -> p b t", b=NB), ACT.Copy)
            last.then_inc(startup_evac, 1)
            for s in range(2):
                act.activation(spl[:, 14 + s:15 + s], c_("page4"), ACT.Copy).then_inc(proj_sb[s], 1)

        def act_project(act, a, b):
            with act.Fori(a, b) as i:
                for s in range(2):
                    act.wait_ge(proj_ps[s], i + 1)
                    n0, n1 = CHUNKS[0][1], CHUNKS[1][1]
                    act.activation(proj_flat[:, bass.ds(i * 2 * TOK + s * TOK, n0)], bank(3 * s)[:, 0:n0], ACT.Copy)
                    act.activation(proj_flat[:, bass.ds(i * 2 * TOK + (s * TOK + n0), 2 * n1)].rearrange("p (c n) -> p c n", c=2),
                                   bank(3 * s + 1, 2).rearrange("p (c n) -> p c n", c=2)[:, :, 0:n1], ACT.Copy)
                    act.drain().then_inc(proj_sb[s], 1)

        def act_bc_inputs(act, step):
            act.drain()
            if step == 0:
                for c in range(2):
                    act.activation(proj[:, GLU_G + c, :], proj[:, GLU_G + c, :], ACT.Sigmoid).then_inc(glu_sig, 1)
            if step == 1:
                for c in range(2):
                    act.activation(proj[:, ZB + c, :], proj[:, ZB + c, :], ACT.Silu)
            if step == 2:
                for c in range(2):
                    act.activation(proj[:, ZC + c, :], proj[:, ZC + c, :], ACT.Silu)
                act.drain().then_inc(bz_silu, 1)

        def act_states(act):
            posted(act, M_ST)
            act.activation(so[0:CB_W - 1, 0, :], mail_bank(M_ST)[0:CB_W - 1, 0:256], ACT.Copy)
            act.activation(so[0:S, 1, :], mail_bank(M_ST)[0:S, 256:512], ACT.Copy)
            act.drain()
            act.drain().then_inc(taken[0], 1)
            act.drain().then_inc(st_sb, 1)
            posted(act, M_ST + 1)
            act.activation(so[0:3, 2, :], mail_bank(M_ST + 1)[0:3, 0:256], ACT.Copy)
            act.activation(so[0:S, 3, :], mail_bank(M_ST + 1)[0:S, 256:512], ACT.Copy)
            act.drain()
            act.drain().then_inc(taken[1], 1)
            act.drain().then_inc(st_sb, 1)

        r_gate = lambda c: proj[:, XC + c, :]

        def act_softplus(act):
            act.wait_ge(ld_par, 16)
            act.activation(spl[:, 0:2], p_("lam", 0, 2), ACT.Abs)
            act.drain()
            act.activation(spl[:, 2:4], spl[:, 0:2], ACT.Exp, scale=-1.0).then_inc(a_done, 1)

        def act_softplus_log(act):
            act.wait_ge(th_done, 1)
            act.activation(spl[:, 6:8], spl[:, 4:6], ACT.Ln).then_inc(a_done, 1)

        def act_gates(act):
            for k, (c, t0, n) in enumerate(CC + CC):
                m = M_GATE + k
                posted(act, m)
                dst = (r_gate(c) if k < 6 else i_gate[c])[:, t0:t0 + n]
                bias = p_("b_a" if k < 6 else "b_x", c)
                act.activation(dst, mail_bank(m)[:, 0:n], ACT.Sigmoid, bias=bias).then_inc(taken[m % 2], 1)
            act.drain()
            act.drain().then_inc(gates_done, 1)

        def act_decay(act, step):
            for c in range(2):
                if step == 0:
                    act.wait_ge(scan_in, c + 1)
                    act.activation(i_gate[c], r_gate(c), ACT.Tanh, scale=spl[:, 10 + c:11 + c]).then_inc(a_done, 1)
                    act.drain()
                    act.activation(r_gate(c), r_gate(c), ACT.Exp, scale=spl[:, 12 + c:13 + c]).then_inc(a_done, 1)
                else:
                    act.wait_ge(th_done, c + 2)
                    act.activation(i_gate[c], i_gate[c], ACT.Sqrt).then_inc(th_sqrt, 1)

        def act_squares(act):
            for k, (c, t0, n) in enumerate(CC):
                act.wait_ge(norm_done, k + 1)
                act.activation(scr2[c][:, t0:t0 + n], conv[c][:, t0:t0 + n], ACT.Square).then_inc(sq_ready, 1)

        def act_var(act):
            for k, (c, t0, n) in enumerate(CC):
                act.wait_ge(var_rt, 6)
                act.activation(scr2[c][:, t0:t0 + n], scr2[c][:, t0:t0 + n], ACT.Sqrt).then_inc(var_rt, 1)

        def act_swish(act):
            for c in range(2):
                act.wait_ge(norm_done, 6 + 3 * (c + 1))
                act.activation(conv[c], conv[c], ACT.Silu, scale=p_("gn_gain", c), bias=p_("gn_bias", c)).then_inc(silu_n, 1)

        def act_last_states(act):
            posted(act, M_H)
            act.activation(so[0:1 + NB, 4, :], mail_bank(M_H)[0:1 + NB, 0:256], ACT.Copy).then_inc(taken[M_H % 2], 1)
            act.wait_ge(taken[M_H % 2], M_H // 2 + 1)
            act.drain().then_inc(st_sb, 1)

        def act_branch_gates(act):
            for j, (t0, n) in enumerate(CHUNKS):
                posted(act, M_G + j)
                act.activation(gates_t[0:3 * H, t0:t0 + n], mail_bank(M_G + j)[0:3 * H, 0:n], ACT.Sigmoid).then_inc(taken[(M_G + j) % 2], 1)
                act.wait_ge(taken[(M_G + j) % 2], (M_G + j) // 2 + 1)
                act.drain().then_inc(gates_sb, 1)

        def act_turn_gates(act):
            posted(act, M_GT)
            act.activation(gate_n[:, :, :], mail_bank(M_GT)[:, 0:NT * 3 * H].rearrange("p (n c) -> p n c", n=NT), ACT.Copy)
            act.activation(gate_t[:, :], mail_bank(M_GT)[0:S, NT * 3 * H:(NT + 1) * 3 * H], ACT.Copy)
            act.drain()
            act.drain().then_inc(taken[M_GT % 2], 1)
            act.drain().then_inc(gate_done, 1)

        conv = [proj[:, GLU_G + c, :] for c in range(2)]
        uu = [proj[:, GLU_V + c, :] for c in range(2)]
        uc = [proj[:, 16 + c, :] for c in range(2)]
        i_gate = [proj[:, 19 + c, :] for c in range(2)]
        scr2 = [proj[:, 21, :], scr]

        def dve_startup(dve):
            dve.wait_ge(ld_rel, 32)
            dve.memset(tab[BUCKETS:BUCKETS + 1, :], NEG)
            dve.tensor_tensor(tab[0:BUCKETS, :], rel[0:BUCKETS, 0:H], rel[0:BUCKETS, H:2 * H], ALU.subtract)
            dve.memset(tok_tab, 0.0)
            dve.drain()
            for t in range(DS):
                for b2 in range(2):
                    dve.tensor_copy(tok_tab[:, t, b2 * Q:(b2 + 1) * Q].rearrange("p (g t r) -> p g t r", g=G, r=R)[:, :, t, :],
                                    tab[0:BUCKETS + 1, :].rearrange("p (g r) -> p g r", g=G))
            dve.wait_ge(ld_cst, 16)
            dve.drain().then_inc(tab_done, 1)
            dve.wait_ge(ld_pg, 16)
            dve.tensor_scalar(row16[:, :], pages[:, :], 4.0, c_("page4"), ALU.mult, ALU.add)
            dve.drain()
            for h in range(2):
                last = dve.tensor_scalar(row8[:, :, h], row16[:, :], 2.0, float(h), ALU.mult, ALU.add)
            last.then_inc(rows_ready, 1)
            dve.wait_ge(ld_par, 16)

            def square(n):
                rows = P if n < NT else S
                dve.wait_ge(sq_done, n + 1)
                dve.tensor_scalar(rstd[0:rows, n:n + 1], ssq[0:rows, n:n + 1], 1.0 / D, EPS, ALU.mult, ALU.add).then_inc(mean_sq, 1)

            def scale(n):
                rows = P if n < NT else S
                dve.wait_ge(rms, n + 1)
                dve.reciprocal(rstd[0:rows, n:n + 1], rstd[0:rows, n:n + 1])
                dve.drain()
                dve.tensor_scalar(xn[0:rows, n, :], xn[0:rows, n, :], rstd[0:rows, n:n + 1], None, ALU.mult).then_inc(x_scaled, 1)

            def evac(n):
                w = P if n < NT else S
                for h in range(2):
                    m = 2 * n + h
                    dve.wait_ge(x_turned, m + 1)
                    src = bank(m % 4).rearrange("p (k t) -> p k t", k=4)[:, :, 0:w]
                    g = p_("g_pre", 4 * h, 4).rearrange("p (k o) -> p k o", o=1).to_broadcast([P, 4, w])
                    dve.tensor_tensor(xT[:, 4 * h:4 * h + 4, n * P:n * P + w], src, g, ALU.mult).then_inc(xt_done, 1)
            for n in range(11):
                if n < 9:
                    square(n)
                if 1 <= n < 10:
                    scale(n - 1)
                if n >= 2:
                    evac(n - 2)

        def dve_compress(dve, v, b0, b1):
            dst = vcn if v else kcn
            dve.wait_ge(ld_wcmp_v if v else ld_wcmp, 16)
            w = wcmp.rearrange("p (j d) -> p j d", j=L_CMP)
            with dve.Fori(b0, b1) as b:
                for h in range(2):
                    dve.wait_ge(stage_ld[h], 16 * b + 16 * (NB * v + 1))
                    for g in range(G):
                        rows = stage[:, h, :].rearrange("p (j g d) -> p j g d", j=16, g=G)[:, :, g, :]
                        dve.tensor_tensor(rows, rows, w[:, 16 * h:16 * h + 16, :], ALU.mult)
                    dve.drain()
                    dve.tensor_reduce(half[:, h, :], stage[:, h, :].rearrange("p (j c) -> p c j", j=16), X, ALU.add).then_inc(stage_free[h], 1)
                dve.drain()
                dve.tensor_tensor(dst[:, bass.ds(b, 1), :].rearrange("p o c -> p (o c)"), half[:, 0, :], half[:, 1, :], ALU.add)
                dve.drain()
            if b1 == NB:
                dve.drain().then_inc(k_compressed, 1)

        def dve_u(dve):
            dve.wait_ge(startup_evac, 7)
            for c in range(2):
                dve.wait_ge(glu_sig, c + 1)
                dve.tensor_tensor(uu[c], uu[c], proj[:, GLU_G + c, :], ALU.mult)
            dve.drain()
            for c in range(2):
                dve.tensor_copy(ext_b[:, c, :, CB_W - 1:], uu[c][:, T:].rearrange("p (b t) -> p b t", b=NB))
            dve.drain()
            dve.drain().then_inc(u_done, 1)

        def dve_xc(dve):
            for s in range(2):
                dve.wait_ge(proj_sb[s], 1 + 3)
            for c in range(2):
                dve.tensor_copy(ext_c[:, c, :, CC_W - 1:], proj[:, XC + c, T:].rearrange("p (b t) -> p b t", b=NB))
            dve.drain()

        def taps(dve, dst, src, ext, width, w, b):
            full = dst[:, 0:T]
            smp = dst[:, T:].rearrange("p (b t) -> p b t", b=NB)
            dve.tensor_scalar(full, src[:, 0:T], w(width - 1), b, ALU.mult, ALU.add)
            dve.tensor_scalar(smp, ext[:, :, width - 1:], w(width - 1), b, ALU.mult, ALU.add)
            for k in range(width - 1):
                lag = width - 1 - k
                dve.drain()
                dve.scalar_tensor_tensor(full[:, lag:], src[:, 0:T - lag], w(k), full[:, lag:], ALU.mult, ALU.add)
                dve.scalar_tensor_tensor(smp, ext[:, :, k:k + DS], w(k), smp, ALU.mult, ALU.add)

        def dve_conv_b(dve, c):
            taps(dve, conv[c], uu[c], ext_b[:, c], CB_W, lambda k: p_("conv_b_w", c * CB_W + k), p_("conv_b_b", c))
            dve.drain().then_inc(conv_done, 1)

        def dve_conv_c(dve):
            for c in range(2):
                taps(dve, uc[c], proj[:, XC + c, :], ext_c[:, c], CC_W, lambda k: p_("conv_c_w", c * CC_W + k), p_("conv_c_b", c))
            dve.drain()
            dve.drain().then_inc(uc_done, 1)

        def dve_softplus(dve):
            dve.wait_ge(a_done, 1)
            dve.tensor_scalar(spl[:, 4:6], spl[:, 2:4], 1.0, None, ALU.add).then_inc(th_done, 1)

        def dve_softplus_end(dve):
            dve.drain()
            dve.tensor_scalar(spl[:, 0:2], spl[:, 4:6], 1.0, None, ALU.subtract)
            dve.drain()
            dve.tensor_scalar(spl[:, 8:10], spl[:, 0:2], 0.0, None, ALU.is_equal)
            dve.drain()
            dve.tensor_tensor(spl[:, 0:2], spl[:, 0:2], spl[:, 8:10], ALU.add)
            dve.wait_ge(a_done, 2)
            dve.tensor_tensor(spl[:, 6:8], spl[:, 6:8], spl[:, 8:10], ALU.add)
            dve.drain()
            dve.reciprocal(spl[:, 0:2], spl[:, 0:2])
            dve.drain()
            dve.tensor_tensor(spl[:, 6:8], spl[:, 6:8], spl[:, 0:2], ALU.mult)
            dve.drain()
            dve.tensor_tensor(spl[:, 6:8], spl[:, 6:8], spl[:, 2:4], ALU.mult)
            dve.tensor_scalar(spl[:, 8:10], p_("lam", 0, 2), -1.0, 0.0, ALU.mult, ALU.max)
            dve.drain()
            dve.tensor_tensor(spl[:, 6:8], spl[:, 6:8], spl[:, 8:10], ALU.add)
            dve.drain()
            dve.tensor_scalar(spl[:, 10:12], spl[:, 6:8], 8.0, None, ALU.mult)
            dve.tensor_scalar(spl[:, 12:14], spl[:, 6:8], -8.0, None, ALU.mult)
            dve.drain()

        def dve_decay(dve):
            dve.wait_ge(gates_done, 1)
            for c in range(2):
                dve.tensor_tensor(uc[c], uc[c], i_gate[c], ALU.mult).then_inc(scan_in, 1)
            for c in range(2):
                a, th, iu = r_gate(c), i_gate[c], uc[c]
                dve.wait_ge(a_done, 2 + 2 * (c + 1))
                sq = scr
                dve.tensor_tensor(sq, a, a, ALU.mult)
                dve.drain()
                dve.scalar_tensor_tensor(th, sq, 1.0, th, ALU.add, ALU.mult)
                dve.drain().then_inc(th_done, 1)

        def dve_scan(dve):
            for c in range(2):
                a, th, iu = r_gate(c), i_gate[c], uc[c]
                dve.wait_ge(th_sqrt, c + 1)
                dve.tensor_tensor(iu, iu, th, ALU.mult)
                starts = lambda x: x[:, T:].rearrange("p (b t) -> p b t", b=NB)[:, :, 0]
                dve.tensor_tensor(h0[:, c, :], h0[:, c, :], starts(a), ALU.mult)
                dve.drain()
                dve.tensor_tensor(starts(iu), starts(iu), h0[:, c, :], ALU.add)
                dve.memset(starts(a), 0.0)
                dve.drain()
                dve.tensor_tensor_scan(th, a, iu, 0.0, ALU.mult, ALU.add).then_inc(h_done, 1)
                dve.drain()
                if c == 0:
                    dve.wait_ge(bz_silu, 1)
                dve.tensor_tensor(proj[:, ZC + c, :], proj[:, ZC + c, :], th, ALU.mult)
            dve.drain().then_inc(scan_done, 1)

        def dve_mean(dve):
            for k, (c, t0, n) in enumerate(CC):
                m = M_MEAN + k
                posted(dve, m)
                y = conv[c][:, t0:t0 + n]
                dve.tensor_tensor(y, y, mail_bank(m)[:, 0:n], ALU.subtract).then_inc(taken[m % 2], 1)
                dve.wait_ge(taken[m % 2], m // 2 + 1)
                dve.drain().then_inc(norm_done, 1)

        def dve_var(dve):
            for k, (c, t0, n) in enumerate(CC):
                m = M_VAR + k
                posted(dve, m)
                y, v = conv[c][:, t0:t0 + n], scr2[c][:, t0:t0 + n]
                dve.tensor_scalar(v, mail_bank(m)[:, 0:n], EPS, None, ALU.add).then_inc(taken[m % 2], 1)
                dve.wait_ge(taken[m % 2], m // 2 + 1)
                dve.drain().then_inc(var_rt, 1)
            for k, (c, t0, n) in enumerate(CC):
                y, v = conv[c][:, t0:t0 + n], scr2[c][:, t0:t0 + n]
                dve.wait_ge(var_rt, 7 + k)
                dve.reciprocal(v, v)
                dve.drain()
                dve.tensor_tensor(y, y, v, ALU.mult).then_inc(norm_done, 1)

        def dve_pointwise(dve):
            dve.wait_ge(bz_silu, 1)
            for k, (c, t0, n) in enumerate(CC):
                m = M_PW + k
                posted(dve, m)
                z = proj[:, ZB + c, t0:t0 + n]
                dve.tensor_tensor(z, z, mail_bank(m)[:, 0:n], ALU.mult).then_inc(taken[m % 2], 1)


        TABLES_AT = 5

        def pe_tables(pe):
            pe.wait_ge(ld_oh, 16)
            pe.wait_ge(tab_done, 2)
            K = BUCKETS + 1
            for n in range(8):
                pe.matmul(bank(6)[:, 448 + n * H:448 + (n + 1) * H], oh[:, n * P:(n + 1) * P], tab[0:K, :], start=True, stop=True)
            for first, n, b in ((0, NBIAS - WIN, 4), (NBIAS - WIN, WIN, 5)):
                for t in range(DS):
                    a = OH_DEC + t * NBIAS + first
                    pe.matmul(bank(b)[:, 0:n], tok_tab[:, t, :], oh[:, a:a + n], start=(t == 0), stop=(t == DS - 1))
            pe.matmul(bank(6)[0:H, 0:SKEW], tab[0:K, :], oh[:, NOH - SKEW:], start=True, stop=True)
            pe.wait_ge(ld_st, 48)
            for c in range(2):
                cols = slice(c * P, (c + 1) * P)
                pe.transpose(bank(6)[:, 384 + 24 * c:408 + 24 * c], states[0:24, 512 + c * P:512 + (c + 1) * P], ident[0:24, 0:24])
                pe.transpose(bank(6)[:, 432 + NB * c:440 + NB * c], states[0:NB, 768 + c * P:768 + (c + 1) * P], ident[0:NB, 0:NB])
                for a in range(2):
                    last = pe.transpose(bank(7)[:, 240 * c + 120 * a:240 * c + 120 * (a + 1)],
                                        states[0:120, 256 * a + c * P:256 * a + (c + 1) * P], ident[0:120, 0:120])
            last.then_inc(oh_used, 1)

        def pe_startup(pe):
            pe.wait_ge(ld_cst, 16)
            for n in range(9):
                if n == TABLES_AT:
                    pe_tables(pe)
                pe.wait_ge(x_scaled, n + 1)
                rows = P if n < NT else S
                for h in range(2):
                    m = 2 * n + h
                    if m >= 4:
                        pe.wait_ge(xt_done, m - 3)
                    for k in range(4):
                        kk = 4 * h + k
                        last = pe.transpose(bank(m % 4)[:, k * P:k * P + rows], xn[0:rows, n, kk * P:(kk + 1) * P], ident[0:rows, 0:rows])
                    last.then_inc(x_turned, 1)
            pe.wait_ge(xt_done, 18)

        def pe_project(pe, a, b):
            with pe.Fori(a, b) as i:
                for s in range(2):
                    pe.wait_ge(w_ld[s], i * 16 + 16)
                    pe.wait_ge(proj_sb[s], i + 1)
                    for j, (t0, n) in enumerate(CHUNKS):
                        for k in range(KD):
                            last = pe.matmul(bank(3 * s + j)[:, 0:n], ring[:, s, k * P:(k + 1) * P],
                                             xT[:, k, t0:t0 + n], start=(k == 0), stop=(k == KD - 1))
                    last.then_inc(proj_ps[s], 1)

        def pe_states(pe):
            pe.wait_ge(startup_evac, 7)
            pe.wait_ge(u_done, 1)
            b = mail_bank(M_ST)
            for c in range(2):
                pe.transpose(b[0:CB_W - 1, c * P:(c + 1) * P], uu[c][:, T - CB_W + 1:T], ident)
                last = pe.transpose(b[0:S, 256 + c * P:256 + (c + 1) * P], uu[c][:, T:], ident)
            post(pe, M_ST, last)
            b = mail_bank(M_ST + 1)
            for c in range(2):
                x = proj[:, XC + c, :]
                pe.transpose(b[0:3, c * P:(c + 1) * P], x[:, T - 3:T], ident)
                last = pe.transpose(b[0:S, 256 + c * P:256 + (c + 1) * P], x[:, T:], ident)
            post(pe, M_ST + 1, last)

        def pe_gates(pe):
            pe.wait_ge(ld_wbc, 16)
            pe.wait_ge(uc_done, 1)
            for k, (c, t0, n) in enumerate(CC + CC):
                m = M_GATE + k
                bank_free(pe, m)
                post(pe, m, pe.matmul(mail_bank(m)[:, 0:n], (w_a if k < 6 else w_x)[:, c, :], uc[c][:, t0:t0 + n], start=True, stop=True))

        def pe_mean(pe):
            pe.wait_ge(conv_done, 2)
            for k, (c, t0, n) in enumerate(CC):
                m = M_MEAN + k
                bank_free(pe, m)
                post(pe, m, pe.matmul(mail_bank(m)[:, 0:n], c_("groupmean"), conv[c][:, t0:t0 + n], start=True, stop=True))

        def pe_var(pe):
            for k, (c, t0, n) in enumerate(CC):
                m = M_VAR + k
                pe.wait_ge(sq_ready, k + 1)
                bank_free(pe, m)
                post(pe, m, pe.matmul(mail_bank(m)[:, 0:n], c_("groupmean"), scr2[c][:, t0:t0 + n], start=True, stop=True))

        def pe_pointwise(pe):
            pe.wait_ge(silu_n, 2)
            for k, (c, t0, n) in enumerate(CC):
                m = M_PW + k
                bank_free(pe, m)
                for kk in range(2):
                    last = pe.matmul(mail_bank(m)[:, 0:n], w_pw[:, kk, c * P:(c + 1) * P], conv[kk][:, t0:t0 + n], start=(kk == 0), stop=(kk == 1))
                post(pe, m, last)

        def pe_last_states(pe):
            pe.wait_ge(h_done, 2)
            m = M_H
            bank_free(pe, m)
            for c in range(2):
                last = pe.transpose(mail_bank(m)[0:1 + NB, c * P:(c + 1) * P], i_gate[c][:, T - 1::DS], ident)
            post(pe, m, last)

        def pe_branch_gates(pe):
            pe.wait_ge(ld_wc, 16)
            for j, (t0, n) in enumerate(CHUNKS):
                bank_free(pe, M_G + j)
                for k in range(KD):
                    last = pe.matmul(mail_bank(M_G + j)[0:3 * H, 0:n], w_gate[:, k, :], xT[:, k, t0:t0 + n], start=(k == 0), stop=(k == KD - 1))
                post(pe, M_G + j, last)

        def pe_turn_gates(pe):
            bank_free(pe, M_GT)
            pe.wait_ge(gates_sb, 3)
            for n in range(NT + 1):
                w = P if n < NT else S
                last = pe.transpose(mail_bank(M_GT)[0:w, n * 3 * H:(n + 1) * 3 * H], gates_t[0:3 * H, n * P:n * P + w], ident[0:3 * H, 0:3 * H])
            post(pe, M_GT, last)

        def carve(a, n):
            return MAIN[:, a:a + n]

        X0 = at["xT"]
        NAT = [VS, VW, KC, VC, KS, KW]
        nat = carve(X0, 6 * 9 * P).rearrange("p (s n c) -> p s n c", s=6, n=9)
        a1 = X0 + 6 * 9 * P
        ptc = carve(a1, NT * G * P).rearrange("p (i g q) -> p i g q", i=NT, g=G)
        qpad = carve(a1 + 2048, 2 * T).rearrange("p (g t) -> p g t", g=G)
        vcur = carve(a1 + 4096, P)
        psel, pwin = carve(a1 + 4224, T), carve(a1 + 4224 + T, 5 * P)
        pt = carve(a1 + 6272, 2 * 512).rearrange("p (b n) -> p b n", b=2)
        vb = carve(a1 + 7296, R * P).rearrange("p (r c) -> p r c", r=R)
        assert a1 + 7808 <= FREE
        sc = carve(0, 2048)
        kd = carve(0, 2 * PAST).rearrange("p (b n) -> p b n", b=2)
        vd = carve(X0, 2 * PAST).rearrange("p (b n) -> p b n", b=2)
        selectors = main("wcmp", 4 * 3 * P)
        NEW = PAST
        NEW_W = PAST + 3 * DS
        SN = PAST + 4 * DS + WIN
        sd = carve(X0 + 8192, SN)
        a2 = X0 + 8192 + SN
        ptd2 = carve(a2, 2 * 512).rearrange("p (b n) -> p b n", b=2)
        qcur = carve(a2 + 1024, P)
        pcur = carve(a2 + 1152, P)
        kncur = carve(a2 + 1280, 2 * 2 * DS).rearrange("p (b k t) -> p b k t", b=2, k=2)
        assert a2 + 1280 + 4 * DS <= FREE
        ktc = proj_flat[:, QT * TOK:QT * TOK + 2 * 1024].rearrange("p (a b n) -> p a b n", a=2, b=2)
        kw_d = diag[:, 0:4, :].rearrange("p h c -> p (h c)").rearrange("p (b n) -> p b n", b=2)
        vw_d = diag[:, 4:8, :].rearrange("p h c -> p (h c)").rearrange("p (b n) -> p b n", b=2)
        kct = late[:, 0:NB * P]
        scd = late[:, NB * P:NB * P + 4 * P].rearrange("p (a n) -> p a n", a=4)
        extb_flat = ext_b[:, :, :, :].rearrange("p c b t -> p (c b t)")
        extc_flat = ext_c[:, :, :, :].rearrange("p c b t -> p (c b t)")
        vccur = late[:, NB * P:NB * P + 2 * P]
        vncur = late[:, NB * P + 2 * P:NB * P + 4 * P]
        ptd = extb_flat[:, 0:4 * P]
        gtmp = extb_flat[:, 512:512 + 12 * H].rearrange("p (a h) -> p a h", h=H)
        vct = w_gate[:, :, :].rearrange("p k c -> p (k c)")[:, 0:P]
        kcs = extb_flat[:, 0:64].rearrange("p (k n) -> p k n", k=2)
        kcb, vc4 = extb_flat[:, 64:128], extb_flat[:, 128:256]
        mc, lc, top8 = extc_flat[:, 0:64], extc_flat[:, 64:128], extc_flat[:, 128:144]
        vn = cwb
        halves = half[:, :, :].rearrange("p a c -> p (a c)")
        pair4 = halves.rearrange("p (a n) -> p a n", a=4)
        kcn_flat = kcn[:, :, :].rearrange("p b c -> p (b c)")
        qbd = kcn_flat[:, 0:NB * Q].rearrange("p (b q) -> p b q", b=NB)
        vnt = kcn_flat[:, NB * Q:NB * Q + NB * 2 * DS]
        mask2 = kcn_flat[:, 640:768]
        osb = kcn_flat[:, 768:896]
        gd = sb("gd", [P, 4, 3])
        sm = sb("sm", [P, 48])
        topk = kcn_flat[:, 896:968]

        names = """bc_done nat_ps nat_out kc_ready vb_ready cmp_max cmp_exp cmp_p cmp_pt_ps cmp_pt kct_sb
            qbd_ready dc_sub dc_exp dc_pair dc_p ld_sel topk_done vnt_ready za_silu
            q_ready vcur_ready pair_done qk_s qk_w mx_s mx_w ex_s ex_w p_s p_w pt_ps pt_sb pv o_ps oz
            cur_ready cur_values kt_ps kt_sb dpair kused vused wkused wvused sd_ps sd_used mx_d ex_d dp_ps o_d o_sb ot_ps
            ld_gp ld_wo y_ps y_sq y_ms y_rt y_free y_out""".split()
        for n in names:
            assert n not in SEM
            SEM[n] = sem(n)
        kd_ld, vd_ld, kw_ld, vw_ld, dp_sb, dv = [[sem(f"{n}{b}") for b in range(2)] for n in
                                                               "kd_ld vd_ld kw_ld vw_ld dp_sb dv".split()]
        nat_sb = [sem("nat_sb0"), sem("nat_sb1")]
        xo_ld, y_st = [sem(f"xo_ld{b}") for b in range(3)], [sem(f"y_st{b}") for b in range(3)]


        def wait_projections(eng, i=NPROJ // 2):
            for s in range(2):
                eng.wait_ge(proj_sb[s], 1 + i)

        def pe_natural(pe):
            wait_projections(pe)
            for n in range(9):
                w = P if n < NT else S
                if n >= 2:
                    pe.wait_ge(nat_sb[n % 2], n // 2)
                b = bank(2 * (n % 2), 2)
                for s, c in enumerate(NAT):
                    last = pe.transpose(b[0:w, s * P:(s + 1) * P], proj[:, c, n * P:n * P + w], ident)
                last.then_inc(SEM["nat_ps"], 1)

        def natural(eng, par):
            for n in range(par, 9, 2):
                w = P if n < NT else S
                eng.wait_ge(SEM["nat_ps"], n + 1)
                o, i = nat[0:w, :, n, :], bank(2 * par, 2)[0:w, 0:6 * P].rearrange("p (s c) -> p s c", s=6)
                (eng.activation(o, i, ACT.Copy) if par == 0 else eng.tensor_copy(o, i)).then_inc(nat_sb[par], 1)

        def wait_natural(eng):
            eng.wait_ge(nat_sb[0], 5)
            eng.wait_ge(nat_sb[1], 4)

        def sp_natural(sp):
            for k, key in enumerate(("win_k", "win_v")):
                sp.dma_start(outs[11 + 2 * k][0, :, 0:WIN - DS].rearrange("b w g d -> b w (g d)"), dram[key][:, DS:, :]).then_inc(out_done, 16)
            wait_natural(sp)
            for s, o in ((2, 2), (3, 4), (4, 6), (0, 8)):
                sp.dma_start(outs[o][0, 0].rearrange("(n p) g d -> p n (g d)", p=P), nat[:, s, 0:NT, :]).then_inc(SEM["nat_out"], 16)
                sp.dma_start(outs[o + 1][0].rearrange("b t g d -> (b t) (g d)"), nat[0:S, s, 8, :]).then_inc(SEM["nat_out"], 16)
            for s, o in ((5, 10), (1, 12)):
                sp.dma_start(outs[o][0, 0].rearrange("(n p) g d -> p n (g d)", p=P), nat[:, s, NT - WIN // P:NT, :]).then_inc(SEM["nat_out"], 16)
                sp.dma_start(outs[o + 1][0, :, WIN - DS:].rearrange("b t g d -> b t (g d)"), nat[0:S, s, 8, :]).then_inc(SEM["nat_out"], 16)

        def dve_prompt_blocks(dve):
            wait_projections(dve, 8)
            q = proj_flat[:, QT * TOK:(QT + R) * TOK]
            dve.tensor_scalar(q, q, HD ** -0.5, None, ALU.mult)
            dve.memset(kcb, 0.0)
            for k, (c, w) in enumerate(((KC, "wk"), (VC, "wv"))):
                wb = p_(w, 0, L_CMP).rearrange("p (o j) -> p o j", o=1).to_broadcast([P, T // L_CMP, L_CMP])
                prod = scr[:, 0:T].rearrange("p (n j) -> p n j", j=L_CMP)
                dve.drain()
                dve.tensor_tensor(prod, proj[:, c, 0:T].rearrange("p (n j) -> p n j", j=L_CMP), wb, ALU.mult)
                dve.drain()
                dve.tensor_reduce(kcs[:, k, :], prod, X, ALU.add)
            dve.drain()
            for g in range(G):
                dve.tensor_copy(kcb[g * HD:(g + 1) * HD, g * 32:(g + 1) * 32], kcs[g * HD:(g + 1) * HD, 0, :])
            dve.tensor_copy(vc4.rearrange("p (r n) -> p r n", r=R), kcs[:, 1:2, :].to_broadcast([P, R, 32]))
            dve.drain().then_inc(SEM["kc_ready"], 1)

        def pe_prompt_blocks(pe):
            pe.wait_ge(SEM["kc_ready"], 1)
            bank_free(pe, M_VC)
            post(pe, M_VC, pe.transpose(mail_bank(M_VC)[:, 0:P], vc4, ident))
            for m in range(M_PC, M_PC + 4):
                bank_free(pe, m)
                s = mail_bank(m).rearrange("p (i r n) -> p i r n", i=2, r=R)
                for j in range(2):
                    i = 2 * (m - M_PC) + j
                    for r in range(R):
                        last = pe.matmul(s[:, j, r, :], proj[:, QT + r, i * P:(i + 1) * P], kcb, start=True, stop=True)
                post(pe, m, last)

        def act_prompt_values(act):
            posted(act, M_VC)
            act.activation(vct, mail_bank(M_VC)[:, 0:P], ACT.Copy).then_inc(taken[M_VC % 2], 1)

        def dve_prompt_cmp(dve):
            o = sc.rearrange("p (i g r n) -> p i g r n", i=NT, r=R, g=G)
            for m in range(M_PC, M_PC + 4):
                posted(dve, m)
                for j in range(2):
                    i = 2 * (m - M_PC) + j
                    s = mail_bank(m)[:, j * 256:(j + 1) * 256].rearrange("p (r g n) -> p g r n", r=R, g=G)
                    b = cbias[:, :, 28 - 4 * i:60 - 4 * i].rearrange("p (g r) n -> p g r n", g=G)
                    last = dve.tensor_tensor(o[:, i], s, b, ALU.add)
                last.then_inc(taken[m % 2], 1)
            dve.wait_ge(taken[m % 2], m // 2 + 1)
            rows = sc.rearrange("p (h n) -> p h n", n=32)
            spread = lambda x: x.rearrange("p (h o) -> p h o", o=1).to_broadcast([P, 64, 32])
            dve.drain()
            dve.tensor_reduce(mc, rows, X, ALU.max)
            dve.drain()
            dve.tensor_scalar(mc, mc, NEG / 10, None, ALU.max)
            dve.drain()
            dve.tensor_tensor(rows, rows, spread(mc), ALU.subtract).then_inc(SEM["cmp_max"], 1)

        def dve_prompt_norm(dve):
            rows = sc.rearrange("p (h n) -> p h n", n=32)
            spread = lambda x: x.rearrange("p (h o) -> p h o", o=1).to_broadcast([P, 64, 32])
            dve.wait_ge(SEM["cmp_exp"], 1)
            dve.tensor_reduce(lc, rows, X, ALU.add)
            dve.drain()
            dve.tensor_scalar(lc, lc, 1e-30, None, ALU.max)
            dve.drain()
            dve.reciprocal(lc, lc)
            dve.wait_ge(gate_done, 1)
            dve.drain()
            dve.tensor_tensor(lc.rearrange("p (i h) -> p i h", h=H), lc.rearrange("p (i h) -> p i h", h=H), gate_n[:, :, 0:H], ALU.mult)
            dve.drain()
            dve.tensor_tensor(rows, rows, spread(lc), ALU.mult).then_inc(SEM["cmp_p"], 1)

        def act_prompt_exp(act):
            act.wait_ge(SEM["cmp_max"], 1)
            act.activation(sc, sc, ACT.Exp).then_inc(SEM["cmp_exp"], 1)

        def pe_prompt_turn(pe):
            pe.wait_ge(SEM["cmp_p"], 1)
            wait_natural(pe)
            for k in range(2 * NT):
                last = pe.transpose(bank(0, 4)[:, k * P:(k + 1) * P], sc[:, k * P:(k + 1) * P], ident)
            last.then_inc(SEM["cmp_pt_ps"], 1)

        def act_prompt_turn(act):
            act.wait_ge(SEM["cmp_pt_ps"], 1)
            flat = ptc.rearrange("p i g q -> p (i g q)")
            for h in range(2):
                act.activation(flat[:, h * T:(h + 1) * T], bank(2 * h, 2), ACT.Copy)
            act.drain().then_inc(SEM["cmp_pt"], 1)

        def act_branch_a_gates(act, c0, c1):
            act.drain()
            for c in range(c0, c1):
                act.activation(proj[:, ZA + c, :], proj[:, ZA + c, :], ACT.Silu)
            act.drain().then_inc(SEM["za_silu"], 1)

        def pe_decode_keys(pe):
            pe.wait_ge(k_compressed, 1)
            for m in range(M_KT, M_KT + 2):
                bank_free(pe, m)
                for b in range(4):
                    last = pe.transpose(mail_bank(m)[:, b * P:(b + 1) * P], kcn[:, 4 * (m - M_KT) + b, :], ident)
                post(pe, m, last)

        def act_decode_keys(act):
            act.wait_ge(SEM["kc_ready"], 1)
            for m in range(M_KT, M_KT + 2):
                posted(act, m)
                act.activation(kct[:, (m - M_KT) * 512:(m - M_KT + 1) * 512], mail_bank(m), ACT.Copy).then_inc(taken[m % 2], 1)
            act.wait_ge(taken[m % 2], m // 2 + 1)
            act.drain().then_inc(SEM["kct_sb"], 1)

        def dve_decode_queries(dve):
            dve.wait_ge(SEM["kct_sb"], 1)
            dve.memset(kcn_flat[:, 0:NB * Q], 0.0)
            dve.drain()
            for g in range(G):
                rows = slice(g * HD, (g + 1) * HD)
                for r in range(R):
                    dve.tensor_copy(qbd[rows].rearrange("p b (g t r) -> p b g t r", g=G, r=R)[:, :, g, :, r],
                                    proj[rows, QT + r, T:].rearrange("p (b t) -> p b t", b=NB))
            dve.drain().then_inc(SEM["qbd_ready"], 1)

        def dve_new_values(dve):
            wait_projections(dve, 10)
            for k, c in enumerate((VS, VW)):
                dve.tensor_copy(vnt.rearrange("p (b k t) -> p b k t", b=NB, k=2)[:, :, k, :], proj[:, c, T:].rearrange("p (b t) -> p b t", b=NB))
            dve.drain().then_inc(SEM["vnt_ready"], 1)

        def act_selectors(act):
            act.wait_ge(k_compressed, 2)
            act.dma_start(selectors, dram["selectors"]).then_inc(SEM["ld_sel"], 16)

        def pe_decode_cmp(pe):
            pe.wait_ge(SEM["ld_sel"], 16)
            pe.wait_ge(gate_done, 1)
            bank_free(pe, M_TG)
            for pr in range(4):
                last = pe.matmul(mail_bank(M_TG)[:, pr * 24:(pr + 1) * 24], sel(pr, 2)[0:S, :], gate_t[:, :], start=True, stop=True)
            post(pe, M_TG, last)
            pe.wait_ge(SEM["qbd_ready"], 1)
            bank_free(pe, M_DC)
            for b in range(NB):
                last = pe.matmul(mail_bank(M_DC)[Q * (b % 2):Q * (b % 2 + 1), b // 2 * P:(b // 2 + 1) * P], qbd[:, b, :], kct[:, b * P:(b + 1) * P], start=True, stop=True)
            post(pe, M_DC, last)

        def sel(pr, k):
            return selectors[:, (pr * 3 + k) * P:(pr * 3 + k + 1) * P]

        def dve_decode_cmp(dve):
            posted(dve, M_TG)
            hm = c_("head").rearrange("p (o h) -> p o h", o=1).to_broadcast([P, 12, H])
            dve.tensor_tensor(gtmp[:, :, :], mail_bank(M_TG)[:, 0:96].rearrange("p (a h) -> p a h", h=H), hm, ALU.mult).then_inc(taken[M_TG % 2], 1)
            dve.wait_ge(taken[M_TG % 2], M_TG // 2 + 1)
            dve.tensor_reduce(gd[:, :, :].rearrange("p a b -> p (a b)"), gtmp[:, :, :], X, ALU.add)
            posted(dve, M_DC)
            spread = lambda x: x.rearrange("p (a o) -> p a o", o=1).to_broadcast([P, 4, P])
            bias = dec_bias[:, 0:NCB].rearrange("p (o n) -> p o n", o=1).to_broadcast([P, 4, P])
            dve.tensor_tensor(scd, mail_bank(M_DC).rearrange("p (a n) -> p a n", a=4), bias, ALU.add).then_inc(taken[M_DC % 2], 1)
            dve.wait_ge(taken[M_DC % 2], M_DC // 2 + 1)
            dve.tensor_reduce(sm[:, 0:4], scd, X, ALU.max)
            dve.drain()
            dve.tensor_tensor(scd, scd, spread(sm[:, 0:4]), ALU.subtract).then_inc(SEM["dc_sub"], 1)
            dve.wait_ge(SEM["dc_exp"], 1)
            dve.tensor_reduce(sm[:, 4:8], scd, X, ALU.add)
            dve.drain()
            dve.reciprocal(sm[:, 4:8], sm[:, 4:8])
            dve.drain()
            dve.tensor_tensor(scd, scd, spread(sm[:, 4:8]), ALU.mult)
            dve.drain()
            two = scd.rearrange("p a (n k) -> p a n k", k=2)
            dve.tensor_tensor(pair4, two[:, :, :, 0], two[:, :, :, 1], ALU.add).then_inc(SEM["dc_pair"], 1)
            dve.drain()
            dve.tensor_tensor(scd, scd, spread(gd[:, :, 0]), ALU.mult).then_inc(SEM["dc_p"], 1)

        def act_decode_exp(act):
            act.wait_ge(SEM["dc_sub"], 1)
            act.activation(scd, scd, ACT.Exp).then_inc(SEM["dc_exp"], 1)

        def pe_importance(pe):
            pe.wait_ge(SEM["dc_pair"], 1)
            bank_free(pe, M_IMP)
            for pr in range(4):
                last = pe.matmul(mail_bank(M_IMP)[:, 0:NBLK], sel(pr, 1), pair4[:, pr, :], start=(pr == 0), stop=(pr == 3))
            post(pe, M_IMP, last)
            pe.wait_ge(SEM["dc_p"], 1)
            bank_free(pe, M_DPT)
            for pr in range(4):
                last = pe.transpose(mail_bank(M_DPT)[:, pr * P:(pr + 1) * P], scd[:, pr, :], ident)
            post(pe, M_DPT, last)

        def dve_select(dve):
            posted(dve, M_IMP)
            dve.tensor_copy(topk[:, 1:NBLK - 1], mail_bank(M_IMP)[:, 1:NBLK - 1]).then_inc(taken[M_IMP % 2], 1)
            dve.memset(topk[:, 0:1], FORCE)
            dve.memset(topk[:, NBLK - 1:NBLK + 1], FORCE)
            for k in range(TOP_K // 8):
                dve.drain()
                dve.max(top8[:, 8 * k:8 * k + 8], topk[:, 0:NBLK + 1])
                dve.drain()
                dve.match_replace(topk[:, 0:NBLK + 1], top8[:, 8 * k:8 * k + 8], topk[:, 0:NBLK + 1], -2.0)
            dve.drain()
            dve.tensor_scalar(topk[:, 0:NBLK], topk[:, 0:NBLK], -2.0, NEG, ALU.not_equal, ALU.mult).then_inc(SEM["topk_done"], 1)

        def act_decode_turn(act):
            act.wait_ge(SEM["cmp_max"], 1)
            posted(act, M_DPT)
            act.activation(ptd, mail_bank(M_DPT), ACT.Copy).then_inc(taken[M_DPT % 2], 1)

        def pe_masks(pe):
            pe.wait_ge(SEM["topk_done"], 1)
            bank_free(pe, M_MASK)
            for pr in range(4):
                last = pe.matmul(mail_bank(M_MASK)[:, pr * NBLK:(pr + 1) * NBLK], sel(pr, 0), topk[:, 0:NBLK], start=True, stop=True)
            post(pe, M_MASK, last)
            pe.wait_ge(SEM["vnt_ready"], 1)
            for h in range(2):
                m = M_VN + h
                bank_free(pe, m)
                for b in range(4):
                    last = pe.transpose(mail_bank(m)[0:2 * DS, b * P:(b + 1) * P], vnt[:, (4 * h + b) * 2 * DS:(4 * h + b + 1) * 2 * DS], ident)
                post(pe, m, last)

        def act_masks(act):
            posted(act, M_MASK)
            act.activation(halves, mail_bank(M_MASK)[:, 0:4 * NBLK], ACT.Copy).then_inc(taken[M_MASK % 2], 1)
            for h in range(2):
                posted(act, M_VN + h)
                act.activation(vn[0:2 * DS, h * 512:(h + 1) * 512], mail_bank(M_VN + h)[0:2 * DS, :], ACT.Copy).then_inc(taken[(M_VN + h) % 2], 1)

        UNITS = [(i, g) for i in range(NT) for g in range(G)]

        def tiles_of(k):
            i = UNITS[k][0]
            w0 = max(0, i - WIN // P)
            return list(range(i + 1)), list(range(w0, i + 1))

        chunk_of, nch = {}, 0
        for k in range(len(UNITS)):
            for br in range(2):
                ts = tiles_of(k)[br]
                chunk_of[k, br] = [(nch + c, ts[4 * c:4 * c + 4]) for c in range((len(ts) + 3) // 4)]
                nch += len(chunk_of[k, br])
        NCH, NU = nch, len(UNITS)
        assert NCH % 2 == 0

        def dve_pairs_prepare(dve):
            wait_projections(dve)
            dve.memset(vb, 0.0)
            dve.wait_ge(taken[M_VC % 2], M_VC // 2 + 1)
            dve.drain()
            for r in range(R):
                dve.tensor_copy(vb[32 * r:32 * r + 32, r, :], vct[32 * r:32 * r + 32, :])
            dve.memset(qpad[HD:P, 0, :], 0.0)
            dve.memset(qpad[0:HD, 1, :], 0.0)
            for g in range(G):
                rows = slice(g * HD, (g + 1) * HD)
                dve.tensor_copy(qpad[rows, g, :], proj[rows, QT, 0:T])
            for _ in range(NT):
                dve.drain().then_inc(SEM["q_ready"], 1)
            dve.drain().then_inc(SEM["vb_ready"], 1)
            for _ in range(2):
                dve.drain().then_inc(SEM["oz"], 1)

        def following(k, r):
            return (k, r) if k < NU else (0, r + 1)

        def act_pairs(act):
            for _ in range(2):
                act.drain().then_inc(SEM["pt_sb"], 1)
            act.wait_ge(SEM["vb_ready"], 1)

            def queries(i, r):
                for g in range(G):
                    rows = slice(g * HD, (g + 1) * HD)
                    last = act.activation(qpad[rows, g, i * P:(i + 1) * P], proj_flat[rows, bass.ds(r * TOK + (QT * TOK + i * P), P)], ACT.Copy)
                act.drain().then_inc(SEM["q_ready"], 1)

            def evac(k, br, r):
                for c, ts in chunk_of[k, br]:
                    act.wait_ge(SEM["pt_ps"], r * NCH + (c + 1))
                    act.wait_ge(SEM["pv"], r * NCH + (c + 1))
                    n = len(ts) * P
                    act.activation(pt[:, c % 2, 0:n], bank(4 + c % 2)[:, 0:n], ACT.Copy).then_inc(SEM["pt_sb"], 1)

            def exp(k, br, r):
                n = len(tiles_of(k)[br]) * P
                act.wait_ge(SEM["mx_s" if br == 0 else "mx_w"], r * NU + (k + 1))
                act.activation((psel, pwin)[br][:, 0:n], bank(2 * br, 2)[:, 0:n], ACT.Exp, bias=sm[:, 8 + br:9 + br],
                               accum_out=sm[:, 10 + br:11 + br]).then_inc(SEM["ex_s" if br == 0 else "ex_w"], 1)
            for br in range(2):
                exp(0, br, 0)
            with act.Fori(0, R) as r:
                act.wait_ge(SEM["pair_done"], r + 1)
                act.activation(vcur, vb[:, bass.ds(r, 1), :].rearrange("p o c -> p (o c)"), ACT.Copy).then_inc(SEM["vcur_ready"], 1)
                for k in range(1, NU + 1):
                    k1, r1 = following(k, r)
                    evac(k - 1, 0, r)
                    exp(k1, 0, r1)
                    evac(k - 1, 1, r)
                    exp(k1, 1, r1)
                    if k < NU and UNITS[k][1] == 1:
                        queries(UNITS[k][0], r + 1)

        def dve_pairs(dve):
            def peak(k, br, r):
                (i, g), ts = UNITS[k], tiles_of(k)[br]
                n = len(ts) * P
                s = bank(2 * br, 2)[:, 0:n]
                dve.wait_ge(SEM["qk_s" if br == 0 else "qk_w"], r * NU + (k + 1))
                w = min(n, 2 * P)
                d = diag[:, bass.ds(r + g * R, 1), 2 * P - w:].rearrange("p o c -> p (o c)")
                dve.tensor_tensor(s[:, n - w:], s[:, n - w:], d, ALU.add)
                if br == 1 and i >= WIN // P:
                    dve.tensor_tensor(s[:, 0:P], s[:, 0:P], c_("winmask"), ALU.add)
                dve.drain()
                dve.tensor_reduce(sm[:, 8 + br:9 + br], s, X, ALU.max, negate=True).then_inc(SEM["mx_s" if br == 0 else "mx_w"], 1)

            def scale(k, br, r):
                (i, g), n = UNITS[k], len(tiles_of(k)[br]) * P
                dve.wait_ge(SEM["ex_s" if br == 0 else "ex_w"], r * NU + (k + 1))
                w = sm[:, 12 + br:13 + br]
                dve.reciprocal(w, sm[:, 10 + br:11 + br])
                dve.drain()
                gate = gate_n[:, i, bass.ds(r + ((br + 1) * H + g * R), 1)]
                p = (psel, pwin)[br][:, 0:n]
                dve.tensor_scalar(p, p, w, gate, ALU.mult, ALU.mult).then_inc(SEM["p_s" if br == 0 else "p_w"], 1)

            def gated(i, r):
                dve.wait_ge(SEM["o_ps"], r * NT + (i + 1))
                z = proj_flat[:, bass.ds(r * TOK + (ZA * TOK + i * P), P)]
                dve.tensor_tensor(z, bank(6 + i % 2)[:, 0:P], z, ALU.mult).then_inc(SEM["oz"], 1)
            peak(0, 0, 0)
            peak(0, 1, 0)
            scale(0, 0, 0)
            dve.wait_ge(SEM["za_silu"], 2)
            with dve.Fori(0, R) as r:
                for k in range(1, NU + 1):
                    k1, r1 = following(k, r)
                    scale(k - 1, 1, r)
                    peak(k1, 0, r1)
                    peak(k1, 1, r1)
                    scale(k1, 0, r1)
                    if k >= 2 and UNITS[k - 2][1] == 1:
                        gated(UNITS[k - 2][0], r)
                gated(NT - 1, r)
            dve.wait_ge(SEM["ex_w"], R * NU + 1)

        def pe_pairs(pe):
            pe.wait_ge(SEM["cmp_pt"], 1)
            for h in range(2):
                pe.wait_ge(taken[(M_VN + h) % 2], (M_VN + h) // 2 + 1)
            pe.drain().then_inc(SEM["pair_done"], 1)
            for _ in range(2):
                pe.drain().then_inc(SEM["pv"], 1)
            pe.wait_ge(strip_in, 16)

            def scores(k, br, r, first=False):
                (i, g), ts = UNITS[k], tiles_of(k)[br]
                if g == 0:
                    pe.wait_ge(SEM["q_ready"], r * NT + (i + 1))
                if not first:
                    pe.wait_ge(SEM["ex_s" if br == 0 else "ex_w"], r * NU + k)
                n, k0 = len(ts) * P, ts[0] * P
                for a in range(0, n, 512):
                    m = min(512, n - a)
                    last = pe.matmul(bank(2 * br, 2)[:, a:a + m], qpad[:, g, i * P:(i + 1) * P],
                                     proj[:, (KS, KW)[br], k0 + a:k0 + a + m], start=True, stop=True)
                last.then_inc(SEM["qk_s" if br == 0 else "qk_w"], 1)

            def turn(r, c, k, br, ts):
                if ts[0] == tiles_of(k)[br][0]:
                    pe.wait_ge(SEM["p_s" if br == 0 else "p_w"], r * NU + (k + 1))
                pe.wait_ge(SEM["pt_sb"], r * NCH + (c + 1))
                for e, t in enumerate(ts):
                    off = (t - tiles_of(k)[br][0]) * P
                    last = pe.transpose(bank(4 + c % 2)[:, e * P:(e + 1) * P], (psel, pwin)[br][:, off:off + P], ident)
                last.then_inc(SEM["pt_ps"], 1)

            def values(r, c, k, br, ts):
                i, g = UNITS[k]
                o = bank(6 + i % 2)[g * HD:(g + 1) * HD, 0:P]
                if br == 0 and ts[0] == 0:
                    if g == 0:
                        pe.wait_ge(SEM["oz"], r * NT + (i + 1))
                    if k == 0:
                        pe.wait_ge(SEM["vcur_ready"], r + 1)
                    pe.matmul(o, vcur[:, g * HD:(g + 1) * HD], ptc[:, i, g, :], start=True, stop=False)
                pe.wait_ge(SEM["pt_sb"], r * NCH + (c + 3))
                for e, t in enumerate(ts):
                    end = br == 1 and t == i
                    last = pe.matmul(o, nat[:, br, t, g * HD:(g + 1) * HD], pt[:, c % 2, e * P:(e + 1) * P], start=False, stop=end)
                last.then_inc(SEM["pv"], 1)
                if end and g == 1:
                    pe.drain().then_inc(SEM["o_ps"], 1)
            for br in range(2):
                scores(0, br, 0, first=True)
            with pe.Fori(0, R) as r:
                late_chunk = None
                for k in range(1, NU + 1):
                    k1, r1 = following(k, r)
                    chunks = [(c, k - 1, br, ts) for br in range(2) for c, ts in chunk_of[k - 1, br]]
                    for br in range(2):
                        scores(k1, br, r1)
                    for chunk in chunks:
                        turn(r, *chunk)
                        if late_chunk:
                            values(r, *late_chunk)
                        late_chunk = chunk
                values(r, *late_chunk)
                pe.drain().then_inc(SEM["pair_done"], 1)

        NC = PAST // 512

        def pool_decode(pool):
            for pr in range(4):
                for b2 in range(2):
                    if pr == 0 and b2 == 0:
                        pool.wait_ge(taken[M_MASK % 2], M_MASK // 2 + 1)
                        pool.wait_ge(SEM["cmp_pt_ps"], 1)
                        pool.wait_ge(so_out, 16 * N_SO)
                    elif b2 == 0:
                        pool.wait_ge(SEM["kused"], pr)
                    pool.indirect_dma_start(kd[:, b2, :], None, dram["sel_k"],
                                            bass.IndirectOffsetOnAxis(row16[:, 2 * pr + b2:2 * pr + b2 + 1], 0)).then_inc(kd_ld[b2], 16)
                for b2 in range(2):
                    if b2 == 0 and pr == 0:
                        pool.wait_ge(SEM["pair_done"], R + 1)
                        pool.wait_ge(SEM["nat_out"], 16 * N_NAT)
                    elif b2 == 0:
                        pool.wait_ge(SEM["vused"], pr)
                    pool.indirect_dma_start(vd[:, b2, :], None, dram["sel_v"],
                                            bass.IndirectOffsetOnAxis(row16[:, 2 * pr + b2:2 * pr + b2 + 1], 0)).then_inc(vd_ld[b2], 16)

        def sp_decode(sp):
            for pr in range(4):
                for src, dst, ld, used in ((dram["win_k"], kw_d, kw_ld, "wkused"), (dram["win_v"], vw_d, vw_ld, "wvused")):
                    if pr == 0:
                        sp.wait_ge(SEM["oz"], 2 + NT * R)
                    else:
                        sp.wait_ge(SEM[used], pr + 1)
                    for b2 in range(2):
                        sp.dma_start(dst[:, b2, :], src[2 * pr + b2].rearrange("(p j) c -> p (j c)", p=P)).then_inc(ld[b2], 16)

        PIECES = 4

        def turned(eng, c, pr):
            par = c % 2
            eng.wait_ge(SEM["dp_ps"], pr * (NC + 2) + (c + 1))
            if c >= 2:
                eng.wait_ge(dv[par], pr * ((NC + 2) // 2) + c // 2)
            rows, n = (P, 512) if c <= NC else (2 * DS, 2 * P)
            o, i = ptd2[0:rows, par, 0:n], bank(4 + par)[0:rows, 0:n]
            (eng.activation(o, i, ACT.Copy) if par == 0 else eng.tensor_copy(o, i)).then_inc(dp_sb[par], 1)

        def act_decode(act):
            act.wait_ge(SEM["dpair"], 1)
            with act.Fori(0, 4) as pr:
                act.wait_ge(SEM["wkused"], pr + 1)
                act.activation(qcur, kcn_flat[:, bass.ds(pr * 2 * Q, 2 * Q)], ACT.Copy)
                new = proj[:, KS:KW + 1:2, bass.ds(pr * 2 * DS + T, 2 * DS)]
                act.activation(kncur, new.rearrange("p k (b t) -> p b k t", b=2), ACT.Copy)
                act.drain().then_inc(SEM["cur_ready"], 1)
                for c in range(NC + 1):
                    act.wait_ge(SEM["kt_ps"], pr * (NC + 1) + (c + 1))
                    if c >= 2:
                        act.wait_ge(SEM["sd_ps"], pr * (NC + 1) + (c - 1))
                    act.activation(ktc[:, c % 2].rearrange("p b n -> p (b n)"), bank(2 + 2 * (c % 2), 2), ACT.Copy).then_inc(SEM["kt_sb"], 1)
                act.wait_ge(SEM["wvused"], pr + 1)
                act.activation(pcur, ptd[:, bass.ds(pr * P, P)], ACT.Copy)
                act.activation(vccur, vcn_flat[:, bass.ds(pr * 2 * P, 2 * P)], ACT.Copy)
                act.activation(vncur[0:2 * DS, :], vn[0:2 * DS, bass.ds(pr * 2 * P, 2 * P)], ACT.Copy).then_inc(SEM["cur_values"], 1)
                act.wait_ge(SEM["mx_d"], pr + 1)
                for n in range(PIECES):
                    if n >= 2:
                        turned(act, 2 * (n - 2), pr)
                    a, b = n * PAST // PIECES, (n + 1) * PAST // PIECES + (DS if n == PIECES - 1 else 0)
                    act.activation(sd[:, a:b], sd[:, a:b], ACT.Exp, bias=sm[:, 40:41], accum_out=sm[:, 28 + n:29 + n]).then_inc(SEM["ex_d"], 1)
                act.activation(sd[:, NEW_W:], sd[:, NEW_W:], ACT.Exp, bias=sm[:, 41:42], accum_out=sm[:, 43:44]).then_inc(SEM["ex_d"], 1)
                for c in range(2 * (PIECES - 2), NC + 2, 2):
                    turned(act, c, pr)

        def dve_decode(dve):
            dve.memset(sd[:, NEW + DS:NEW_W], 0.0)
            dve.drain().then_inc(SEM["dpair"], 1)
            near = dec_bias[:, NCB:NCB + L_CMP * NEAR].rearrange("p (j e) -> p j e", e=NEAR)
            new = dec_bias[:, NCB + L_CMP * NEAR:NCB + L_CMP * NEAR + DS]
            win = dec_bias[:, NBIAS - WIN:]
            peaks = sm[:, 16:16 + NC + 3]
            with dve.Fori(0, 4) as pr:
                dve.tensor_copy(mask2.rearrange("p (n k) -> p n k", k=2),
                                halves[:, bass.ds(pr * NBLK, NBLK)].rearrange("p (n o) -> p n o", o=1).to_broadcast([P, NBLK, 2]))
                dve.drain()
                for c in range(NC + 1):
                    dve.wait_ge(SEM["sd_ps"], pr * (NC + 1) + (c + 1))
                    s = bank(c % 2)
                    if c < NC:
                        v = s.rearrange("p (j k) -> p j k", j=4)
                        e = v[:, :, P - NEAR:]
                        dve.tensor_tensor(e, e, near[:, 4 * c:4 * c + 4, :], ALU.add)
                        dve.drain()
                        m = mask2.rearrange("p (o k) -> p o k", o=1).to_broadcast([P, 4, P])
                        dve.tensor_tensor_reduce(sd[:, c * 512:(c + 1) * 512].rearrange("p (j k) -> p j k", j=4), v, m, 1.0, NEG,
                                                 ALU.add, ALU.max, peaks[:, c:c + 1]).then_inc(SEM["sd_used"], 1)
                    else:
                        two = sd[:, NEW:NEW + 4 * DS].rearrange("p (k t) -> p k t", t=DS)[:, 0:4:3, :]
                        dve.tensor_tensor(two, bank(7)[:, 0:2 * DS].rearrange("p (k t) -> p k t", k=2),
                                          new.rearrange("p (o t) -> p o t", o=1).to_broadcast([P, 2, DS]), ALU.add)
                        dve.tensor_tensor_reduce(sd[:, NEW_W + DS:], s, win, 1.0, NEG, ALU.add, ALU.max, peaks[:, NC + 2:NC + 3])
                        dve.drain()
                        dve.tensor_reduce(peaks[:, NC:NC + 2], two, X, ALU.max)
                dve.drain()
                dve.tensor_reduce(sm[:, 40:41], peaks[:, 0:NC + 1], X, ALU.max, negate=True)
                dve.tensor_reduce(sm[:, 41:42], peaks[:, NC + 1:], X, ALU.max, negate=True)
                dve.drain().then_inc(SEM["mx_d"], 1)
                for c in range(1, NC + 2, 2):
                    turned(dve, c, pr)
                dve.tensor_reduce(sm[:, 42:43], sm[:, 28:28 + PIECES], X, ALU.add)
                dve.drain()
                dve.reciprocal(sm[:, 42:44], sm[:, 42:44])
                dve.drain()
                dve.tensor_tensor(sm[:, 44:46], sm[:, 42:44], gd[:, bass.ds(pr, 1), 1:3].rearrange("p o b -> p (o b)"), ALU.mult)
                dve.drain()
                dve.wait_ge(SEM["o_d"], pr + 1)
                dve.tensor_scalar(osb, bank(7)[:, P:2 * P], sm[:, 45:46], None, ALU.mult)
                dve.drain()
                dve.scalar_tensor_tensor(osb, bank(6)[:, 0:P], sm[:, 44:45], osb, ALU.mult, ALU.add)
                dve.drain()
                dve.tensor_tensor(osb, osb, bank(6)[:, P:2 * P], ALU.add).then_inc(SEM["o_sb"], 1)
                dve.wait_ge(SEM["ot_ps"], pr + 1)
                for g in range(G):
                    rows = slice(g * HD, (g + 1) * HD)
                    o = bank(6)[rows, 2 * P:3 * P].rearrange("p (b g t r) -> p g r b t", b=2, g=G, r=R)[:, g]
                    z = proj[rows, ZA:ZA + R, bass.ds(pr * 2 * DS + T, 2 * DS)].rearrange("p r (b t) -> p r b t", b=2)
                    dve.tensor_tensor(z, o, z, ALU.mult)
                dve.drain().then_inc(SEM["dpair"], 1)

        def pe_decode(pe):
            pe.wait_ge(SEM["oz"], 2 + NT * R)
            for name in ("ex_s", "ex_w"):
                pe.wait_ge(SEM[name], R * NU + 1)
            pe.drain().then_inc(SEM["wkused"], 1)
            pe.drain().then_inc(SEM["wvused"], 1)
            with pe.Fori(0, 4) as pr:
                def turn(c):
                    if c == 0 or c == NC:
                        for b2 in range(2):
                            pe.wait_ge((kd_ld if c == 0 else kw_ld)[b2], pr * 16 + 16)
                    if c >= 2:
                        pe.wait_ge(SEM["kt_sb"], pr * (NC + 1) + (c - 1))
                    for b2 in range(2):
                        src = kd[:, b2, c * 512:(c + 1) * 512] if c < NC else kw_d[:, b2, :]
                        for j in range(4):
                            last = pe.transpose(bank(2 + 2 * (c % 2) + b2)[:, j * P:(j + 1) * P], src[:, j * P:(j + 1) * P], ident)
                    last.then_inc(SEM["kt_ps"], 1)

                def scores(c):
                    if 2 <= c:
                        pe.wait_ge(SEM["sd_used"], pr * NC + (c - 1))
                    pe.wait_ge(SEM["kt_sb"], pr * (NC + 1) + (c + 1))
                    for b2 in range(2):
                        last = pe.matmul(bank(c % 2)[Q * b2:Q * (b2 + 1), :], qcur[:, Q * b2:Q * (b2 + 1)], ktc[:, c % 2, b2, :], start=True, stop=True)
                    last.then_inc(SEM["sd_ps"], 1)
                turn(0)
                turn(1)
                pe.wait_ge(SEM["cur_ready"], pr + 1)
                for c in range(NC + 1):
                    if c == NC:
                        for b2 in range(2):
                            pe.matmul(bank(7)[Q * b2:Q * (b2 + 1), 0:2 * DS], qcur[:, Q * b2:Q * (b2 + 1)], kncur[:, b2].rearrange("p k t -> p (k t)"), start=True, stop=True)
                    scores(c)
                    if c + 2 <= NC:
                        turn(c + 2)
                    if c == NC - 2:
                        pe.drain().then_inc(SEM["kused"], 1)
                pe.drain().then_inc(SEM["wkused"], 1)

                def turn_p(c):
                    if c >= 2:
                        pe.wait_ge(dp_sb[c % 2], pr * ((NC + 2) // 2) + c // 2)
                    if c <= NC:
                        if c % 2 == 0:
                            pe.wait_ge(SEM["ex_d"], pr * (PIECES + 1) + (c // 2 + 1))
                        a = c * 512 if c < NC else NEW_W + DS
                        for j in range(4):
                            last = pe.transpose(bank(4 + c % 2)[:, j * P:(j + 1) * P], sd[:, a + j * P:a + (j + 1) * P], ident)
                    else:
                        for k in range(2):
                            last = pe.transpose(bank(4 + c % 2)[0:2 * DS, k * P:(k + 1) * P], sd[:, NEW + 2 * DS * k:NEW + 2 * DS * (k + 1)], ident)
                    last.then_inc(SEM["dp_ps"], 1)

                selected = lambda b2: bank(6)[Q * b2:Q * (b2 + 1), 0:P]
                window = lambda b2: bank(7)[Q * b2:Q * (b2 + 1), P:2 * P]

                def values(c):
                    pe.wait_ge(dp_sb[c % 2], pr * ((NC + 2) // 2) + (c // 2 + 1))
                    if c in (0, NC):
                        for b2 in range(2):
                            pe.wait_ge((vd_ld if c == 0 else vw_ld)[b2], pr * 16 + 16)
                    if c <= NC:
                        for j in range(4):
                            for b2 in range(2):
                                o = selected(b2) if c < NC else window(b2)
                                v = (vd[:, b2, c * 512:(c + 1) * 512] if c < NC else vw_d[:, b2, :])[:, j * P:(j + 1) * P]
                                last = pe.matmul(o, ptd2[:, c % 2, j * P + Q * b2:j * P + Q * (b2 + 1)], v, start=(c in (0, NC) and j == 0), stop=False)
                    else:
                        for k, o in enumerate((selected, window)):
                            for b2 in range(2):
                                last = pe.matmul(o(b2), ptd2[0:2 * DS, c % 2, k * P + Q * b2:k * P + Q * (b2 + 1)],
                                                 vncur[0:2 * DS, b2 * P:(b2 + 1) * P], start=False, stop=True)
                    last.then_inc(dv[c % 2], 1)
                pe.wait_ge(SEM["cur_values"], pr + 1)
                for b2 in range(2):
                    pe.matmul(bank(6)[Q * b2:Q * (b2 + 1), P:2 * P], pcur[:, Q * b2:Q * (b2 + 1)],
                              vccur[:, b2 * P:(b2 + 1) * P], start=True, stop=True)
                turn_p(0)
                for c in range(NC + 2):
                    if c <= NC:
                        turn_p(c + 1)
                    values(c)
                    if c == NC - 1:
                        pe.drain().then_inc(SEM["vused"], 1)
                pe.drain().then_inc(SEM["wvused"], 1)
                pe.drain().then_inc(SEM["o_d"], 1)
                pe.wait_ge(SEM["o_sb"], pr + 1)
                pe.transpose(bank(6)[:, 2 * P:3 * P], osb, ident).then_inc(SEM["ot_ps"], 1)

        vcn_flat = vcn[:, :, :].rearrange("p b c -> p (b c)")

        MIX = [ZA, ZA + 1, ZA + 2, ZA + 3, ZB, ZB + 1, ZC, ZC + 1]
        wo = carve(0, KD * D).rearrange("p (k n) -> p k n", k=KD)
        gpost = late[:, 0:D]
        xo = carve(X0, 3 * D).rearrange("p (b n) -> p b n", b=3)
        junk = carve(X0 + 3 * D, D)

        def rows_of(n):
            return P if n < NT else S

        def x_rows(n):
            return dram["x_prompt"][n * P:(n + 1) * P, :] if n < NT else dram["x_sample"]

        def y_rows(n):
            return outs[0][0, n * P:(n + 1) * P, :] if n < NT else outs[1].rearrange("b t d -> (b t) d")

        def sp_output(sp):
            sp.wait_ge(SEM["oz"], 2 + NT * R)
            sp.dma_start(gpost, dram["g_post"].to_broadcast([P, D])).then_inc(SEM["ld_gp"], 16)
            sp.wait_ge(SEM["kused"], 4)
            sp.dma_start(wo, dram["w_out"]).then_inc(SEM["ld_wo"], 16)
            sp.wait_ge(SEM["vused"], 4)
            for n in range(3):
                sp.dma_start(xo[0:rows_of(n), n, :], x_rows(n)).then_inc(xo_ld[n], 16)
            for n in range(9):
                b = n % 3
                sp.wait_ge(SEM["y_out"], n + 1)
                sp.dma_start(y_rows(n), xo[0:rows_of(n), b, :]).then_inc(y_st[b], 16)
                if n + 3 < 9:
                    sp.wait_ge(y_st[b], 16 * (n // 3 + 1))
                    sp.dma_start(xo[0:rows_of(n + 3), b, :], x_rows(n + 3)).then_inc(xo_ld[b], 16)
            for b in range(3):
                sp.wait_ge(y_st[b], 48)

        def pe_output(pe):
            pe.wait_ge(SEM["ld_wo"], 16)
            pe.wait_ge(SEM["dpair"], 5)
            for n in range(9):
                w = rows_of(n)
                if n >= 2:
                    pe.wait_ge(SEM["y_free"], n - 1)
                for h in range(2):
                    for k in range(KD):
                        last = pe.matmul(bank(2 * (n % 2) + h)[0:w, :], proj[:, MIX[k], n * P:n * P + w], wo[:, k, h * 512:(h + 1) * 512],
                                         start=(k == 0), stop=(k == KD - 1))
                last.then_inc(SEM["y_ps"], 1)

        def act_output(act):
            act.wait_ge(SEM["vused"], 4)
            for n in range(9):
                w = rows_of(n)
                act.wait_ge(SEM["y_ps"], n + 1)
                act.drain()
                act.activation(junk[0:w, :], bank(2 * (n % 2), 2)[0:w, :], ACT.Square, accum_out=ssq[0:w, n:n + 1]).then_inc(SEM["y_sq"], 1)
                act.wait_ge(SEM["y_ms"], n + 1)
                act.activation(rstd[0:w, n:n + 1], rstd[0:w, n:n + 1], ACT.Sqrt).then_inc(SEM["y_rt"], 1)

        def dve_output(dve):
            dve.wait_ge(SEM["ld_gp"], 16)
            for n in range(9):
                w, b = rows_of(n), n % 3
                dve.wait_ge(SEM["y_sq"], n + 1)
                dve.tensor_scalar(rstd[0:w, n:n + 1], ssq[0:w, n:n + 1], 1.0 / D, EPS, ALU.mult, ALU.add).then_inc(SEM["y_ms"], 1)
                dve.wait_ge(SEM["y_rt"], n + 1)
                dve.reciprocal(rstd[0:w, n:n + 1], rstd[0:w, n:n + 1])
                dve.wait_ge(xo_ld[b], 16 * (n // 3 + 1))
                dve.drain()
                y = yb[0:w, n % 2, :]
                dve.scalar_tensor_tensor(y, bank(2 * (n % 2), 2)[0:w, :], rstd[0:w, n:n + 1], gpost[0:w, :], ALU.mult, ALU.mult).then_inc(SEM["y_free"], 1)
                dve.wait_ge(SEM["y_free"], n + 1)
                dve.tensor_tensor(xo[0:w, b, :], xo[0:w, b, :], y, ALU.add).then_inc(SEM["y_out"], 1)

        yb = carve(X0 + 4 * D, 2 * D).rearrange("p (b n) -> p b n", b=2)
        N_SO = 5 + NB
        N_NAT = 12

        @block.sync
        def _(sp):
            sp_startup(sp)
            sp_project(sp, 1, 9)
            sp_states(sp)
            sp_project(sp, 9, 12)
            sp_natural(sp)
            sp_decode(sp)
            sp_output(sp)
            sp.wait_ge(out_done, 16 * 3)
            sp.wait_ge(so_out, 16 * N_SO)
            sp.wait_ge(SEM["nat_out"], 16 * N_NAT)

        @block.gpsimd
        def _(pool):
            pool_startup(pool)
            pool_compress(pool)
            pool_decode(pool)

        @block.scalar
        def _(act):
            act_startup(act)
            act_softplus(act)
            act_project(act, 0, 2)
            act_bc_inputs(act, 0)
            act_softplus_log(act)
            act_project(act, 2, 4)
            act_states(act)
            act_branch_gates(act)
            act_turn_gates(act)
            act_bc_inputs(act, 1)
            act_project(act, 4, 5)
            act_gates(act)
            act_decay(act, 0)
            act_bc_inputs(act, 2)
            act_project(act, 5, 6)
            act_decay(act, 1)
            act_project(act, 6, 7)
            act_squares(act)
            act_project(act, 7, 8)
            act_var(act)
            act_swish(act)
            act_last_states(act)
            act.wait_ge(scan_done, 1)
            act_project(act, 8, 10)
            act_decode_keys(act)
            act_prompt_values(act)
            act_prompt_exp(act)
            act_selectors(act)
            act.wait_ge(SEM["bc_done"], 1)
            act_project(act, 10, 11)
            act_decode_exp(act)
            act_branch_a_gates(act, 0, 2)
            act.wait_ge(so_out, 16 * N_SO)
            act_project(act, 11, 12)
            act_decode_turn(act)
            act_masks(act)
            natural(act, 0)
            act_prompt_turn(act)
            act_branch_a_gates(act, 2, 4)
            act_pairs(act)
            act_decode(act)
            act_output(act)

        @block.vector
        def _(dve):
            dve_startup(dve)
            dve_softplus(dve)
            dve_compress(dve, 0, 0, NB)
            dve_u(dve)
            dve_conv_b(dve, 0)
            dve_softplus_end(dve)
            dve_xc(dve)
            dve_conv_c(dve)
            dve_conv_b(dve, 1)
            dve_decay(dve)
            dve_compress(dve, 1, 0, 1)
            dve_scan(dve)
            dve_compress(dve, 1, 1, 3)
            dve_mean(dve)
            dve_compress(dve, 1, 3, 5)
            dve_var(dve)
            dve_compress(dve, 1, 5, 6)
            dve_pointwise(dve)
            dve.drain().then_inc(SEM["bc_done"], 1)
            dve_prompt_blocks(dve)
            dve_compress(dve, 1, 6, NB)
            dve_prompt_cmp(dve)
            dve_decode_queries(dve)
            dve_prompt_norm(dve)
            dve_decode_cmp(dve)
            dve_select(dve)
            dve_new_values(dve)
            dve_pairs_prepare(dve)
            natural(dve, 1)
            dve_pairs(dve)
            dve_decode(dve)
            dve_output(dve)

        @block.tensor
        def _(pe):
            pe_startup(pe)
            pe_project(pe, 0, 4)
            pe_states(pe)
            pe_branch_gates(pe)
            pe_turn_gates(pe)
            pe_project(pe, 4, 5)
            pe_gates(pe)
            pe_project(pe, 5, 7)
            pe_mean(pe)
            pe_project(pe, 7, 8)
            pe_var(pe)
            pe_last_states(pe)
            pe_project(pe, 8, 9)
            pe_pointwise(pe)
            pe_project(pe, 9, 10)
            pe_decode_keys(pe)
            pe_prompt_blocks(pe)
            pe_project(pe, 10, 11)
            pe_decode_cmp(pe)
            pe_project(pe, 11, 12)
            pe_importance(pe)
            pe_masks(pe)
            pe_natural(pe)
            pe_prompt_turn(pe)
            pe_pairs(pe)
            pe_decode(pe)
            pe_output(pe)


def lay_out(i):
    w_in, w_out = i["w_in"][0], i["w_out"][0]
    kv = 6 * G * HD
    q0, kv0 = 0, H * HD
    gate0 = kv0 + kv
    za0 = gate0 + 3 * H
    glu0 = za0 + H * HD
    zb0 = glu0 + 512
    xc0 = zb0 + 256
    zc0 = xc0 + 256

    def pair(a, r):
        return np.r_[a + r * HD:a + (r + 1) * HD, a + (r + R) * HD:a + (r + R + 1) * HD]

    def run(a, n):
        return [np.arange(a + P * c, a + P * (c + 1)) for c in range(n)]
    tiles = run(glu0, 4) + run(xc0, 2) + run(zb0, 2) + run(zc0, 2) + [pair(q0, r) for r in range(R)] \
        + run(kv0, 6) + [pair(za0, r) for r in range(R)]

    def k_major(w):
        return w.reshape(KD, P, -1).transpose(1, 0, 2)
    w_tiles = np.stack([k_major(w_in[:, c]).reshape(P, KD * P) for c in tiles])
    rows = np.concatenate([pair(0, r) for r in range(R)] + [np.arange(512, 1024)])

    def per_channel(v):
        v = v.reshape(-1, 2, P)
        return v.transpose(2, 1, 0).reshape(P, -1)

    def blocks(w):
        o = np.zeros((P, 2, P), np.float32)
        for c in range(2):
            for h in range(2):
                o[h * HD:(h + 1) * HD, c, h * HD:(h + 1) * HD] = w[2 * c + h]
        return o.reshape(P, -1)
    par = dict(g_pre=i["g_pre"][0].reshape(KD, P).T, conv_b_b=per_channel(i["conv_b_b"][0]),
               gn_gain=per_channel(i["gn_gain"][0]), gn_bias=per_channel(i["gn_bias"][0]),
               conv_c_b=per_channel(i["conv_c_b"][0]), b_a=per_channel(i["b_lru_a"][0]),
               b_x=per_channel(i["b_lru_x"][0]), lam=per_channel(i["lru_lambda"][0]),
               conv_b_w=per_channel(i["conv_b_w"][0]), conv_c_w=per_channel(i["conv_c_w"][0]),
               wk=np.tile(i["w_cmp_k"][0].T, (2, 1)), wv=np.tile(i["w_cmp_v"][0].T, (2, 1)))
    pool = lambda a, n: a[0].reshape(-1, n * G * HD)
    return {
        "constants": constant_pack(),
        "parameters": np.concatenate([par[n] for n in PAR_COLS], 1),
        "one_hot": one_hot_tables(),
        "selectors": decode_selectors(),
        "x_prompt": i["x_prompt"][0], "x_sample": i["x_sample"].reshape(S, D),
        "w_tiles": w_tiles,
        "w_gate": k_major(w_in[:, gate0:za0]),
        "w_small": np.concatenate([i["w_pw_b"][0].reshape(2, P, 256).transpose(1, 0, 2).reshape(P, -1),
                                   blocks(i["w_lru_a"][0]), blocks(i["w_lru_x"][0])], 1),
        "w_out": k_major(w_out[rows]),
        "g_post": i["g_post"],
        "rel_bias": i["rel_bias"],
        "pages": np.repeat(i["page_table"].T, PAGE // L_CMP, 0),
        "w_cmp_k": i["w_cmp_k"].reshape(1, -1), "w_cmp_v": i["w_cmp_v"].reshape(1, -1),
        "state_conv_b": i["state_conv_b"][0], "state_conv_c": i["state_conv_c"].reshape(NB * 3, 256),
        "state_rglru": i["state_rglru"][0],
        "cmp_k": pool(i["cache_cmp_k"], 16), "cmp_v": pool(i["cache_cmp_v"], 16),
        "sel_k": pool(i["cache_sel_k"], 32), "sel_v": pool(i["cache_sel_v"], 32),
        "win_k": i["cache_win_k"][0].reshape(NB, WIN, G * HD), "win_v": i["cache_win_v"][0].reshape(NB, WIN, G * HD),
    }


_KV_P, _KV_S = (1, 1, T, G, HD), (1, NB, DS, G, HD)
_WIN_P, _WIN_S = (1, 1, WIN, G, HD), (1, NB, WIN, G, HD)
_OUTS = [(1, T, D), (NB, DS, D)] + [_KV_P, _KV_S] * 4 + [_WIN_P, _WIN_S] * 2 \
    + [(1, 1, CB_W - 1, 256), (1, NB, CB_W - 1, 256), (1, 1, CC_W - 1, 256), (1, NB, CC_W - 1, 256), (1, 1, 256), (1, NB, 256)]


def kernel(**inputs):
    import concourse.bacc as _bacc
    from concourse.bass_utils import run_bass_kernel_spmd as _run

    nc = _bacc.Bacc("TRN2", target_bir_lowering=False, num_devices=1)
    arrays, dram = {}, {}
    for name, a in lay_out({k: np.asarray(v) for k, v in inputs.items()}).items():
        a = np.ascontiguousarray(a)
        arrays[f"in_{name}_dram"] = a
        dram[name] = nc.dram_tensor(f"in_{name}_dram", a.shape, mybir.dt.from_np(a.dtype), kind="ExternalInput").ap()
    outs = [nc.dram_tensor(f"out_{n}_dram", shape, F32, kind="ExternalOutput").ap() for n, shape in enumerate(_OUTS)]
    strip = nc.dram_tensor("bias_strip", (H, P, SKEW), F32, kind="Internal").ap()
    skewed = bass.AP(strip.tensor, P - 1, [[SKEW - 1, P], [P * SKEW, H], [1, 2 * P]])
    program(nc, dram, outs, {"strip": strip, "skewed": skewed})
    r = _run(nc, [arrays], core_ids=[0])
    return tuple(r.results[0][f"out_{n}_dram"] for n in range(len(_OUTS)))
```
